# Optimizing a Trainium2 kernel written in Bass

```python
import math
import jax, jax.numpy as jnp
from jax import lax
import numpy as np

D_MODEL = 1024
BATCH = 1
SEQ = 256
DEPTH = 2

HEAD_DIM = 64
MOBA_HEADS = 8
DSA_HEADS = 8
MOBA_BLOCK = 256
MOBA_TOPK = 3
MOBA_QCHUNK = 32
DSA_TOPK = 256
DSA_QBLOCK = 128
IDX_HEADS = 4
IDX_DIM = 64
REL_BUCKETS = 32
REL_MAX_DIST = 1024
MLA_HEADS = 16
MLA_Q_RANK = 384
MLA_KV_RANK = 256
MLA_NOPE = 64
MLA_ROPE = 32
MLA_V = 64
MLA_QK = MLA_NOPE + MLA_ROPE
MLA_QBLOCK = 128
ROPE_BASE = 10000.0
D_FF_DENSE = 2816
N_EXPERTS = 8
TOP_K = 2
D_FF_EXPERT = 3584
EPS = 1e-6

EVEN_IN_SIZES = [MOBA_HEADS * HEAD_DIM] * 3 + [DSA_HEADS * HEAD_DIM] * 3 + [IDX_HEADS * IDX_DIM, IDX_DIM, IDX_HEADS]
D_IN_EVEN = sum(EVEN_IN_SIZES)
ODD_IN_SIZES = [MLA_Q_RANK, MLA_KV_RANK, MLA_ROPE]
D_IN_ODD = sum(ODD_IN_SIZES)

kernel_name = "hybrid_moba_dsa_mla_moe"

def _split(a, sizes):
    return jnp.split(a, [int(s) for s in np.cumsum(sizes)[:-1]], axis=-1)

def rmsnorm(x, g):
    xf = x.astype(jnp.float32)
    y = xf * lax.rsqrt(jnp.mean(xf * xf, axis=-1, keepdims=True) + EPS)
    return (y * g.astype(jnp.float32)).astype(x.dtype)

def rel_bucket(dist):
    n = jnp.maximum(dist, 0)
    max_exact = REL_BUCKETS // 2
    nf = jnp.maximum(n, 1).astype(jnp.float32)
    large = max_exact + (jnp.log(nf / max_exact) / math.log(REL_MAX_DIST / max_exact)
                         * (REL_BUCKETS - max_exact)).astype(jnp.int32)
    large = jnp.minimum(large, REL_BUCKETS - 1)
    return jnp.where(n < max_exact, n, large)

def moba_attention(q, k, v, rel_bias_h):
    B, S, H, Dh = q.shape
    nb = -(-S // MOBA_BLOCK)
    S_pad = nb * MOBA_BLOCK
    pad = S_pad - S
    to_bhsd = lambda a: jnp.pad(a, ((0, 0), (0, pad), (0, 0), (0, 0))).transpose(0, 2, 1, 3)
    qh, kh, vh = to_bhsd(q), to_bhsd(k), to_bhsd(v)
    kb = kh.reshape(B, H, nb, MOBA_BLOCK, Dh)
    vb = vh.reshape(B, H, nb, MOBA_BLOCK, Dh)
    kmean = jnp.mean(kb.astype(jnp.float32), axis=3)
    n_sel = min(MOBA_TOPK, nb - 1)
    scale = Dh ** -0.5
    bias_t = rel_bias_h.T.astype(jnp.float32)
    head_ix = jnp.arange(H)[None, :, None, None, None]
    gather_blocks = jax.vmap(jax.vmap(lambda a, i: a[i]))

    def chunk(c):
        t0 = c * MOBA_QCHUNK
        tq = t0 + jnp.arange(MOBA_QCHUNK)
        qc = lax.dynamic_slice_in_dim(qh, t0, MOBA_QCHUNK, axis=2)
        blk = t0 // MOBA_BLOCK
        k_own = lax.dynamic_index_in_dim(kb, blk, axis=2, keepdims=False)
        v_own = lax.dynamic_index_in_dim(vb, blk, axis=2, keepdims=False)
        s_own = blk * MOBA_BLOCK + jnp.arange(MOBA_BLOCK)
        lo = jnp.einsum('bhqd,bhkd->bhqk', qc, k_own, preferred_element_type=jnp.float32) * scale
        lo = lo + rel_bias_h.astype(jnp.float32)[rel_bucket(tq[:, None] - s_own[None, :])].transpose(2, 0, 1)[None]
        lo = jnp.where(s_own[None, :] <= tq[:, None], lo, -jnp.inf)
        if n_sel > 0:
            gate = jnp.einsum('bhqd,bhnd->bhqn', qc.astype(jnp.float32), kmean)
            gate = jnp.where(jnp.arange(nb) < blk, gate, -jnp.inf)
            g_val, sel = lax.top_k(gate, n_sel)
            valid = jnp.isfinite(g_val)
            k_sel = gather_blocks(kb, sel)
            v_sel = gather_blocks(vb, sel)
            s_sel = sel[..., None] * MOBA_BLOCK + jnp.arange(MOBA_BLOCK)
            ls = jnp.einsum('bhqd,bhqnkd->bhqnk', qc, k_sel, preferred_element_type=jnp.float32) * scale
            ls = ls + bias_t[head_ix, rel_bucket(tq[None, None, :, None, None] - s_sel)]
            ls = jnp.where(valid[..., None], ls, -jnp.inf)
            ls = ls.reshape(B, H, MOBA_QCHUNK, n_sel * MOBA_BLOCK)
            p = jax.nn.softmax(jnp.concatenate([lo, ls], axis=-1), axis=-1).astype(v.dtype)
            p_own, p_sel = p[..., :MOBA_BLOCK], p[..., MOBA_BLOCK:].reshape(B, H, MOBA_QCHUNK, n_sel, MOBA_BLOCK)
            return (jnp.einsum('bhqk,bhkd->bhqd', p_own, v_own)
                    + jnp.einsum('bhqnk,bhqnkd->bhqd', p_sel, v_sel))
        p = jax.nn.softmax(lo, axis=-1).astype(v.dtype)
        return jnp.einsum('bhqk,bhkd->bhqd', p, v_own)

    out = lax.map(chunk, jnp.arange(S_pad // MOBA_QCHUNK))
    return out.transpose(1, 0, 3, 2, 4).reshape(B, S_pad, H, Dh)[:, :S]

def dsa_attention(q, k, v, iq, ik, iw, rel_bias_h):
    B, S, H, Dh = q.shape
    n_keep = min(DSA_TOPK, S // 4)
    pos = jnp.arange(S)
    scale = Dh ** -0.5
    idx_scale = (IDX_DIM ** -0.5) * (IDX_HEADS ** -0.5)
    ikf = ik.astype(jnp.float32)
    bias = rel_bias_h.astype(jnp.float32)
    gather_keys = jax.vmap(lambda a, i: a[i])

    def block(c):
        t0 = c * DSA_QBLOCK
        tq = t0 + jnp.arange(DSA_QBLOCK)
        qc = lax.dynamic_slice_in_dim(q, t0, DSA_QBLOCK, axis=1)
        iqc = lax.dynamic_slice_in_dim(iq, t0, DSA_QBLOCK, axis=1).astype(jnp.float32)
        iwc = lax.dynamic_slice_in_dim(iw, t0, DSA_QBLOCK, axis=1).astype(jnp.float32)
        rel = jax.nn.relu(jnp.einsum('bqhd,bsd->bqhs', iqc, ikf))
        score = jnp.einsum('bqh,bqhs->bqs', iwc, rel) * idx_scale
        score = jnp.where(pos[None, None, :] <= tq[None, :, None], score, -jnp.inf)
        s_val, s_idx = lax.top_k(score, n_keep)
        valid = jnp.isfinite(s_val)
        k_sel = gather_keys(k, s_idx)
        v_sel = gather_keys(v, s_idx)
        lg = jnp.einsum('bqhd,bqkhd->bhqk', qc, k_sel, preferred_element_type=jnp.float32) * scale
        lg = lg + bias[rel_bucket(tq[None, :, None] - s_idx)].transpose(0, 3, 1, 2)
        lg = jnp.where(valid[:, None], lg, -jnp.inf)
        p = jax.nn.softmax(lg, axis=-1).astype(v.dtype)
        return jnp.einsum('bhqk,bqkhd->bqhd', p, v_sel)

    out = lax.map(block, jnp.arange(S // DSA_QBLOCK))
    return out.transpose(1, 0, 2, 3, 4).reshape(B, S, H, Dh)

def rope(x, pos):
    half = x.shape[-1] // 2
    freqs = ROPE_BASE ** (-jnp.arange(half, dtype=jnp.float32) / half)
    ang = pos.astype(jnp.float32)[:, None] * freqs
    cos, sin = jnp.cos(ang)[:, None, :], jnp.sin(ang)[:, None, :]
    xf = x.astype(jnp.float32)
    x1, x2 = xf[..., :half], xf[..., half:]
    return jnp.concatenate([x1 * cos - x2 * sin, x1 * sin + x2 * cos], axis=-1).astype(x.dtype)

def causal_attention_blocks(q, k, v):
    B, S, H, D = q.shape
    scale = D ** -0.5
    pos = jnp.arange(S)

    def block(c):
        t0 = c * MLA_QBLOCK
        tq = t0 + jnp.arange(MLA_QBLOCK)
        qc = lax.dynamic_slice_in_dim(q, t0, MLA_QBLOCK, axis=1)
        lg = jnp.einsum('bqhd,bshd->bhqs', qc, k, preferred_element_type=jnp.float32) * scale
        lg = jnp.where(pos[None, :] <= tq[:, None], lg, -jnp.inf)
        p = jax.nn.softmax(lg, axis=-1).astype(v.dtype)
        return jnp.einsum('bhqs,bshd->bqhd', p, v)

    out = lax.map(block, jnp.arange(S // MLA_QBLOCK))
    return out.transpose(1, 0, 2, 3, 4).reshape(B, S, H, v.shape[-1])

def sparse_mixers(h, w_in, moba_q_norm, moba_k_norm, dsa_q_norm, dsa_k_norm, rel_bias, w_out):
    B, S, _ = h.shape
    mq, mk, mv, dq, dk, dv, iq, ik, iw = _split(h @ w_in, EVEN_IN_SIZES)
    heads = lambda a, n: a.reshape(B, S, n, HEAD_DIM)
    mq = rmsnorm(heads(mq, MOBA_HEADS), moba_q_norm)
    mk = rmsnorm(heads(mk, MOBA_HEADS), moba_k_norm)
    dq = rmsnorm(heads(dq, DSA_HEADS), dsa_q_norm)
    dk = rmsnorm(heads(dk, DSA_HEADS), dsa_k_norm)
    a = moba_attention(mq, mk, heads(mv, MOBA_HEADS), rel_bias[:, :MOBA_HEADS])
    b = dsa_attention(dq, dk, heads(dv, DSA_HEADS), iq.reshape(B, S, IDX_HEADS, IDX_DIM), ik, iw,
                      rel_bias[:, MOBA_HEADS:])
    o = jnp.concatenate([a.reshape(B, S, -1), b.reshape(B, S, -1)], axis=-1)
    return o @ w_out

def mla_mixer(h, w_in, q_a_norm, kv_a_norm, w_uq, w_ukv, q_norm, k_norm, w_out):
    B, S, _ = h.shape
    pos = jnp.arange(S)
    cq, ckv, k_pe = _split(h @ w_in, ODD_IN_SIZES)
    q = (rmsnorm(cq, q_a_norm) @ w_uq).reshape(B, S, MLA_HEADS, MLA_QK)
    kv = (rmsnorm(ckv, kv_a_norm) @ w_ukv).reshape(B, S, MLA_HEADS, MLA_NOPE + MLA_V)
    k_nope, v = kv[..., :MLA_NOPE], kv[..., MLA_NOPE:]
    k = jnp.concatenate([k_nope, jnp.broadcast_to(k_pe[:, :, None, :], (B, S, MLA_HEADS, MLA_ROPE))], axis=-1)
    q = rmsnorm(q, q_norm)
    k = rmsnorm(k, k_norm)
    q = jnp.concatenate([q[..., :MLA_NOPE], rope(q[..., MLA_NOPE:], pos)], axis=-1)
    k = jnp.concatenate([k[..., :MLA_NOPE], rope(k[..., MLA_NOPE:], pos)], axis=-1)
    o = causal_attention_blocks(q, k, v)
    return o.reshape(B, S, MLA_HEADS * MLA_V) @ w_out

def swiglu(h, w_gate, w_up, w_down):
    return (jax.nn.silu(h @ w_gate) * (h @ w_up)) @ w_down

def moe_swiglu(h, w_router, b_router, w_gate, w_up, w_down):
    B, S, D = h.shape
    ht = h.reshape(B * S, D)
    logits = (ht @ w_router).astype(jnp.float32) + b_router.astype(jnp.float32)
    top_val, top_idx = lax.top_k(logits, TOP_K)
    gates = jax.nn.softmax(top_val, axis=-1)
    combine = jnp.sum(jax.nn.one_hot(top_idx, N_EXPERTS, dtype=jnp.float32) * gates[..., None], axis=1)
    y = jnp.zeros_like(ht)
    for e in range(N_EXPERTS):
        y = y + combine[:, e:e + 1].astype(h.dtype) * swiglu(ht, w_gate[e], w_up[e], w_down[e])
    return y.reshape(B, S, D)

def setup_inputs(seed: int = 0) -> dict:
    key = jax.random.key(seed)
    ks = iter(jax.random.split(key, 40))
    f32 = jnp.float32
    def w(shape, fan_in):
        return jax.random.normal(next(ks), shape, f32) * (fan_in ** -0.5)
    def gain(shape):
        return 1.0 + 0.1 * jax.random.normal(next(ks), shape, f32)
    NE = (DEPTH + 1) // 2
    NO = DEPTH // 2
    return {
        "x": jax.random.normal(next(ks), (BATCH, SEQ, D_MODEL), f32),
        "rel_bias": 0.5 * jax.random.normal(next(ks), (REL_BUCKETS, MOBA_HEADS + DSA_HEADS), f32),
        "mix_norm_e": gain((NE, D_MODEL)),
        "w_in_e": w((NE, D_MODEL, D_IN_EVEN), D_MODEL),
        "moba_q_norm": gain((NE, HEAD_DIM)),
        "moba_k_norm": gain((NE, HEAD_DIM)),
        "dsa_q_norm": gain((NE, HEAD_DIM)),
        "dsa_k_norm": gain((NE, HEAD_DIM)),
        "w_out_e": w((NE, (MOBA_HEADS + DSA_HEADS) * HEAD_DIM, D_MODEL), (MOBA_HEADS + DSA_HEADS) * HEAD_DIM),
        "ffn_norm_e": gain((NE, D_MODEL)),
        "w_gate_e": w((NE, D_MODEL, D_FF_DENSE), D_MODEL),
        "w_up_e": w((NE, D_MODEL, D_FF_DENSE), D_MODEL),
        "w_down_e": w((NE, D_FF_DENSE, D_MODEL), D_FF_DENSE),
        "mix_norm_o": gain((NO, D_MODEL)),
        "w_in_o": w((NO, D_MODEL, D_IN_ODD), D_MODEL),
        "q_a_norm": gain((NO, MLA_Q_RANK)),
        "kv_a_norm": gain((NO, MLA_KV_RANK)),
        "w_uq": w((NO, MLA_Q_RANK, MLA_HEADS * MLA_QK), MLA_Q_RANK),
        "w_ukv": w((NO, MLA_KV_RANK, MLA_HEADS * (MLA_NOPE + MLA_V)), MLA_KV_RANK),
        "mla_q_norm": gain((NO, MLA_QK)),
        "mla_k_norm": gain((NO, MLA_QK)),
        "w_out_o": w((NO, MLA_HEADS * MLA_V, D_MODEL), MLA_HEADS * MLA_V),
        "ffn_norm_o": gain((NO, D_MODEL)),
        "w_router": w((NO, D_MODEL, N_EXPERTS), D_MODEL),
        "b_router": 0.01 * jax.random.normal(next(ks), (NO, N_EXPERTS), f32),
        "w_gate_o": w((NO, N_EXPERTS, D_MODEL, D_FF_EXPERT), D_MODEL),
        "w_up_o": w((NO, N_EXPERTS, D_MODEL, D_FF_EXPERT), D_MODEL),
        "w_down_o": w((NO, N_EXPERTS, D_FF_EXPERT, D_MODEL), D_FF_EXPERT),
    }

def reference(x, rel_bias, mix_norm_e, w_in_e, moba_q_norm, moba_k_norm, dsa_q_norm, dsa_k_norm,
              w_out_e, ffn_norm_e, w_gate_e, w_up_e, w_down_e, mix_norm_o, w_in_o, q_a_norm, kv_a_norm,
              w_uq, w_ukv, mla_q_norm, mla_k_norm, w_out_o, ffn_norm_o, w_router, b_router,
              w_gate_o, w_up_o, w_down_o):
    for layer in range(DEPTH):
        i = layer // 2
        if layer % 2 == 0:
            h = rmsnorm(x, mix_norm_e[i])
            x = x + sparse_mixers(h, w_in_e[i], moba_q_norm[i], moba_k_norm[i], dsa_q_norm[i],
                                  dsa_k_norm[i], rel_bias, w_out_e[i])
            h = rmsnorm(x, ffn_norm_e[i])
            x = x + swiglu(h, w_gate_e[i], w_up_e[i], w_down_e[i])
        else:
            h = rmsnorm(x, mix_norm_o[i])
            x = x + mla_mixer(h, w_in_o[i], q_a_norm[i], kv_a_norm[i], w_uq[i], w_ukv[i],
                              mla_q_norm[i], mla_k_norm[i], w_out_o[i])
            h = rmsnorm(x, ffn_norm_o[i])
            x = x + moe_swiglu(h, w_router[i], b_router[i], w_gate_o[i], w_up_o[i], w_down_o[i])
    return x


_drawn_inputs = setup_inputs


def setup_inputs(seed=0):
    import zlib

    import numpy as np

    out = dict(_drawn_inputs(seed))
    spreads = {}
    factors = {}
    for name, (base, spread) in spreads.items():
        noise = np.random.default_rng([zlib.crc32(name.encode()), seed]).standard_normal(out[name].shape)
        drawn = base * np.exp(spread * noise) if base else spread * noise
        out[name] = __import__('jax').numpy.asarray(drawn.astype(out[name].dtype))
    for name, factor in factors.items():
        out[name] = (out[name] * factor).astype(out[name].dtype)
    return out
```

```python
import concourse.bass as bass
from concourse import mybir
from contextlib import ExitStack

P = 128
S = 256
TT = S // P
D = 1024
DC = D // P
HD = 64
NH = 16
IDXH = 4
BUCKETS = 32
FFD = 2816
QR, KVR, ROPE = 384, 256, 32
QKD = 96
NE = 8
FFE = 3584
DSA_KEEP = 64
EPS = 1e-6
MASKED = -1e30
TAKEN = -3e38

K_ID, K_IOTA, K_TRI, K_ONES = 0, 128, 256, 384
K_MASK = 512
K_COS, K_SIN = 896, 1024
K_LOW = 1152
K_ALL = 1216
LOG = 384

RAW = 7
STG = 3
CW = 2048
NT = 512

G_MIX_E, G_FFN_E, G_MIX_O, G_FFN_O, G_QA, G_KVA, G_HEAD, G_ROWS = 0, 8, 16, 24, 32, 35, 37, 41

IDXW = IDXH * HD + HD + IDXH
FF_TILES = -(-FFD // NT)
FE_TILES = FFE // NT
EXPERT_CHUNKS = 4 * FE_TILES + FFE // P // 2
GROUPS = 4
GH = NH // GROUPS


def hybrid_trunk(nc, x, rel_bias, mix_norm_e, w_in_e, moba_q_norm, moba_k_norm, dsa_q_norm,
                 dsa_k_norm, w_out_e, ffn_norm_e, w_gate_e, w_up_e, w_down_e, mix_norm_o, w_in_o,
                 q_a_norm, kv_a_norm, w_uq, w_ukv, mla_q_norm, mla_k_norm, w_out_o, ffn_norm_o,
                 w_router, b_router, w_gate_o, w_up_o, w_down_o, consts, buckets, out):
    f32, f32r, i32 = mybir.dt.float32, mybir.dt.float32r, mybir.dt.int32
    ALU, ACT, AX = mybir.AluOpType, mybir.ActivationFunctionType, mybir.AxisListType

    def rows(w, r0, k, c0, n):
        return w[0][r0:r0 + k * P, c0:c0 + n].rearrange("(k p) n -> p k n", p=P)

    chunks = []

    def plan(aps):
        first = len(chunks)
        chunks.extend(aps)
        return first

    IN_TILES = [(6 * NT, IDXW)] + [(n * NT, NT) for n in range(6)]
    IN_TURN = [0, 1, 2, None, 3, 4, None]
    C_IN = plan([rows(w_in_e, kh * 512, 4, c, n) for c, n in IN_TILES for kh in range(2)])
    C_OUTE = plan([rows(w_out_e, kh * 512, 4, n * NT, NT) for n in range(2) for kh in range(2)])
    FF_W = [min(NT, FFD - j * NT) for j in range(FF_TILES)]
    C_FF = plan([rows(w, kh * 512, 4, j * NT, FF_W[j]) for j in range(FF_TILES)
                 for w in (w_gate_e, w_up_e) for kh in range(2)])
    C_FD = plan([rows(w_down_e, q * 256, 2, 0, D) for q in range(FFD // 256)])
    LAT = [(0, QR), (QR, KVR + ROPE)]
    C_LAT = plan([rows(w_in_o, kh * 512, 4, c, n) for c, n in LAT for kh in range(2)])
    C_HEADS = plan([a for g in range(GROUPS) for a in
                    (rows(w_uq, 0, 3, g * GH * QKD, GH * QKD), rows(w_ukv, 0, 2, g * GH * P, GH * P))])
    C_OUTO = plan([rows(w_out_o, kh * 512, 4, n * NT, NT) for n in range(2) for kh in range(2)])
    C_ROUTE = plan([rows(w_router, 0, DC, 0, NE)])
    C_MOE = len(chunks)

    with ExitStack() as ctx:
        sems = {}

        def sem(name):
            if name not in sems:
                sems[name] = ctx.enter_context(nc.semaphore(name))
            return sems[name]

        def sb(name, shape, dt=f32):
            return ctx.enter_context(nc.sbuf_tensor(name, shape, dt))

        raw = sb("raw", [P, RAW, CW])
        w_hi = sb("w_hi", [P, STG, CW], f32r)
        w_lo = sb("w_lo", [P, STG, CW], f32r)
        X = sb("X", [P, TT, D])
        a_hi = sb("a_hi", [P, DC, S], f32r)
        a_lo = sb("a_lo", [P, DC, S], f32r)
        cst = sb("cst", [P, K_ALL])
        gain = sb("gain", [P, G_ROWS + 4])
        gate_bias = sb("gate_bias", [P, NE])
        st = sb("st", [P, 96])
        nm = sb("nm", [P, 2 * NH, 2])
        top8 = sb("top8", [P, 16])
        rs = sb("rs", [P, 2 * NH, 4])
        pos = sb("pos", [P, TT, 2 * NE])
        comb = sb("comb", [P, TT, NE])
        need = sb("need", [1, 2 * NE], i32)
        ident = cst[:, K_ID:K_ID + P]
        iota = cst[:, K_IOTA:K_IOTA + P]
        mask = cst[:, K_MASK:K_MASK + LOG]

        arena_words = 18784
        arena = sb("arena", [P, arena_words])
        base = nc.sbuf_base - 4 * arena_words

        def place(at, name, shape, dt=f32):
            n = 1
            for v in shape[1:]:
                n *= v
            assert at + n <= arena_words, (name, at + n)
            return nc.alloc_sbuf_tensor_at(name, shape, dt, offset=base + 4 * at), at + n

        xn, z = place(0, "xn", [P, TT, D])
        v0, _ = place(0, "v0", [P, TT, NH * HD])
        qT0, z = place(z, "qT0", [P, 8, S])
        kT0, z = place(z, "kT0", [P, 8, S])
        brev, z = place(z, "brev", [P, NH, S])
        sq, z = place(z, "sq", [P, TT, NT])
        qn, z1 = place(z, "qn", [P, 2, TT, NT])
        lg, z2 = place(z, "lg", [P, 4, LOG])
        pT, _ = place(z2, "pT", [P, 2, LOG])
        z = max(z1, z2 + 2 * LOG)
        idxn, z1 = place(z, "idxn", [P, TT, 384])
        iqT, z1 = place(z1, "iqT", [P, 2, S])
        ikT, z1 = place(z1, "ikT", [P, S])
        relu, z1 = place(z1, "relu", [P, 2, LOG])
        score, z1 = place(z1, "score", [P, LOG])
        dmask, z1 = place(z1, "dmask", [P, LOG])
        brow, z1 = place(z1, "brow", [16, LOG])
        bias_in, z1 = place(z1, "bias_in", [BUCKETS + 1, LOG + 16])
        grow, _ = place(z - 512, "grow", [G_ROWS, P])
        z0 = TT * D
        act_hi, z = place(z0, "act_hi", [P, FFD // P, S], f32r)
        act_lo, z = place(z, "act_lo", [P, FFD // P, S], f32r)
        sg, z = place(z, "sg", [P, TT, NT])
        hn, z = place(z, "hn", [P, 2, TT, NT])
        latn, z = place(z0, "latn", [P, TT, QR + KVR])
        lat_hi, z = place(z, "lat_hi", [P, 5, S], f32r)
        lat_lo, z = place(z, "lat_lo", [P, 5, S], f32r)
        kpe, z = place(z, "kpe", [P, TT, ROPE])
        sq1, z = place(z, "sq1", [P, TT * GH * (QKD + 64)])
        qk, z = place(z, "qk", [P, 4 * TT * GH // 2, QKD])
        kpj, _ = place(z, "kpj", [P, TT * ROPE])
        rot, z = place(z, "rot", [P, 4, 16, 16])
        qkT, z = place(z, "qkT", [P, GH, 2 * S])
        v1, z = place(z, "v1", [P, TT, GH * 64])
        lg1, z = place(z, "lg1", [P, 4, LOG])
        pT1, z = place(z, "pT1", [P, 2, LOG])
        gbc, z = place(z, "gbc", [P, 2, QKD])
        h_hi, z = place(z0, "h_hi", [P, TT, D], f32r)
        h_lo, z = place(z, "h_lo", [P, TT, D], f32r)
        zr = z
        ffg, _ = place(zr, "ffg", [P, D])
        rt, _ = place(zr + D, "rt", [P, 10, TT * NE * NE])
        e_hi, z = place(zr, "e_hi", [P, FFE // P, P], f32r)
        e_lo, z = place(z, "e_lo", [P, FFE // P, P], f32r)
        sge, z = place(z, "sge", [P, 2, NT])
        he, z = place(z, "he", [P, 2, NT])
        y_hi, z = place(z, "y_hi", [P, D], f32r)
        y_lo, z = place(0, "y_lo", [P, D], f32r)
        pick, z = place(z, "pick", [P, TT, P], f32r)
        pickg, z = place(z, "pickg", [P, TT, P])
        backT, z = place(z, "backT", [P, S], f32r)

        PS = ctx.enter_context(nc.psum_tensor("PS", [P, 8, NT], f32))
        bias_dram = nc.dram_tensor("bias_scratch", [16, LOG], f32)

        raw_full = [sem(f"raw_full{i}") for i in range(RAW)]
        hi_done, lo_done, mm_done = sem("hi_done"), sem("lo_done"), sem("mm_done")

        FB = [2 * (w // 256) // 2 for w in FF_W]
        FB0 = [sum(FB[:j]) for j in range(FF_TILES + 1)]
        N_SMALL, N_X = 16, 2

        block = ctx.enter_context(nc.Block())

        @block.sync
        def _(sp):
            sp.dma_start(X[:, :, :], x[0].rearrange("(t p) d -> p t d", p=P)).then_inc(sem("x_in"), 16)
            sp.dma_start(cst[:, :], consts).then_inc(sem("x_in"), 16)

            sp.wait_ge(sem("small_in"), 16 * N_SMALL)
            for c, src in enumerate(chunks):
                if c >= RAW:
                    sp.wait_ge(lo_done, c - RAW + 1)
                k, n = src.shape[1], src.shape[2]
                sp.dma_start(raw[:, c % RAW, 0:k * n].rearrange("p (k n) -> p k n", k=k), src)\
                    .then_inc(raw_full[c % RAW], 16)
            sp.wait_ge(sem("need_set"), 1)
            with sp.Fori(0, 2) as b:
                with sp.Fori(0, NE) as e:
                    i = b * NE + e
                    tokens = sp.value_load(need[0:1, bass.ds(i, 1)], min_val=-S, max_val=S)
                    with sp.If(tokens > 0):
                        for k in range(EXPERT_CHUNKS):
                            slot = (C_MOE + k) % RAW
                            sp.wait_ge(lo_done, C_MOE + k - RAW + 1 + i * EXPERT_CHUNKS)
                            if k < 4 * FE_TILES:
                                w = (w_gate_o, w_up_o)[k // 2 % 2]
                                src = w[0][bass.ds(e, 1), (k % 2) * 512:(k % 2) * 512 + 512,
                                           (k // 4) * NT:(k // 4 + 1) * NT]\
                                    .rearrange("a (k p) n -> p (a k) n", p=P)
                            else:
                                q = k - 4 * FE_TILES
                                src = w_down_o[0][bass.ds(e, 1), q * 256:(q + 1) * 256, :]\
                                    .rearrange("a (k p) n -> p (a k) n", p=P)
                            sp.dma_start(raw[:, slot, :].rearrange("p (k n) -> p k n", k=src.shape[1]), src)\
                                .then_inc(raw_full[slot], 16)
                    with sp.Else():
                        sp.wait_ge(lo_done, C_MOE + i * EXPERT_CHUNKS)
                        for slot in range(RAW):
                            sp.sem_inc(raw_full[slot], 16 * EXPERT_CHUNKS // RAW)
            sp.wait_ge(sem("moe_add"), 4 * 2 * NE)
            sp.dma_start(out[0].rearrange("(t p) d -> p t d", p=P), X[:, :, :]).then_inc(sem("stored"), 16)
            sp.wait_ge(sem("stored"), 16)

        @block.scalar
        def _(act):
            for r0, src in ((G_MIX_E, mix_norm_e), (G_FFN_E, ffn_norm_e), (G_MIX_O, mix_norm_o),
                            (G_FFN_O, ffn_norm_o), (G_QA, q_a_norm), (G_KVA, kv_a_norm)):
                n = src.shape[1] // P
                act.dma_start(grow[r0:r0 + n, :], src[0].rearrange("(r p) -> r p", p=P)).then_inc(sem("small_in"), 16)
            for m, src in enumerate((moba_q_norm, moba_k_norm, dsa_q_norm, dsa_k_norm)):
                for half in range(2):
                    act.dma_start(grow[G_HEAD + m:G_HEAD + m + 1, half * HD:(half + 1) * HD], src)\
                        .then_inc(sem("small_in"), 16)
            act.dma_start(bias_in[:, 0:LOG], buckets).then_inc(sem("small_in"), 16)
            act.dma_start(bias_in[0:BUCKETS, LOG:LOG + 16], rel_bias).then_inc(sem("small_in"), 16)

            nsplit = [0]

            def split(c):
                assert nsplit[0] == c
                nsplit[0] += 1
                act.wait_ge(raw_full[c % RAW], 16 * (c // RAW + 1))
                if c >= STG:
                    act.wait_ge(mm_done, c - STG + 1)
                n = chunks[c].shape[1] * chunks[c].shape[2]
                nc.scalar.activation(w_hi[:, c % STG, 0:n], raw[:, c % RAW, 0:n], ACT.Copy).then_inc(hi_done, 1)

            def split_to(c):
                while nsplit[0] < c:
                    split(nsplit[0])

            def norm(q):
                act.wait_ge(sem("x_in"), 32) if q == 0 else act.wait_ge(sem("resid"), q)
                for t in range(TT):
                    nc.scalar.activation(xn[:, t, :], X[:, t, :], ACT.Square,
                                         accum_out=st[:, 2 * q + t:2 * q + t + 1]).then_inc(sem("norm_ss"), 1)
                act.wait_ge(sem("norm_ms"), q + 1)
                nc.scalar.activation(st[:, 16 + 2 * q:18 + 2 * q], st[:, 8 + 2 * q:10 + 2 * q], ACT.Sqrt)\
                    .then_inc(sem("norm_rt"), 1)
                if q == 3:
                    act.wait_ge(sem("hn_set"), 2)
                    for t in range(TT):
                        nc.scalar.activation(h_hi[:, t, :], xn[:, t, :], ACT.Copy).then_inc(sem("hnat_hi"), 1)
                for c in range(4):
                    act.wait_ge(sem("norm_t"), 4 * q + c + 1)
                    if q == 3:
                        nc.scalar.activation(a_hi[:, 2 * c:2 * c + 2, :],
                                             PS[:, 4 + c, :].rearrange("p (d t) -> p d t", d=2), ACT.Copy)\
                            .then_inc(sem("norm_hi"), 2)
                        continue
                    for d in range(2):
                        dc = 2 * c + d
                        nc.scalar.activation(a_hi[:, dc, :], PS[:, 4 + c, d * S:(d + 1) * S], ACT.Copy,
                                             scale=gain[:, 8 * q + dc:8 * q + dc + 1]).then_inc(sem("norm_hi"), 1)

            def heads(h0, n, logits, probs_t):
                for s in range(n + 3):
                    if s < n:
                        h = h0 + s
                        act.wait_ge(sem("at_max"), h + 1)
                        nc.scalar.activation(logits[:, h % 4, 0:P], logits[:, h % 4, 0:P], ACT.Exp,
                                             bias=nm[:, h, 0:1], accum_out=rs[:, h, 0:1]).then_inc(sem("at_exp"), 1)
                        nc.scalar.activation(logits[:, h % 4, P:LOG], logits[:, h % 4, P:LOG], ACT.Exp,
                                             bias=nm[:, h, 1:2], accum_out=rs[:, h, 1:2]).then_inc(sem("at_exp"), 1)
                    if 2 <= s <= n + 1:
                        h = h0 + s - 2
                        act.wait_ge(sem("at_tr"), h + 1)
                        if h >= 2:
                            act.wait_ge(sem("at_pv"), h - 1)
                        nc.scalar.activation(probs_t[:, h % 2, :], PS[:, 6 + h % 2, 0:LOG], ACT.Copy)\
                            .then_inc(sem("at_pt"), 1)
                    if s >= 3 and (h0 + s - 3) % 2:
                        h = h0 + s - 3
                        act.wait_ge(sem("at_pv"), h + 1)
                        nc.scalar.activation(a_hi[:, h // 2 % 8, :], PS[:, h // 2 % 2, 0:S], ACT.Copy)\
                            .then_inc(sem("at_ohi"), 1)

            split_to(STG)
            act.wait_ge(sem("gain_set"), 1)
            norm(0)
            def qk_evac(m):
                for half in range(2):
                    act.wait_ge(sem("qk_tr"), 2 * m + half + 1)
                    bank = 4 + 2 * (m % 2) + half
                    src = PS[:, bank, :].rearrange("p (d t) -> p d t", d=2)
                    if m == 0:
                        if half == 0:
                            ins = nc.scalar.activation(iqT[:, :, :], src, ACT.Copy)
                        else:
                            ins = nc.scalar.activation(ikT[:, :], PS[:, bank, 0:S], ACT.Copy)
                    else:
                        pair, is_k = (m - 1) // 2, (m - 1) % 2
                        dst = (qT0, kT0)[is_k][:, 4 * pair + 2 * half:4 * pair + 2 * half + 2, :]
                        g = G_HEAD + m - 1 if is_k else G_ROWS + m - 1
                        ins = nc.scalar.activation(dst, src, ACT.Copy, scale=gain[:, g:g + 1])
                    ins.then_inc(sem("qk_evac"), 1)

            for n in range(7):
                split_to(min(C_IN + 2 * n + 4, C_OUTE + 1))
                m = IN_TURN[n]
                if m:
                    act.wait_ge(mm_done, C_IN + 2 * n + 2)
                    if m >= 2:
                        act.wait_ge(sem("sq_read"), m - 1)
                    nc.scalar.activation(sq[:, :, :], PS[:, 2 * (n % 2):2 * (n % 2) + 2, :], ACT.Square)\
                        .then_inc(sem("sq_set"), 1)
                    act.wait_ge(sem("qk_ms"), m)
                    nc.scalar.activation(st[:, 64:80], st[:, 48:64], ACT.Sqrt).then_inc(sem("qk_rt"), 1)
                if n >= 1 and IN_TURN[n - 1] is not None:
                    qk_evac(IN_TURN[n - 1])
                if n == 2:
                    for h in range(IDXH):
                        act.wait_ge(sem("idx_mm"), h + 1)
                        if h >= 2:
                            act.wait_ge(sem("idx_acc"), 2 * (h - 1))
                        nc.scalar.activation(relu[:, h % 2, :], PS[:, 4 + h % 2, 0:LOG], ACT.Relu).then_inc(sem("idx_relu"), 1)
            split_to(C_OUTE + STG)
            heads(0, NH, lg, pT)
            split_to(C_FF)
            split_to(C_FF + STG)
            norm(1)

            def ff_evac(j):
                for k in range(FB0[j], FB0[j + 1]):
                    act.wait_ge(sem("ff_tr"), k + 1)
                    nc.scalar.activation(act_hi[:, 2 * k:2 * k + 2, :],
                                         PS[:, 4 + k % 4, :].rearrange("p (d t) -> p d t", d=2), ACT.Copy)\
                        .then_inc(sem("ff_hi"), 1)

            for k in range(4 * FF_TILES + 4):
                split_to(max(nsplit[0], C_FF + k + 1))
                if k % 4 == 3 and k // 4 < FF_TILES:
                    j = k // 4
                    w = FF_W[j]
                    act.wait_ge(mm_done, C_FF + 4 * j + 2)
                    if j >= 1:
                        act.wait_ge(sem("up_read"), j)
                    nc.scalar.activation(sg[:, :, 0:w], PS[:, 0:2, 0:w], ACT.Silu).then_inc(sem("gate_read"), 1)
                if k % 4 == 3 and k >= 7:
                    ff_evac((k - 7) // 4)
            split_to(C_LAT + STG)

            norm(2)
            split_to(C_LAT + 4)
            act.wait_ge(mm_done, C_LAT + 4)
            split_to(C_HEADS + 3)
            for t in range(TT):
                for col, bank, c0, n, junk in (
                        (24, 0, 0, QR, sq1[:, t * QR:(t + 1) * QR]),
                        (26, 2, 0, KVR, sq1[:, TT * QR + t * KVR:TT * QR + (t + 1) * KVR]),
                        (28, 2, KVR, ROPE, kpj[:, t * ROPE:(t + 1) * ROPE])):
                    nc.scalar.activation(junk, PS[:, bank + t, c0:c0 + n], ACT.Square,
                                         accum_out=st[:, col + t:col + t + 1]).then_inc(sem("lat_ss"), 1)
            act.wait_ge(sem("lat_ms"), 1)
            nc.scalar.activation(st[:, 34:38], st[:, 30:34], ACT.Sqrt).then_inc(sem("lat_rt"), 1)
            for d in range(5):
                bank, off = ((4, 0), (4, S), (5, 0), (6, 0), (6, S))[d]
                act.wait_ge(sem("lat_tr"), bank - 3)
                nc.scalar.activation(lat_hi[:, d, :], PS[:, bank, off:off + S], ACT.Copy,
                                     scale=gain[:, G_QA + d:G_QA + d + 1]).then_inc(sem("lat_hi"), 1)
            for g in range(GROUPS):
                split_to(C_HEADS + 2 * g + 2)
                act.wait_ge(mm_done, C_HEADS + 2 * g + 2)
                if g >= 1:
                    act.wait_ge(sem("grp_sqread"), 2 * g)
                nc.scalar.activation(sq1[:, 0:TT * QR].rearrange("p (t n) -> p t n", t=TT),
                                     PS[:, 0:2, 0:GH * QKD], ACT.Square).then_inc(sem("grp_sq"), 1)
                nc.scalar.activation(sq1[:, TT * QR:TT * QR + TT * GH * 64].rearrange("p (t h n) -> p t h n", t=TT, h=GH),
                                     PS[:, 2:4, :].rearrange("p t (h n) -> p t h n", h=GH)[:, :, :, 0:64],
                                     ACT.Square).then_inc(sem("grp_sq"), 1)
                act.wait_ge(sem("grp_ms"), g + 1)
                nc.scalar.activation(st[:, 64:80], st[:, 48:64], ACT.Sqrt).then_inc(sem("grp_rt"), 1)
                split_to(C_HEADS + 2 * g + 4)
                for h in range(GH):
                    act.wait_ge(sem("grp_tr"), GH * g + h + 1)
                    if h % 2 == 0:
                        nc.scalar.activation(qkT[0:QKD, h, :], PS[0:QKD, 4 + h, :], ACT.Copy).then_inc(sem("grp_ev_act"), 1)
                heads(NH + GH * g, GH, lg1, pT1)
            split_to(C_MOE)
            norm(3)
            act.wait_ge(sem("top_sub"), 1)
            nc.scalar.activation(rt[:, 4, 0:TT * NE], rt[:, 3, 0:TT * NE], ACT.Exp).then_inc(sem("top_exp"), 1)

            act.wait_ge(sem("need_set"), 1)
            with act.Fori(0, 2) as b:
                with act.Fori(0, NE) as e:
                    i = b * NE + e
                    tokens = act.value_load(need[0:1, bass.ds(i, 1)], min_val=-S, max_val=S)
                    with act.If(tokens > 0):
                        def esplit(k):
                            c = C_MOE + k
                            act.wait_ge(raw_full[c % RAW], 16 * (c // RAW + 1) + i * (16 * EXPERT_CHUNKS // RAW))
                            act.wait_ge(mm_done, c - STG + 1 + i * EXPERT_CHUNKS)
                            nc.scalar.activation(w_hi[:, c % STG, :], raw[:, c % RAW, :], ACT.Copy).then_inc(hi_done, 1)
                        for k in range(STG):
                            esplit(k)
                        for h in range(2):
                            act.wait_ge(sem("moe_gath"), 2 * i + h + 1)
                            nc.scalar.activation(a_hi[:, 4 * h:4 * h + 4, 0:P],
                                                 PS[:, 4 + h, :].rearrange("p (d t) -> p d t", d=4), ACT.Copy)\
                                .then_inc(sem("moe_xhi"), 1)
                        for k in range(STG, EXPERT_CHUNKS):
                            esplit(k)
                            if k % 4 == 3 and k // 4 < FE_TILES:
                                j = k // 4
                                act.wait_ge(mm_done, C_MOE + 4 * j + 2 + i * EXPERT_CHUNKS)
                                if j >= 2:
                                    act.wait_ge(sem("moe_mul"), j - 1 + i * FE_TILES)
                                nc.scalar.activation(sge[:, j % 2, :], PS[:, j % 2, :], ACT.Silu).then_inc(sem("moe_silu"), 1)
                            if k % 4 == 3 and 7 <= k < 7 + 4 * FE_TILES:
                                j = (k - 7) // 4
                                act.wait_ge(sem("moe_tr"), j + 1 + i * FE_TILES)
                                nc.scalar.activation(e_hi[:, 4 * j:4 * j + 4, :],
                                                     PS[:, 6 + j % 2, :].rearrange("p (d t) -> p d t", d=4), ACT.Copy)\
                                    .then_inc(sem("moe_ahi"), 1)
                        act.wait_ge(mm_done, C_MOE + (i + 1) * EXPERT_CHUNKS)
                        nc.scalar.activation(y_hi[:, :].rearrange("p (a n) -> p a n", a=2), PS[:, 2:4, :], ACT.Copy,
                                             scale=st[:, 90:91]).then_inc(sem("moe_yhi"), 1)
                    with act.Else():
                        act.drain()
                        act.sem_inc(hi_done, EXPERT_CHUNKS)
                        act.sem_inc(sem("moe_xhi"), 2)
                        act.sem_inc(sem("moe_silu"), FE_TILES)
                        act.sem_inc(sem("moe_ahi"), FE_TILES)
                        act.sem_inc(sem("moe_yhi"), 1)

        @block.vector
        def _(dve):
            steps = [0]

            def step(ins):
                steps[0] += 1
                ins.then_inc(sem("dve_step"), 1)
                dve.wait_ge(sem("dve_step"), steps[0])

            nsplit = [0]

            def split(c):
                assert nsplit[0] == c
                nsplit[0] += 1
                n = chunks[c].shape[1] * chunks[c].shape[2]
                dve.wait_ge(hi_done, c + 1)
                nc.vector.tensor_tensor(w_lo[:, c % STG, 0:n], raw[:, c % RAW, 0:n], w_hi[:, c % STG, 0:n],
                                        ALU.subtract).then_inc(lo_done, 1)

            def split_to(c):
                while nsplit[0] < c:
                    split(nsplit[0])

            def norm(q):
                dve.wait_ge(sem("norm_ss"), 2 * q + 2)
                nc.vector.tensor_scalar(st[:, 8 + 2 * q:10 + 2 * q], st[:, 2 * q:2 * q + 2], 1.0 / D, EPS,
                                        ALU.mult, ALU.add).then_inc(sem("norm_ms"), 1)
                dve.wait_ge(sem("norm_rt"), q + 1)
                step(nc.vector.reciprocal(st[:, 24 - 24 + 40:42], st[:, 16 + 2 * q:18 + 2 * q]))
                for t in range(TT):
                    ins = nc.vector.tensor_scalar(xn[:, t, :], X[:, t, :], st[:, 40 + t:41 + t], None, ALU.mult)
                    if q == 3:
                        step(ins)
                        ins = nc.vector.tensor_tensor(xn[:, t, :], xn[:, t, :], ffg[:, :], ALU.mult)
                        ins.then_inc(sem("hn_set"), 1)
                    else:
                        ins.then_inc(sem("norm_xn"), 1)
                if q == 3:
                    for t in range(TT):
                        dve.wait_ge(sem("hnat_hi"), t + 1)
                        nc.vector.tensor_tensor(h_lo[:, t, :], xn[:, t, :], h_hi[:, t, :], ALU.subtract)\
                            .then_inc(sem("hnat_lo"), 1)
                for c in range(4):
                    dve.wait_ge(sem("norm_hi"), 8 * q + 2 * c + 2)
                    if q == 3:
                        nc.vector.tensor_tensor(a_lo[:, 2 * c:2 * c + 2, :],
                                                PS[:, 4 + c, :].rearrange("p (d t) -> p d t", d=2),
                                                a_hi[:, 2 * c:2 * c + 2, :], ALU.subtract).then_inc(sem("norm_lo"), 2)
                        continue
                    for d in range(2):
                        dc = 2 * c + d
                        nc.vector.scalar_tensor_tensor(out=a_lo[:, dc, :], in0=PS[:, 4 + c, d * S:(d + 1) * S],
                                                       scalar=gain[:, 8 * q + dc:8 * q + dc + 1],
                                                       in1=a_hi[:, dc, :].bitcast(f32), op0=ALU.mult,
                                                       op1=ALU.subtract).then_inc(sem("norm_lo"), 1)

            def heads(h0, n, logits, bias):
                for s in range(n + 3):
                    if s < n:
                        h = h0 + s
                        dve.wait_ge(sem("at_qk"), h + 1)
                        if h >= h0 + 4 or h >= 4:
                            dve.wait_ge(sem("at_tr"), h - 3)
                        bank = PS[:, 4 + h % 2, :]
                        if bias:
                            nc.vector.tensor_tensor(logits[:, h % 4, 0:P], bank[:, 0:P], brev[:, h, 0:P][:, ::-1], ALU.add)
                            nc.vector.tensor_tensor(logits[:, h % 4, P:LOG], bank[:, P:LOG], brev[:, h, :][:, ::-1],
                                                    ALU.add).then_inc(sem("at_add"), 1)
                            dve.wait_ge(sem("at_add"), h + 1)
                            if h >= 8:
                                step(nc.vector.tensor_tensor(logits[:, h % 4, :], logits[:, h % 4, :], dmask[:, :], ALU.add))
                        else:
                            nc.vector.tensor_tensor(logits[:, h % 4, :], bank[:, 0:LOG], mask, ALU.add)\
                                .then_inc(sem("at_add"), 1)
                            dve.wait_ge(sem("at_add"), h + 1)
                        nc.vector.tensor_reduce(nm[:, h, 0:1], logits[:, h % 4, 0:P], AX.X, ALU.max, negate=True)
                        nc.vector.tensor_reduce(nm[:, h, 1:2], logits[:, h % 4, P:LOG], AX.X, ALU.max, negate=True)\
                            .then_inc(sem("at_max"), 1)
                    if 1 <= s <= n:
                        h = h0 + s - 1
                        dve.wait_ge(sem("at_exp"), 2 * h + 2)
                        step(nc.vector.reciprocal(rs[:, h, 2:4], rs[:, h, 0:2]))
                        nc.vector.tensor_scalar(logits[:, h % 4, 0:P], logits[:, h % 4, 0:P], rs[:, h, 2:3], None, ALU.mult)
                        nc.vector.tensor_scalar(logits[:, h % 4, P:LOG], logits[:, h % 4, P:LOG], rs[:, h, 3:4], None,
                                                ALU.mult).then_inc(sem("at_norm"), 1)
                    if s >= 3 and (h0 + s - 3) % 2:
                        h = h0 + s - 3
                        dve.wait_ge(sem("at_ohi"), h // 2 + 1)
                        nc.vector.tensor_tensor(a_lo[:, h // 2 % 8, :], PS[:, h // 2 % 2, 0:S], a_hi[:, h // 2 % 8, :],
                                                ALU.subtract).then_inc(sem("at_olo"), 1)

            nc.vector.memset(bias_in[BUCKETS:BUCKETS + 1, LOG:LOG + 16], 1.0).then_inc(sem("ones_set"), 1)
            dve.wait_ge(sem("set_tr"), 2)
            nc.vector.tensor_copy(brow[:, :], PS[0:16, 1, 0:LOG]).then_inc(sem("brow_set"), 1)
            nc.vector.tensor_copy(gain[:, 0:G_ROWS], PS[:, 0, 0:G_ROWS]).then_inc(sem("gain_copy"), 1)
            dve.wait_ge(sem("gain_copy"), 1)
            nc.vector.tensor_scalar(gain[:, G_ROWS:G_ROWS + 4], gain[:, G_HEAD:G_HEAD + 4], HD ** -0.5, None, ALU.mult)\
                .then_inc(sem("gain_set"), 1)
            dve.wait_ge(sem("gain_set"), 1)
            split_to(STG)
            norm(0)
            def top_rounds(r0, r1):
                for r in range(r0, r1):
                    nc.vector.max(top8[:, 0:8], score[:, 0:P])
                    step(nc.vector.max(top8[:, 8:16], score[:, P:LOG]))
                    nc.vector.match_replace(score[:, 0:P], top8[:, 0:8], score[:, 0:P], TAKEN)
                    step(nc.vector.match_replace(score[:, P:LOG], top8[:, 8:16], score[:, P:LOG], TAKEN))

            for n in range(7):
                split_to(min(C_IN + 2 * n + 4, C_OUTE + 1))
                dve.wait_ge(mm_done, C_IN + 2 * n + 2)
                pair = PS[:, 2 * (n % 2):2 * (n % 2) + 2, :]
                m = IN_TURN[n]
                if m:
                    dve.wait_ge(sem("sq_set"), m)
                    nc.vector.tensor_reduce(st[:, 80:96], sq[:, :, :].rearrange("p t (h d) -> p (t h) d", d=HD), AX.X, ALU.add)\
                        .then_inc(sem("sq_read"), 1)
                    dve.wait_ge(sem("sq_read"), m)
                    nc.vector.tensor_scalar(st[:, 48:64], st[:, 80:96], 1.0 / HD, EPS, ALU.mult, ALU.add)\
                        .then_inc(sem("qk_ms"), 1)
                    dve.wait_ge(sem("qk_rt"), m)
                    step(nc.vector.reciprocal(st[:, 48:64], st[:, 64:80]))
                    if m >= 3:
                        dve.wait_ge(sem("qk_tr"), 2 * (m - 1))
                    nc.vector.tensor_tensor(qn[:, m % 2, :, :].rearrange("p t (h d) -> p t h d", d=HD),
                                            pair.rearrange("p t (h d) -> p t h d", d=HD),
                                            st[:, 48:64].rearrange("p (t h) -> p t h", t=TT).unsqueeze(3).to_broadcast([P, TT, 8, HD]),
                                            ALU.mult).then_inc(sem("tile_read"), 1)
                elif n:
                    if n == 3:
                        dve.wait_ge(sem("norm_t"), 4)
                    nc.vector.tensor_copy(v0[:, :, (n // 6) * NT:(n // 6 + 1) * NT], pair).then_inc(sem("tile_read"), 1)
                else:
                    nc.vector.tensor_copy(idxn[:, :, 0:320], pair[:, :, 0:320])
                    nc.vector.tensor_copy(idxn[:, :, 320:384], pair[:, :, 256:320])
                    nc.vector.tensor_scalar(st[:, 16:24].rearrange("p (t h) -> p t h", t=TT), pair[:, :, 320:324],
                                            HD ** -0.5 * IDXH ** -0.5, None, ALU.mult).then_inc(sem("tile_read"), 1)
                if n == 2:
                    for h in range(IDXH):
                        dve.wait_ge(sem("idx_relu"), h + 1)
                        for t, (a, b) in enumerate(((0, P), (P, LOG))):
                            if h:
                                dve.wait_ge(sem("idx_acc"), 2 * h - 1 + t)
                            nc.vector.scalar_tensor_tensor(out=score[:, a:b], in0=relu[:, h % 2, a:b],
                                                           scalar=st[:, 16 + 4 * t + h:17 + 4 * t + h],
                                                           in1=(score[:, a:b] if h else cst[:, K_MASK + a:K_MASK + b]),
                                                           op0=ALU.mult, op1=ALU.add).then_inc(sem("idx_acc"), 1)
                    dve.wait_ge(sem("idx_acc"), 2 * IDXH)
                if 3 <= n <= 6:
                    top_rounds(2 * (n - 3), 2 * (n - 2))
            step(nc.vector.tensor_scalar(dmask[:, :], score[:, :], TAKEN / 2, MASKED, ALU.is_gt, ALU.mult))
            split_to(C_OUTE + STG)
            dve.wait_ge(sem("bias_in"), 16)
            heads(0, NH, lg, True)

            def residual(c_last, bank, n, k):
                dve.wait_ge(mm_done, c_last + 1)
                ins = nc.vector.tensor_tensor(X[:, :, n * NT:(n + 1) * NT], X[:, :, n * NT:(n + 1) * NT],
                                              PS[:, bank:bank + 2, :], ALU.add)
                ins.then_inc(sem("resid"), 1) if n == 1 else None

            split_to(C_OUTE + 4)
            residual(C_OUTE + 1, 0, 0, 0)
            residual(C_OUTE + 3, 2, 1, 0)
            split_to(C_FF + STG)
            norm(1)

            def ff_evac(j):
                for k in range(FB0[j], FB0[j + 1]):
                    dve.wait_ge(sem("ff_hi"), k + 1)
                    nc.vector.tensor_tensor(act_lo[:, 2 * k:2 * k + 2, :],
                                            PS[:, 4 + k % 4, :].rearrange("p (d t) -> p d t", d=2),
                                            act_hi[:, 2 * k:2 * k + 2, :], ALU.subtract).then_inc(sem("ff_lo"), 1)

            for k in range(4 * FF_TILES + 4):
                split_to(max(nsplit[0], C_FF + k + 1))
                if k % 4 == 1 and k >= 5:
                    j = (k - 5) // 4
                    w = FF_W[j]
                    dve.wait_ge(sem("gate_read"), j + 1)
                    dve.wait_ge(mm_done, C_FF + 4 * j + 4)
                    if j >= 2:
                        dve.wait_ge(sem("ff_tr"), FB0[j - 1])
                    nc.vector.tensor_tensor(hn[:, j % 2, :, 0:w], PS[:, 2:4, 0:w], sg[:, :, 0:w], ALU.mult)\
                        .then_inc(sem("up_read"), 1)
                if k % 4 == 3 and k >= 7:
                    ff_evac((k - 7) // 4)
            split_to(C_LAT)
            dve.wait_ge(mm_done, C_LAT)
            nc.vector.tensor_tensor(X[:, :, :].rearrange("p t (a n) -> p (t a) n", a=2),
                                    X[:, :, :].rearrange("p t (a n) -> p (t a) n", a=2),
                                    PS[:, 0:4, :], ALU.add).then_inc(sem("resid"), 1)
            split_to(C_LAT + STG)
            norm(2)
            split_to(C_HEADS + 3)
            dve.wait_ge(sem("lat_ss"), 6)
            nc.vector.tensor_scalar(st[:, 30:32], st[:, 24:26], 1.0 / QR, EPS, ALU.mult, ALU.add)
            nc.vector.tensor_scalar(st[:, 32:34], st[:, 26:28], 1.0 / KVR, EPS, ALU.mult, ALU.add)\
                .then_inc(sem("lat_ms"), 1)
            dve.wait_ge(sem("lat_rt"), 1)
            step(nc.vector.reciprocal(st[:, 44:48], st[:, 34:38]))
            for t in range(TT):
                nc.vector.tensor_scalar(latn[:, t, 0:QR], PS[:, t, 0:QR], st[:, 44 + t:45 + t], None, ALU.mult)
                nc.vector.tensor_copy(kpe[:, t, :], PS[:, 2 + t, KVR:KVR + ROPE])
                nc.vector.tensor_scalar(latn[:, t, QR:QR + KVR], PS[:, 2 + t, 0:KVR], st[:, 46 + t:47 + t], None, ALU.mult)\
                    .then_inc(sem("lat_n"), 1)
            for d in range(5):
                bank, off = ((4, 0), (4, S), (5, 0), (6, 0), (6, S))[d]
                dve.wait_ge(sem("lat_hi"), (2, 2, 3, 5, 5)[d])
                nc.vector.scalar_tensor_tensor(out=lat_lo[:, d, :], in0=PS[:, bank, off:off + S],
                                               scalar=gain[:, G_QA + d:G_QA + d + 1],
                                               in1=lat_hi[:, d, :].bitcast(f32), op0=ALU.mult, op1=ALU.subtract)\
                    .then_inc(sem("lat_lo"), 1)
            dve.wait_ge(sem("gbc_in"), 32)
            step(nc.vector.tensor_scalar(gbc[:, 0, :], gbc[:, 0, :], QKD ** -0.5, None, ALU.mult))
            TH = TT * GH
            for g in range(GROUPS):
                split_to(C_HEADS + 2 * g + 2)
                dve.wait_ge(sem("grp_sq"), 2 * g + 2)
                nc.vector.tensor_reduce(st[:, 80:80 + TH], sq1[:, 0:TT * QR].rearrange("p (a n) -> p a n", n=QKD),
                                        AX.X, ALU.add).then_inc(sem("grp_sqread"), 1)
                nc.vector.tensor_reduce(st[:, 80 + TH:96],
                                        sq1[:, TT * QR:TT * QR + TH * 64].rearrange("p (a n) -> p a n", n=64),
                                        AX.X, ALU.add).then_inc(sem("grp_sqread"), 1)
                dve.wait_ge(sem("grp_sqread"), 2 * g + 2)
                for t in range(TT):
                    ins = nc.vector.tensor_scalar(st[:, 80 + TH + GH * t:80 + TH + GH * t + GH],
                                                  st[:, 80 + TH + GH * t:80 + TH + GH * t + GH],
                                                  st[:, 28 + t:29 + t], None, ALU.add)
                step(ins)
                nc.vector.tensor_scalar(st[:, 48:64], st[:, 80:96], 1.0 / QKD, EPS, ALU.mult, ALU.add)\
                    .then_inc(sem("grp_ms"), 1)
                dve.wait_ge(sem("grp_rt"), g + 1)
                step(nc.vector.reciprocal(st[:, 48:64], st[:, 64:80]))
                if g >= 1:
                    dve.wait_ge(sem("grp_tr"), GH * g)
                    dve.wait_ge(sem("at_pv"), NH + GH * g)
                rq = st[:, 48:48 + TH].rearrange("p (t h) -> p t h", t=TT)
                rk = st[:, 48 + TH:64].rearrange("p (t h) -> p t h", t=TT)
                q4 = qk[:, 0:TH, :].rearrange("p (t h) n -> p t h n", t=TT)
                k4 = qk[:, TH:2 * TH, :].rearrange("p (t h) n -> p t h n", t=TT)
                kv = PS[:, 2:4, :].rearrange("p t (h n) -> p t h n", h=GH)
                nc.vector.tensor_tensor(q4, PS[:, 0:2, 0:GH * QKD].rearrange("p t (h n) -> p t h n", h=GH),
                                        rq.unsqueeze(3).to_broadcast([P, TT, GH, QKD]), ALU.mult)
                nc.vector.tensor_tensor(k4[:, :, :, 0:64], kv[:, :, :, 0:64],
                                        rk.unsqueeze(3).to_broadcast([P, TT, GH, 64]), ALU.mult)
                nc.vector.tensor_copy(v1[:, :, :].rearrange("p t (h n) -> p t h n", h=GH), kv[:, :, :, 64:128])
                step(nc.vector.tensor_tensor(k4[:, :, :, 64:96], kpe[:, :, :].unsqueeze(2).to_broadcast([P, TT, GH, ROPE]),
                                             rk.unsqueeze(3).to_broadcast([P, TT, GH, ROPE]), ALU.mult))
                qk2 = qk[:, :, :].rearrange("p (s a) n -> p s a n", s=2)
                step(nc.vector.tensor_tensor(qk2, qk2, gbc[:, :, :].unsqueeze(2).to_broadcast([P, 2, TH, QKD]), ALU.mult))
                x1, x2 = qk2[:, :, :, 64:80], qk2[:, :, :, 80:96]
                cos = cst[:, K_COS:K_COS + P].rearrange("p (a n) -> p a n", n=16).unsqueeze(1).to_broadcast([P, 2, TH, 16])
                sin = cst[:, K_SIN:K_SIN + P].rearrange("p (a n) -> p a n", n=16).unsqueeze(1).to_broadcast([P, 2, TH, 16])
                r4 = [rot[:, k, :, :].rearrange("p (s a) n -> p s a n", s=2) for k in range(4)]
                nc.vector.tensor_tensor(r4[0], x1, cos, ALU.mult)
                nc.vector.tensor_tensor(r4[1], x2, sin, ALU.mult)
                nc.vector.tensor_tensor(r4[2], x1, sin, ALU.mult)
                step(nc.vector.tensor_tensor(r4[3], x2, cos, ALU.mult))
                nc.vector.tensor_tensor(x1, r4[0], r4[1], ALU.subtract)
                nc.vector.tensor_tensor(x2, r4[2], r4[3], ALU.add).then_inc(sem("grp_qk"), 1)
                split_to(C_HEADS + 2 * g + 4)
                for h in range(1, GH, 2):
                    dve.wait_ge(sem("grp_tr"), GH * g + h + 1)
                    nc.vector.tensor_copy(qkT[0:QKD, h, :], PS[0:QKD, 4 + h, :]).then_inc(sem("grp_ev_dve"), 1)
                heads(NH + GH * g, GH, lg1, False)
            split_to(C_OUTO + 4)
            residual(C_OUTO + 1, 0, 0, 0)
            residual(C_OUTO + 3, 2, 1, 0)
            split_to(C_MOE)
            dve.wait_ge(sem("ffg_in"), 16)
            norm(3)

            dve.wait_ge(sem("bias8_in"), 16)
            dve.wait_ge(mm_done, C_ROUTE + 1)
            R = lambda k: rt[:, k, 0:TT * NE].rearrange("p (t e) -> p t e", t=TT)
            F = lambda k: rt[:, k, :].rearrange("p (t e f) -> p t e f", t=TT, e=NE)
            wide = [P, TT, NE, NE]
            step(nc.vector.tensor_tensor(R(0), PS[:, 0:2, 0:NE],
                                         gate_bias[:, :].unsqueeze(1).to_broadcast([P, TT, NE]), ALU.add))
            other, own = R(0).unsqueeze(2).to_broadcast(wide), R(0).unsqueeze(3).to_broadcast(wide)
            low = cst[:, K_LOW:K_LOW + NE * NE].rearrange("p (e f) -> p e f", e=NE).unsqueeze(1).to_broadcast(wide)
            nc.vector.tensor_tensor(F(1), other, own, ALU.is_gt)
            nc.vector.tensor_reduce(st[:, 40:42], R(0), AX.X, ALU.max)
            step(nc.vector.tensor_tensor(F(2), other, own, ALU.is_equal))
            nc.vector.tensor_tensor(R(3), R(0), st[:, 40:42].unsqueeze(2).to_broadcast([P, TT, NE]), ALU.subtract)\
                .then_inc(sem("top_sub"), 1)
            step(nc.vector.tensor_tensor(F(2), F(2), low, ALU.mult))
            step(nc.vector.tensor_tensor(F(1), F(1), F(2), ALU.add))
            step(nc.vector.tensor_reduce(R(5), F(1), AX.X, ALU.add))
            nc.vector.tensor_scalar(R(6), R(5), 1.5, None, ALU.is_lt).then_inc(sem("sel_set"), 1)
            dve.wait_ge(sem("sel_set"), 1)
            dve.wait_ge(sem("top_exp"), 1)
            step(nc.vector.tensor_tensor(R(4), R(4), R(6), ALU.mult))
            step(nc.vector.tensor_reduce(st[:, 42:44], R(4), AX.X, ALU.add))
            step(nc.vector.reciprocal(st[:, 40:42], st[:, 42:44]))
            step(nc.vector.tensor_tensor(comb[:, :, :], R(4), st[:, 40:42].unsqueeze(2).to_broadcast([P, TT, NE]), ALU.mult))
            FAR = 1000.0
            dve.wait_ge(sem("place_mm"), 1)
            step(nc.vector.tensor_scalar(R(7), PS[:, 4:6, 0:NE], FAR, None, ALU.add))
            step(nc.vector.tensor_tensor(R(7), R(7), R(6), ALU.mult))
            for b in range(2):
                nc.vector.tensor_scalar(pos[:, :, b * NE:(b + 1) * NE], R(7), -FAR - b * P, None, ALU.add)
                ins = nc.vector.tensor_scalar(need[0:1, b * NE:(b + 1) * NE], PS[0:1, 6, 0:NE], -float(b * P), None, ALU.add)
            ins.then_inc(sem("need_set"), 1)
            dve.wait_ge(sem("need_set"), 1)

            with dve.Fori(0, 2) as b:
                with dve.Fori(0, NE) as e:
                    i = b * NE + e
                    tokens = dve.value_load(need[0:1, bass.ds(i, 1)], min_val=-S, max_val=S)
                    with dve.If(tokens > 0):
                        def esplit(k):
                            c = C_MOE + k
                            dve.wait_ge(hi_done, c + 1 + i * EXPERT_CHUNKS)
                            nc.vector.tensor_tensor(w_lo[:, c % STG, :], raw[:, c % RAW, :], w_hi[:, c % STG, :],
                                                    ALU.subtract).then_inc(lo_done, 1)
                        for t in range(TT):
                            nc.vector.tensor_scalar(pick[:, t, :], iota, pos[:, t, bass.ds(i, 1)], None, ALU.is_equal)
                            ins = nc.vector.tensor_scalar(pickg[:, t, :], iota, pos[:, t, bass.ds(i, 1)],
                                                          comb[:, t, bass.ds(e, 1)], ALU.is_equal, ALU.mult)
                        ins.then_inc(sem("moe_pick"), 1)
                        for k in range(STG):
                            esplit(k)
                        for h in range(2):
                            dve.wait_ge(sem("moe_xhi"), 2 * i + h + 1)
                            nc.vector.tensor_tensor(a_lo[:, 4 * h:4 * h + 4, 0:P],
                                                    PS[:, 4 + h, :].rearrange("p (d t) -> p d t", d=4),
                                                    a_hi[:, 4 * h:4 * h + 4, 0:P], ALU.subtract).then_inc(sem("moe_xlo"), 1)
                        dve.wait_ge(sem("moe_turn"), i + 1)
                        nc.vector.tensor_reduce(st[:, 90:91], PS[:, 6, 0:S], AX.X, ALU.add)
                        nc.vector.tensor_scalar(backT[:, :], PS[:, 6, 0:S], 0.0, None, ALU.is_gt).then_inc(sem("moe_back"), 1)
                        for k in range(STG, EXPERT_CHUNKS):
                            esplit(k)
                            if k % 4 == 1 and 5 <= k < 5 + 4 * FE_TILES:
                                j = (k - 5) // 4
                                dve.wait_ge(sem("moe_silu"), j + 1 + i * FE_TILES)
                                dve.wait_ge(mm_done, C_MOE + 4 * j + 4 + i * EXPERT_CHUNKS)
                                if j >= 2:
                                    dve.wait_ge(sem("moe_tr"), j - 1 + i * FE_TILES)
                                nc.vector.tensor_tensor(he[:, j % 2, :], PS[:, 2 + j % 2, :], sge[:, j % 2, :], ALU.mult)\
                                    .then_inc(sem("moe_mul"), 1)
                            if k % 4 == 3 and 7 <= k < 7 + 4 * FE_TILES:
                                j = (k - 7) // 4
                                dve.wait_ge(sem("moe_ahi"), j + 1 + i * FE_TILES)
                                nc.vector.tensor_tensor(e_lo[:, 4 * j:4 * j + 4, :],
                                                        PS[:, 6 + j % 2, :].rearrange("p (d t) -> p d t", d=4),
                                                        e_hi[:, 4 * j:4 * j + 4, :], ALU.subtract).then_inc(sem("moe_alo"), 1)
                        dve.wait_ge(sem("moe_yhi"), i + 1)
                        nc.vector.scalar_tensor_tensor(out=y_lo[:, :].rearrange("p (a n) -> p a n", a=2), in0=PS[:, 2:4, :],
                                                       scalar=st[:, 90:91],
                                                       in1=y_hi[:, :].bitcast(f32).rearrange("p (a n) -> p a n", a=2),
                                                       op0=ALU.mult, op1=ALU.subtract).then_inc(sem("moe_ylo"), 1)
                        for s in range(4):
                            t, h = s // 2, s % 2
                            dve.wait_ge(sem("moe_sc"), 4 * i + s + 1)
                            nc.vector.tensor_tensor(X[:, t, h * NT:(h + 1) * NT], X[:, t, h * NT:(h + 1) * NT],
                                                    PS[:, 4 + s % 2, :], ALU.add).then_inc(sem("moe_add"), 1)
                    with dve.Else():
                        dve.drain()
                        dve.sem_inc(lo_done, EXPERT_CHUNKS)
                        dve.sem_inc(sem("moe_pick"), 1)
                        dve.sem_inc(sem("moe_xlo"), 2)
                        dve.sem_inc(sem("moe_back"), 1)
                        dve.sem_inc(sem("moe_mul"), FE_TILES)
                        dve.sem_inc(sem("moe_alo"), FE_TILES)
                        dve.sem_inc(sem("moe_ylo"), 1)
                        dve.sem_inc(sem("moe_add"), 4)

        @block.gpsimd
        def _(pool):
            pool.wait_ge(sem("brow_set"), 1)
            pool.dma_start(bias_dram[:, :], brow[:, :]).then_inc(sem("bias_out"), 16)
            pool.wait_ge(sem("bias_out"), 16)
            with nc.allow_non_contiguous_dma(reason="a window of the table for each partition"):
                pool.dma_start(brev[:, :, :], bass.AP(bias_dram, 0, [[1, P], [LOG, NH], [1, S]]))\
                    .then_inc(sem("bias_in"), 16)
            pool.dma_start(gate_bias[:, :], b_router.to_broadcast([P, NE])).then_inc(sem("bias8_in"), 16)
            pool.wait_ge(sem("resid"), 2)
            pool.dma_start(gbc[:, 0, :], mla_q_norm.to_broadcast([P, QKD])).then_inc(sem("gbc_in"), 16)
            pool.dma_start(gbc[:, 1, :], mla_k_norm.to_broadcast([P, QKD])).then_inc(sem("gbc_in"), 16)
            pool.wait_ge(sem("resid"), 3)
            pool.dma_start(ffg[:, :], ffn_norm_o.to_broadcast([P, D])).then_inc(sem("ffg_in"), 16)

        @block.tensor
        def _(pe):
            def product(dst, xh, xl, wh, wl, first, last):
                nc.tensor.matmul(dst, xh, wh, start=first, stop=False)
                nc.tensor.matmul(dst, xh, wl, start=False, stop=False)
                return nc.tensor.matmul(dst, xl, wh, start=False, stop=last)

            def chunk(c, kn, n, body):
                pe.wait_ge(lo_done, c + 1)
                hi = w_hi[:, c % STG, 0:kn * n].rearrange("p (k n) -> p k n", k=kn)
                lo = w_lo[:, c % STG, 0:kn * n].rearrange("p (k n) -> p k n", k=kn)
                body(hi, lo).then_inc(mm_done, 1)

            def project(c0, nchunks, kn, n, bank, xh=a_hi, xl=a_lo, x0=0):
                for q in range(nchunks):
                    def body(hi, lo):
                        for t in range(TT):
                            for k in range(kn):
                                kk = x0 + q * kn + k
                                ins = product(PS[:, bank + t, 0:n], xh[:, kk, t * P:(t + 1) * P], xl[:, kk, t * P:(t + 1) * P],
                                              hi[:, k, :], lo[:, k, :], q == 0 and k == 0, q == nchunks - 1 and k == kn - 1)
                        return ins
                    chunk(c0 + q, kn, n, body)

            def norm(q):
                pe.wait_ge(sem("norm_xn"), 2 * q + 2) if q < 3 else pe.wait_ge(sem("hn_set"), 2)
                for c in range(4):
                    for d in range(2):
                        for t in range(TT):
                            dc = 2 * c + d
                            ins = nc.tensor.transpose(PS[:, 4 + c, d * S + t * P:d * S + (t + 1) * P],
                                                      xn[:, t, dc * P:(dc + 1) * P], ident)
                    ins.then_inc(sem("norm_t"), 1)
                pe.wait_ge(sem("norm_lo"), 8 * (q + 1))

            def heads(h0, n, q_of, k_of, v_of, probs_t):
                for s in range(n + 3):
                    if s < n:
                        h = h0 + s
                        if h >= 2:
                            pe.wait_ge(sem("at_add"), h - 1)
                        bank = PS[:, 4 + h % 2, :]
                        nc.tensor.matmul(bank[:, 0:P], q_of(h, 0), k_of(h)[:, 0:P], start=True, stop=True)
                        nc.tensor.matmul(bank[:, P:LOG], q_of(h, 1), k_of(h), start=True, stop=True).then_inc(sem("at_qk"), 1)
                    if 2 <= s <= n + 1:
                        h = h0 + s - 2
                        pe.wait_ge(sem("at_norm"), h + 1)
                        if h >= 2:
                            pe.wait_ge(sem("at_pt"), h - 1)
                        lgb = (lg if h < NH else lg1)
                        for k in range(3):
                            ins = nc.tensor.transpose(PS[:, 6 + h % 2, k * P:(k + 1) * P], lgb[:, h % 4, k * P:(k + 1) * P], ident)
                        ins.then_inc(sem("at_tr"), 1)
                    if s >= 3:
                        h = h0 + s - 3
                        pe.wait_ge(sem("at_pt"), h + 1)
                        if h >= 4 and h % 2 == 0:
                            pe.wait_ge(sem("at_olo"), h // 2 - 1)
                        dst = PS[64 * (h % 2):64 * (h % 2) + 64, h // 2 % 2, 0:S]
                        nc.tensor.matmul(dst, v_of(h, 0), probs_t[:, h % 2, 0:S], start=True, stop=False)
                        nc.tensor.matmul(dst[:, P:S], v_of(h, 1), probs_t[:, h % 2, S:LOG], start=False, stop=True)\
                            .then_inc(sem("at_pv"), 1)

            pe.wait_ge(sem("x_in"), 32)
            pe.wait_ge(sem("small_in"), 16 * N_SMALL)
            pe.wait_ge(sem("ones_set"), 1)
            nc.tensor.transpose(PS[:, 0, 0:G_ROWS], grow[:, :], cst[0:G_ROWS, K_ID:K_ID + G_ROWS]).then_inc(sem("set_tr"), 1)
            nc.tensor.matmul(PS[0:16, 1, 0:LOG], bias_in[:, LOG:LOG + 16], bias_in[:, 0:LOG], start=True, stop=True)\
                .then_inc(sem("set_tr"), 1)
            norm(0)
            def turn_heads(m):
                if m == 2:
                    pe.wait_ge(sem("idx_relu"), IDXH)
                if m >= 2:
                    pe.wait_ge(sem("qk_evac"), 2 * (m - 1))
                for half in range(2):
                    bank = 4 + 2 * (m % 2) + half
                    for d in range(2 if (m or half == 0) else 1):
                        for t in range(TT):
                            f = (2 * half + d) * P
                            src = qn[:, m % 2, t, f:f + P] if m else idxn[:, t, f:f + P]
                            ins = nc.tensor.transpose(PS[:, bank, d * S + t * P:d * S + (t + 1) * P], src, ident)
                    ins.then_inc(sem("qk_tr"), 1)

            def turn_after(n):
                if IN_TURN[n] is not None:
                    pe.wait_ge(sem("tile_read"), n + 1)
                    turn_heads(IN_TURN[n])

            for n in range(7):
                if n >= 2:
                    pe.wait_ge(sem("tile_read"), n - 1)
                elif n == 0:
                    pe.wait_ge(sem("brow_set"), 1)
                    pe.wait_ge(sem("gain_copy"), 1)
                project(C_IN + 2 * n, 2, 4, IN_TILES[n][1], 2 * (n % 2))
                if n >= 1:
                    turn_after(n - 1)
                if n == 2:
                    pe.wait_ge(sem("qk_evac"), 2)
                    for h in range(IDXH):
                        r = HD * (h % 2)
                        if h >= 2:
                            pe.wait_ge(sem("idx_relu"), h - 1)
                        nc.tensor.matmul(PS[:, 4 + h % 2, 0:P], iqT[r:r + HD, h // 2, 0:P], ikT[r:r + HD, 0:P], start=True, stop=True)
                        nc.tensor.matmul(PS[:, 4 + h % 2, P:LOG], iqT[r:r + HD, h // 2, P:S], ikT[r:r + HD, :], start=True, stop=True)\
                            .then_inc(sem("idx_mm"), 1)
            pe.wait_ge(sem("tile_read"), 7)
            pe.wait_ge(sem("qk_evac"), 10)

            def r0(h):
                return HD * (h % 2)
            heads(0, NH, lambda h, t: qT0[r0(h):r0(h) + HD, h // 2, t * P:(t + 1) * P],
                  lambda h: kT0[r0(h):r0(h) + HD, h // 2, :],
                  lambda h, t: v0[:, t, h * HD:(h + 1) * HD], pT)
            pe.wait_ge(sem("at_olo"), NH // 2)
            for n in range(2):
                project(C_OUTE + 2 * n, 2, 4, NT, 2 * n)
            norm(1)

            def turn_ff(j):
                pe.wait_ge(sem("up_read"), j + 1)
                for k in range(FB0[j], FB0[j + 1]):
                    if k >= 4:
                        pe.wait_ge(sem("ff_lo"), k - 3)
                    for d in range(2):
                        for t in range(TT):
                            f = (2 * (k - FB0[j]) + d) * P
                            ins = nc.tensor.transpose(PS[:, 4 + k % 4, d * S + t * P:d * S + (t + 1) * P],
                                                      hn[:, j % 2, t, f:f + P], ident)
                    ins.then_inc(sem("ff_tr"), 1)

            for j in range(FF_TILES):
                if j:
                    pe.wait_ge(sem("gate_read"), j)
                project(C_FF + 4 * j, 2, 4, FF_W[j], 0)
                if j:
                    turn_ff(j - 1)
                project(C_FF + 4 * j + 2, 2, 4, FF_W[j], 2)
            pe.wait_ge(sem("gate_read"), FF_TILES)
            pe.wait_ge(sem("up_read"), FF_TILES)
            for q in range(FFD // 256):
                pe.wait_ge(sem("ff_lo"), q + 1)

                def body(hi, lo):
                    for t in range(TT):
                        for k in range(2):
                            f = 2 * q + k
                            xs = [a[:, f, t * P:(t + 1) * P] for a in (act_hi, act_lo)]
                            for half in range(2):
                                cols = slice(half * NT, (half + 1) * NT)
                                ins = product(PS[:, 2 * t + half, :], *xs, hi[:, k, cols], lo[:, k, cols],
                                              f == 0, f == FFD // P - 1)
                    return ins
                chunk(C_FD + q, 2, D, body)
                if q == 1:
                    turn_ff(FF_TILES - 1)
            norm(2)
            for n in range(2):
                project(C_LAT + 2 * n, 2, 4, LAT[n][1], 2 * n)
            pe.wait_ge(sem("lat_n"), 2)
            for d in range(5):
                bank, off = ((4, 0), (4, S), (5, 0), (6, 0), (6, S))[d]
                for t in range(TT):
                    ins = nc.tensor.transpose(PS[:, bank, off + t * P:off + (t + 1) * P], latn[:, t, d * P:(d + 1) * P], ident)
                if d in (1, 2, 4):
                    ins.then_inc(sem("lat_tr"), 1)
            pe.wait_ge(sem("lat_lo"), 5)
            for g in range(GROUPS):
                if g:
                    pe.wait_ge(sem("at_olo"), NH // 2 + GH // 2 * g)
                project(C_HEADS + 2 * g, 1, 3, GH * QKD, 0, lat_hi, lat_lo, 0)
                project(C_HEADS + 2 * g + 1, 1, 2, GH * P, 2, lat_hi, lat_lo, 3)
                pe.wait_ge(sem("grp_qk"), g + 1)
                for h in range(GH):
                    for s in range(2):
                        for t in range(TT):
                            ins = nc.tensor.transpose(PS[0:QKD, 4 + h, s * S + t * P:s * S + (t + 1) * P],
                                                      qk[:, s * TT * GH + t * GH + h, :], ident)
                    ins.then_inc(sem("grp_tr"), 1)
                pe.wait_ge(sem("grp_ev_act"), GH // 2 * (g + 1))
                pe.wait_ge(sem("grp_ev_dve"), GH // 2 * (g + 1))
                heads(NH + GH * g, GH, lambda h, t: qkT[0:QKD, h % GH, t * P:(t + 1) * P],
                      lambda h: qkT[0:QKD, h % GH, S:2 * S],
                      lambda h, t: v1[:, t, (h % GH) * 64:(h % GH + 1) * 64], pT1)
            pe.wait_ge(sem("at_olo"), NH)
            for n in range(2):
                project(C_OUTO + 2 * n, 2, 4, NT, 2 * n)
            norm(3)
            project(C_ROUTE, 1, DC, NE, 0)
            pe.wait_ge(sem("sel_set"), 1)
            tri, ones = cst[:, K_TRI:K_TRI + P], cst[:, K_ONES:K_ONES + P]
            sel = [rt[:, 6, t * NE:(t + 1) * NE] for t in range(TT)]
            nc.tensor.matmul(PS[:, 4, 0:NE], tri, sel[0], start=True, stop=True)
            nc.tensor.matmul(PS[:, 5, 0:NE], ones, sel[0], start=True, stop=False)
            nc.tensor.matmul(PS[:, 5, 0:NE], tri, sel[1], start=False, stop=True)
            nc.tensor.matmul(PS[:, 6, 0:NE], ones, sel[0], start=True, stop=False)
            nc.tensor.matmul(PS[:, 6, 0:NE], ones, sel[1], start=False, stop=True).then_inc(sem("place_mm"), 1)
            pe.wait_ge(sem("hnat_lo"), 2)
            pe.wait_ge(sem("need_set"), 1)
            with pe.Fori(0, 2) as b:
                with pe.Fori(0, NE) as e:
                    i = b * NE + e
                    tokens = pe.value_load(need[0:1, bass.ds(i, 1)], min_val=-S, max_val=S)
                    with pe.If(tokens > 0):
                        pe.wait_ge(sem("moe_pick"), i + 1)
                        for dc in range(DC):
                            for t in range(TT):
                                for h, part in enumerate((h_hi, h_lo)):
                                    ins = nc.tensor.matmul(PS[:, 4 + dc // 4, (dc % 4) * P:(dc % 4 + 1) * P],
                                                           part[:, t, dc * P:(dc + 1) * P], pick[:, t, :],
                                                           start=(t == 0 and h == 0), stop=(t == 1 and h == 1))
                            if dc % 4 == 3:
                                ins.then_inc(sem("moe_gath"), 1)
                        for t in range(TT):
                            ins = nc.tensor.transpose(PS[:, 6, t * P:(t + 1) * P], pickg[:, t, :], ident)
                        ins.then_inc(sem("moe_turn"), 1)

                        def echunk(k, kn, n, body):
                            c = C_MOE + k
                            pe.wait_ge(lo_done, c + 1 + i * EXPERT_CHUNKS)
                            hi = w_hi[:, c % STG, :].rearrange("p (k n) -> p k n", k=kn)
                            lo = w_lo[:, c % STG, :].rearrange("p (k n) -> p k n", k=kn)
                            body(hi, lo).then_inc(mm_done, 1)

                        def turn(j):
                            pe.wait_ge(sem("moe_mul"), j + 1 + i * FE_TILES)
                            if j >= 2:
                                pe.wait_ge(sem("moe_alo"), j - 1 + i * FE_TILES)
                            for f in range(4):
                                ins = nc.tensor.transpose(PS[:, 6 + j % 2, f * P:(f + 1) * P],
                                                          he[:, j % 2, f * P:(f + 1) * P], ident)
                            ins.then_inc(sem("moe_tr"), 1)

                        pe.wait_ge(sem("moe_xlo"), 2 * i + 2)
                        pe.wait_ge(sem("moe_back"), i + 1)
                        for k in range(4 * FE_TILES):
                            j, w, kh = k // 4, k // 2 % 2, k % 2
                            if j >= 2 and kh == 0:
                                pe.wait_ge(sem("moe_silu" if w == 0 else "moe_mul"), j - 1 + i * FE_TILES)

                            def body(hi, lo):
                                for kk in range(4):
                                    dc = 4 * kh + kk
                                    ins = product(PS[:, 2 * w + j % 2, :], a_hi[:, dc, 0:P], a_lo[:, dc, 0:P],
                                                  hi[:, kk, :], lo[:, kk, :], dc == 0, dc == DC - 1)
                                return ins
                            echunk(k, 4, NT, body)
                            if k % 4 == 1 and k >= 5:
                                turn((k - 5) // 4)
                        pe.wait_ge(sem("moe_mul"), (i + 1) * FE_TILES)
                        turn(FE_TILES - 1)
                        for q in range(FFE // P // 2):
                            if q % 2 == 0:
                                pe.wait_ge(sem("moe_alo"), q // 2 + 1 + i * FE_TILES)

                            def body(hi, lo):
                                for kk in range(2):
                                    f = 2 * q + kk
                                    for half in range(2):
                                        cols = slice(half * NT, (half + 1) * NT)
                                        ins = product(PS[:, 2 + half, :], e_hi[:, f, :], e_lo[:, f, :],
                                                      hi[:, kk, cols], lo[:, kk, cols], f == 0, f == FFE // P - 1)
                                return ins
                            echunk(4 * FE_TILES + q, 2, D, body)
                        pe.wait_ge(sem("moe_ylo"), i + 1)
                        for s in range(4):
                            t, half = s // 2, s % 2
                            if s >= 2:
                                pe.wait_ge(sem("moe_add"), 4 * i + s - 1)
                            cols = slice(half * NT, (half + 1) * NT)
                            nc.tensor.matmul(PS[:, 4 + s % 2, :], backT[:, t * P:(t + 1) * P], y_hi[:, cols], start=True, stop=False)
                            nc.tensor.matmul(PS[:, 4 + s % 2, :], backT[:, t * P:(t + 1) * P], y_lo[:, cols], start=False, stop=True)\
                                .then_inc(sem("moe_sc"), 1)
                        pe.wait_ge(sem("moe_add"), 4 * i + 4)
                    with pe.Else():
                        pe.drain()
                        pe.sem_inc(mm_done, EXPERT_CHUNKS)
                        pe.sem_inc(sem("moe_gath"), 2)
                        pe.sem_inc(sem("moe_turn"), 1)
                        pe.sem_inc(sem("moe_tr"), FE_TILES)
                        pe.sem_inc(sem("moe_sc"), 4)


_INS = ['x', 'rel_bias', 'mix_norm_e', 'w_in_e', 'moba_q_norm', 'moba_k_norm', 'dsa_q_norm', 'dsa_k_norm',
        'w_out_e', 'ffn_norm_e', 'w_gate_e', 'w_up_e', 'w_down_e', 'mix_norm_o', 'w_in_o', 'q_a_norm', 'kv_a_norm',
        'w_uq', 'w_ukv', 'mla_q_norm', 'mla_k_norm', 'w_out_o', 'ffn_norm_o', 'w_router', 'b_router',
        'w_gate_o', 'w_up_o', 'w_down_o']


def shape_constants():
    import math
    import numpy as np
    c = np.zeros((P, K_ALL), np.float32)
    c[:, K_ID:K_ID + P] = np.eye(P)
    c[:, K_IOTA:K_IOTA + P] = np.arange(P)[None]
    c[:, K_TRI:K_TRI + P] = np.arange(P)[:, None] < np.arange(P)[None]
    c[:, K_ONES:K_ONES + P] = 1
    t, s = np.arange(P)[:, None], np.arange(S)[None]
    c[:, K_MASK:K_MASK + P] = np.where(s[:, :P] <= t, 0, MASKED)
    c[:, K_MASK + P:K_MASK + LOG] = np.where(s <= t + P, 0, MASKED)
    half = ROPE // 2
    freqs = np.float32(10000.0) ** (-np.arange(half, dtype=np.float32) / np.float32(half))
    ang = np.arange(S, dtype=np.float32)[:, None] * freqs
    for at, f in ((K_COS, np.cos), (K_SIN, np.sin)):
        tab = f(ang).reshape(TT, P, 1, half).repeat(GH, 2)
        c[:, at:at + P] = tab.transpose(1, 0, 2, 3).reshape(P, TT * GH * half)
    c[:, K_LOW:K_LOW + NE * NE] = (np.arange(NE)[None] < np.arange(NE)[:, None]).reshape(1, -1)
    n = np.arange(LOG) - (P - 1)
    exact = BUCKETS // 2
    nf = np.maximum(n, 1).astype(np.float32)
    large = exact + (np.log(nf / np.float32(exact)) / np.float32(math.log(1024 / exact)) * np.float32(BUCKETS - exact)).astype(np.int32)
    bucket = np.where(n < exact, np.maximum(n, 0), np.minimum(large, BUCKETS - 1))
    b = np.zeros((BUCKETS + 1, LOG), np.float32)
    b[bucket, np.arange(LOG)] = 1
    b[BUCKETS] = np.where(n < 0, MASKED, 0)
    return c, b


def kernel(**inputs):
    import numpy as _np
    import concourse.bacc as _bacc
    from concourse import mybir as _mybir
    from concourse.bass_utils import run_bass_kernel_spmd as _run

    nc = _bacc.Bacc("TRN2", target_bir_lowering=False, num_devices=1)
    arrays, args = {}, []
    consts, buckets = shape_constants()
    given = [(name, inputs[name]) for name in _INS] + [("consts", consts), ("buckets", buckets)]
    for name, value in given:
        a = _np.ascontiguousarray(value)
        arrays[f"in_{name}_dram"] = a
        args.append(nc.dram_tensor(f"in_{name}_dram", a.shape, _mybir.dt.from_np(a.dtype), kind="ExternalInput").ap())
    args.append(nc.dram_tensor("out_0_dram", (1, S, D), _mybir.dt.float32, kind="ExternalOutput").ap())
    hybrid_trunk(nc, *args)
    r = _run(nc, [arrays], core_ids=[0])
    return r.results[0]["out_0_dram"]
```

```python
import concourse.bass as bass
from concourse import mybir
from contextlib import ExitStack

P = 128
S = 256
TT = S // P
D = 1024
DC = D // P
HD = 64
NH = 16
IDXH = 4
BUCKETS = 32
FFD = 2816
QR, KVR, ROPE = 384, 256, 32
QKD = 96
NE = 8
FFE = 3584
DSA_KEEP = 64
EPS = 1e-6
MASKED = -1e30
TAKEN = -3e38

K_ID, K_IOTA, K_TRI, K_ONES = 0, 128, 256, 384
K_MASK = 512
K_COS, K_SIN = 896, 928
K_LOW = 960
K_ALL = 1024
LOG = 384

RAW = 7
STG = 3
CW = 2048
NT = 512

G_MIX_E, G_FFN_E, G_MIX_O, G_FFN_O, G_QA, G_KVA, G_HEAD, G_MLA, G_ROWS = 0, 8, 16, 24, 32, 35, 37, 41, 43

IDXW = IDXH * HD + HD + IDXH
FF_TILES = -(-FFD // NT)
FE_TILES = FFE // NT
EXPERT_CHUNKS = 4 * FE_TILES + FFE // P // 2
GATHER_AT = 4 * FE_TILES + 3
GROUPS = 4
GH = NH // GROUPS


def hybrid_trunk(nc, x, rel_bias, mix_norm_e, w_in_e, moba_q_norm, moba_k_norm, dsa_q_norm,
                 dsa_k_norm, w_out_e, ffn_norm_e, w_gate_e, w_up_e, w_down_e, mix_norm_o, w_in_o,
                 q_a_norm, kv_a_norm, w_uq, w_ukv, mla_q_norm, mla_k_norm, w_out_o, ffn_norm_o,
                 w_router, b_router, w_gate_o, w_up_o, w_down_o, consts, buckets, out):
    f32, f32r, i32 = mybir.dt.float32, mybir.dt.float32r, mybir.dt.int32
    ALU, ACT, AX = mybir.AluOpType, mybir.ActivationFunctionType, mybir.AxisListType

    def rows(w, r0, k, c0, n):
        return w[0][r0:r0 + k * P, c0:c0 + n].rearrange("(k p) n -> p k n", p=P)

    chunks = []

    def plan(aps):
        first = len(chunks)
        chunks.extend(aps)
        return first

    IN_TILES = [(6 * NT, IDXW)] + [(n * NT, NT) for n in range(6)]
    IN_TURN = [0, 1, 2, None, 3, 4, None]
    C_IN = plan([rows(w_in_e, kh * 512, 4, c, n) for c, n in IN_TILES for kh in range(2)])
    C_OUTE = plan([rows(w_out_e, kh * 512, 4, n * NT, NT) for n in range(2) for kh in range(2)])
    FF_W = [min(NT, FFD - j * NT) for j in range(FF_TILES)]
    C_FF = plan([rows(w, kh * 512, 4, j * NT, FF_W[j]) for j in range(FF_TILES)
                 for w in (w_gate_e, w_up_e) for kh in range(2)])
    C_FD = plan([rows(w_down_e, q * 256, 2, 0, D) for q in range(FFD // 256)])
    LAT = [(0, QR), (QR, KVR + ROPE)]
    C_LAT = plan([rows(w_in_o, kh * 512, 4, c, n) for c, n in LAT for kh in range(2)])
    C_HEADS = plan([a for g in range(GROUPS) for a in
                    (rows(w_uq, 0, 3, g * GH * QKD, GH * QKD), rows(w_ukv, 0, 2, g * GH * P, GH * P))])
    C_OUTO = plan([rows(w_out_o, kh * 512, 4, n * NT, NT) for n in range(2) for kh in range(2)])
    C_ROUTE = plan([rows(w_router, 0, DC, 0, NE)])
    C_MOE = len(chunks)

    with ExitStack() as ctx:
        sems = {}

        def sem(name):
            if name not in sems:
                sems[name] = ctx.enter_context(nc.semaphore(name))
            return sems[name]

        def sb(name, shape, dt=f32):
            return ctx.enter_context(nc.sbuf_tensor(name, shape, dt))

        raw = sb("raw", [P, RAW, CW])
        w_hi = sb("w_hi", [P, STG, CW], f32r)
        w_lo = sb("w_lo", [P, STG, CW], f32r)
        X = sb("X", [P, TT, D])
        a_hi = sb("a_hi", [P, DC, S], f32r)
        a_lo = sb("a_lo", [P, DC, S], f32r)
        cst = sb("cst", [P, K_ALL])
        gain = sb("gain", [P, G_ROWS + 5])
        gate_bias = sb("gate_bias", [P, NE])
        st = sb("st", [P, 96])
        nm = sb("nm", [P, 2 * NH, 2])
        top8 = sb("top8", [P, 16])
        rs = sb("rs", [P, 2 * NH, 4])
        pos = sb("pos", [P, TT, 2 * NE])
        comb = sb("comb", [P, TT, NE])
        need = sb("need", [1, NE], i32)
        ident = cst[:, K_ID:K_ID + P]
        iota = cst[:, K_IOTA:K_IOTA + P]
        mask = cst[:, K_MASK:K_MASK + LOG]

        arena_words = 18976
        arena = sb("arena", [P, arena_words])
        base = nc.sbuf_base - 4 * arena_words

        def place(at, name, shape, dt=f32):
            n = 1
            for v in shape[1:]:
                n *= v
            assert at + n <= arena_words, (name, at + n)
            return nc.alloc_sbuf_tensor_at(name, shape, dt, offset=base + 4 * at), at + n

        xn, z = place(0, "xn", [P, TT, D])
        v0, _ = place(0, "v0", [P, TT, NH * HD])
        qT0, z = place(z, "qT0", [P, 8, S])
        kT0, z = place(z, "kT0", [P, 8, S])
        brev, z = place(z, "brev", [P, NH, S])
        sq, z = place(z, "sq", [P, TT, NT])
        qn, z1 = place(z, "qn", [P, 2, TT, NT])
        lg, z2 = place(z, "lg", [P, 4, LOG])
        pT, _ = place(z2, "pT", [P, 2, LOG])
        z = max(z1, z2 + 2 * LOG)
        idxn, z1 = place(z, "idxn", [P, TT, 384])
        iqT, z1 = place(z1, "iqT", [P, 2, S])
        ikT, z1 = place(z1, "ikT", [P, S])
        relu, z1 = place(z1, "relu", [P, 2, LOG])
        score, z1 = place(z1, "score", [P, LOG])
        dmask, z1 = place(z1, "dmask", [P, LOG])
        brow, z1 = place(z1, "brow", [16, LOG])
        bias_in, z1 = place(z1, "bias_in", [BUCKETS + 1, LOG + 16])
        grow, _ = place(z - 512, "grow", [G_ROWS, P])
        z0 = TT * D
        act_hi, z = place(z0, "act_hi", [P, FFD // P, S], f32r)
        act_lo, z = place(z, "act_lo", [P, FFD // P, S], f32r)
        sg, z = place(z, "sg", [P, TT, NT])
        hn, z = place(z, "hn", [P, 2, TT, NT])
        v1, _ = place(0, "v1", [P, TT, NH * 64])
        latn, z = place(z0, "latn", [P, TT, QR + KVR])
        rot, _ = place(z0, "rot", [P, 2, TT * GH * ROPE])
        lat_hi, z = place(z, "lat_hi", [P, 5, S], f32r)
        lg1, z1 = place(z0, "lg1", [P, 4, LOG])
        pT1, z1 = place(z1, "pT1", [P, 2, LOG])
        assert z1 <= z
        lat_lo, z = place(z, "lat_lo", [P, 5, S], f32r)
        kpe, z = place(z, "kpe", [P, TT, ROPE])
        qkT, z = place(z, "qkT", [P, NH, 2 * S])
        kpj, _ = place(z, "kpj", [P, TT * ROPE])
        qk, z = place(z, "qk", [P, 2, 2 * TT * GH, QKD])
        sq1, z = place(z, "sq1", [P, TT * (QR + KVR)])
        gbc, z = place(z, "gbc", [P, 2, ROPE])
        rtab, z = place(z, "rtab", [P, 2, 2, TT, ROPE])
        h_hi, z = place(z0, "h_hi", [P, TT, D], f32r)
        h_lo, z = place(z, "h_lo", [P, TT, D], f32r)
        zr = z
        ffg, _ = place(zr, "ffg", [P, D])
        rt, _ = place(zr + D, "rt", [P, 10, TT * NE * NE])
        e_hi, z = place(zr, "e_hi", [P, FFE // P, P], f32r)
        e_lo, z = place(z, "e_lo", [P, FFE // P, P], f32r)
        sge, z = place(z, "sge", [P, 2, NT])
        he, z = place(z, "he", [P, 2, NT])
        y_hi, z = place(z, "y_hi", [P, D], f32r)
        y_lo, z = place(0, "y_lo", [P, D], f32r)
        pick, z = place(z, "pick", [P, TT, P], f32r)
        pickg, z = place(z, "pickg", [P, TT, P])
        backT, z = place(z, "backT", [P, S], f32r)

        PS = ctx.enter_context(nc.psum_tensor("PS", [P, 8, NT], f32))
        bias_dram = nc.dram_tensor("bias_scratch", [16, LOG], f32)

        raw_full = [sem(f"raw_full{i}") for i in range(RAW)]
        hi_done, lo_done, mm_done = sem("hi_done"), sem("lo_done"), sem("mm_done")

        FB = [2 * (w // 256) // 2 for w in FF_W]
        FB0 = [sum(FB[:j]) for j in range(FF_TILES + 1)]
        N_SMALL = 6 + 4 + 2

        block = ctx.enter_context(nc.Block())

        @block.sync
        def _(sp):
            sp.dma_start(X[:, :, :], x[0].rearrange("(t p) d -> p t d", p=P)).then_inc(sem("x_in"), 16)
            sp.dma_start(cst[:, :], consts).then_inc(sem("x_in"), 16)

            sp.wait_ge(sem("small_in"), 16 * N_SMALL)
            for c, src in enumerate(chunks):
                if c >= RAW:
                    sp.wait_ge(lo_done, c - RAW + 1)
                k, n = src.shape[1], src.shape[2]
                sp.dma_start(raw[:, c % RAW, 0:k * n].rearrange("p (k n) -> p k n", k=k), src)\
                    .then_inc(raw_full[c % RAW], 16)
            sp.wait_ge(sem("need_set"), 1)

            def expert_weights(i, e):
                for k in range(EXPERT_CHUNKS):
                    slot = (C_MOE + k) % RAW
                    sp.wait_ge(lo_done, C_MOE + k - RAW + 1 + i * EXPERT_CHUNKS)
                    if k < 4 * FE_TILES:
                        w = (w_gate_o, w_up_o)[k // 2 % 2]
                        src = w[0][bass.ds(e, 1), (k % 2) * 512:(k % 2) * 512 + 512, (k // 4) * NT:(k // 4 + 1) * NT]
                    else:
                        q = k - 4 * FE_TILES
                        src = w_down_o[0][bass.ds(e, 1), q * 256:(q + 1) * 256, :]
                    src = src.rearrange("a (k p) n -> p (a k) n", p=P)
                    sp.dma_start(raw[:, slot, :].rearrange("p (k n) -> p k n", k=src.shape[1]), src)\
                        .then_inc(raw_full[slot], 16)

            with sp.Fori(0, NE) as e:
                expert_weights(e, e)
            sp.wait_ge(sem("need_set"), 1)
            with sp.Fori(0, NE) as e:
                tokens = sp.value_load(need[0:1, bass.ds(e, 1)], min_val=-S, max_val=S)
                with sp.If(tokens > 0):
                    expert_weights(e + NE, e)
                with sp.Else():
                    sp.wait_ge(lo_done, C_MOE + (e + NE) * EXPERT_CHUNKS)
                    for slot in range(RAW):
                        sp.sem_inc(raw_full[slot], 16 * EXPERT_CHUNKS // RAW)
            sp.wait_ge(sem("moe_add"), 4 * (2 * NE + 1))
            sp.dma_start(out[0].rearrange("(t p) d -> p t d", p=P), X[:, :, :]).then_inc(sem("stored"), 16)
            sp.wait_ge(sem("stored"), 16)

        @block.scalar
        def _(act):
            for r0, src in ((G_MIX_E, mix_norm_e), (G_FFN_E, ffn_norm_e), (G_MIX_O, mix_norm_o),
                            (G_FFN_O, ffn_norm_o), (G_QA, q_a_norm), (G_KVA, kv_a_norm)):
                n = src.shape[1] // P
                act.dma_start(grow[r0:r0 + n, :], src[0].rearrange("(r p) -> r p", p=P)).then_inc(sem("small_in"), 16)
            for m, src in enumerate((moba_q_norm, moba_k_norm, dsa_q_norm, dsa_k_norm)):
                act.dma_start(grow[G_HEAD + m:G_HEAD + m + 1, :].rearrange("r (a n) -> r a n", a=2),
                              src.unsqueeze(1).to_broadcast([1, 2, HD])).then_inc(sem("small_in"), 16)
            act.dma_start(bias_in[:, 0:LOG], buckets).then_inc(sem("small_in"), 16)
            act.dma_start(bias_in[0:BUCKETS, LOG:LOG + 16], rel_bias).then_inc(sem("small_in"), 16)

            nsplit = [0]

            def split(c):
                assert nsplit[0] == c
                nsplit[0] += 1
                act.wait_ge(raw_full[c % RAW], 16 * (c // RAW + 1))
                if c >= STG:
                    act.wait_ge(mm_done, c - STG + 1)
                n = chunks[c].shape[1] * chunks[c].shape[2]
                nc.scalar.activation(w_hi[:, c % STG, 0:n], raw[:, c % RAW, 0:n], ACT.Copy).then_inc(hi_done, 1)

            def split_to(c):
                while nsplit[0] < c:
                    split(nsplit[0])

            def norm(q):
                act.wait_ge(sem("x_in"), 32) if q == 0 else act.wait_ge(sem("resid"), q)
                for t in range(TT):
                    nc.scalar.activation(xn[:, t, :], X[:, t, :], ACT.Square,
                                         accum_out=st[:, 2 * q + t:2 * q + t + 1]).then_inc(sem("norm_ss"), 1)
                act.wait_ge(sem("norm_ms"), q + 1)
                nc.scalar.activation(st[:, 16 + 2 * q:18 + 2 * q], st[:, 8 + 2 * q:10 + 2 * q], ACT.Sqrt)\
                    .then_inc(sem("norm_rt"), 1)
                if q == 3:
                    act.wait_ge(sem("hn_set"), 2)
                    for t in range(TT):
                        nc.scalar.activation(h_hi[:, t, :], xn[:, t, :], ACT.Copy).then_inc(sem("hnat_hi"), 1)
                for c in range(4):
                    act.wait_ge(sem("norm_t"), 4 * q + c + 1)
                    if q == 3:
                        nc.scalar.activation(a_hi[:, 2 * c:2 * c + 2, :],
                                             PS[:, 4 + c, :].rearrange("p (d t) -> p d t", d=2), ACT.Copy)\
                            .then_inc(sem("norm_hi"), 2)
                        continue
                    for d in range(2):
                        dc = 2 * c + d
                        nc.scalar.activation(a_hi[:, dc, :], PS[:, 4 + c, d * S:(d + 1) * S], ACT.Copy,
                                             scale=gain[:, 8 * q + dc:8 * q + dc + 1]).then_inc(sem("norm_hi"), 1)

            def heads(h0, n, logits, probs_t):
                for s in range(n + 4):
                    if 3 <= s <= n + 2:
                        h = h0 + s - 3
                        act.wait_ge(sem("at_tr"), h + 1)
                        if h >= 2:
                            act.wait_ge(sem("at_pv"), h - 1)
                        nc.scalar.activation(probs_t[:, h % 2, :], PS[:, 6 + h % 2, 0:LOG], ACT.Copy)\
                            .then_inc(sem("at_pt"), 1)
                    if s < n:
                        h = h0 + s
                        act.wait_ge(sem("at_max"), h + 1)
                        nc.scalar.activation(logits[:, h % 4, 0:P], logits[:, h % 4, 0:P], ACT.Exp,
                                             bias=nm[:, h, 0:1], accum_out=rs[:, h, 0:1]).then_inc(sem("at_exp"), 1)
                        nc.scalar.activation(logits[:, h % 4, P:LOG], logits[:, h % 4, P:LOG], ACT.Exp,
                                             bias=nm[:, h, 1:2], accum_out=rs[:, h, 1:2]).then_inc(sem("at_exp"), 1)
                    if s >= 4 and (h0 + s - 4) % 2:
                        h = h0 + s - 4
                        act.wait_ge(sem("at_pv"), h + 1)
                        nc.scalar.activation(a_hi[:, h // 2 % 8, :], PS[:, h // 2 % 2, 0:S], ACT.Copy)\
                            .then_inc(sem("at_ohi"), 1)

            split_to(STG)
            act.wait_ge(sem("gain_set"), 1)
            norm(0)
            def qk_evac(m):
                for half in range(2):
                    act.wait_ge(sem("qk_tr"), 2 * m + half + 1)
                    bank = 4 + 2 * (m % 2) + half
                    src = PS[:, bank, :].rearrange("p (d t) -> p d t", d=2)
                    if m == 0:
                        if half == 0:
                            ins = nc.scalar.activation(iqT[:, :, :], src, ACT.Copy)
                        else:
                            ins = nc.scalar.activation(ikT[:, :], PS[:, bank, 0:S], ACT.Copy)
                    else:
                        pair, is_k = (m - 1) // 2, (m - 1) % 2
                        dst = (qT0, kT0)[is_k][:, 4 * pair + 2 * half:4 * pair + 2 * half + 2, :]
                        g = G_HEAD + m - 1 if is_k else G_ROWS + m - 1
                        ins = nc.scalar.activation(dst, src, ACT.Copy, scale=gain[:, g:g + 1])
                    ins.then_inc(sem("qk_evac"), 1)

            for n in range(7):
                split_to(min(C_IN + 2 * n + 4, C_OUTE + 1))
                m = IN_TURN[n]
                if m:
                    act.wait_ge(mm_done, C_IN + 2 * n + 2)
                    if m >= 2:
                        act.wait_ge(sem("sq_read"), m - 1)
                    nc.scalar.activation(sq[:, :, :], PS[:, 2 * (n % 2):2 * (n % 2) + 2, :], ACT.Square)\
                        .then_inc(sem("sq_set"), 1)
                    act.wait_ge(sem("qk_ms"), m)
                    nc.scalar.activation(st[:, 64:80], st[:, 48:64], ACT.Sqrt).then_inc(sem("qk_rt"), 1)
                if n >= 1 and IN_TURN[n - 1] is not None:
                    qk_evac(IN_TURN[n - 1])
                if n == 2:
                    for h in range(IDXH):
                        act.wait_ge(sem("idx_mm"), h + 1)
                        if h >= 2:
                            act.wait_ge(sem("idx_acc"), 2 * (h - 1))
                        nc.scalar.activation(relu[:, h % 2, :], PS[:, 4 + h % 2, 0:LOG], ACT.Relu).then_inc(sem("idx_relu"), 1)
            split_to(C_OUTE + STG)
            heads(0, NH, lg, pT)
            split_to(C_FF)
            split_to(C_FF + STG)
            norm(1)

            def ff_evac(j):
                for k in range(FB0[j], FB0[j + 1]):
                    act.wait_ge(sem("ff_tr"), k + 1)
                    nc.scalar.activation(act_hi[:, 2 * k:2 * k + 2, :],
                                         PS[:, 4 + k % 4, :].rearrange("p (d t) -> p d t", d=2), ACT.Copy)\
                        .then_inc(sem("ff_hi"), 1)

            for k in range(4 * FF_TILES + 4):
                split_to(max(nsplit[0], C_FF + k + 1))
                if k % 4 == 3 and k // 4 < FF_TILES:
                    j = k // 4
                    w = FF_W[j]
                    act.wait_ge(mm_done, C_FF + 4 * j + 2)
                    if j >= 1:
                        act.wait_ge(sem("up_read"), j)
                    nc.scalar.activation(sg[:, :, 0:w], PS[:, 0:2, 0:w], ACT.Silu).then_inc(sem("gate_read"), 1)
                if k % 4 == 3 and k >= 7:
                    ff_evac((k - 7) // 4)
            split_to(C_LAT + STG)

            norm(2)
            split_to(C_LAT + 4)
            act.wait_ge(mm_done, C_LAT + 4)
            split_to(C_HEADS + 3)
            for t in range(TT):
                for col, bank, c0, n, junk in (
                        (24, 0, 0, QR, sq1[:, t * QR:(t + 1) * QR]),
                        (26, 2, 0, KVR, sq1[:, TT * QR + t * KVR:TT * QR + (t + 1) * KVR]),
                        (28, 2, KVR, ROPE, kpj[:, t * ROPE:(t + 1) * ROPE])):
                    nc.scalar.activation(junk, PS[:, bank + t, c0:c0 + n], ACT.Square,
                                         accum_out=st[:, col + t:col + t + 1]).then_inc(sem("lat_ss"), 1)
            act.wait_ge(sem("lat_ms"), 1)
            nc.scalar.activation(st[:, 34:38], st[:, 30:34], ACT.Sqrt).then_inc(sem("lat_rt"), 1)
            for d in range(5):
                bank, off = ((4, 0), (4, S), (5, 0), (6, 0), (6, S))[d]
                act.wait_ge(sem("lat_tr"), bank - 3)
                nc.scalar.activation(lat_hi[:, d, :], PS[:, bank, off:off + S], ACT.Copy,
                                     scale=gain[:, G_QA + d:G_QA + d + 1]).then_inc(sem("lat_hi"), 1)
            def group_evac(g):
                for h in range(GH * g, GH * g + GH):
                    act.wait_ge(sem("grp_tr"), h + 1)
                    for s, col in enumerate((G_ROWS + 4, G_MLA + 1)):
                        nc.scalar.activation(qkT[0:QKD, h, s * S:(s + 1) * S], PS[0:QKD, 6 + h % 2, s * S:(s + 1) * S],
                                             ACT.Copy, scale=gain[0:QKD, col:col + 1]).then_inc(sem("grp_ev"), 1)

            for g in range(GROUPS):
                qb, kb = 2 * (2 * g % 3), 2 * ((2 * g + 1) % 3)
                kv = PS[:, kb:kb + 2, :].rearrange("p t (h n) -> p t h n", h=GH)
                act.wait_ge(mm_done, C_HEADS + 2 * g + 1)
                if g >= 1:
                    act.wait_ge(sem("grp_sqread"), 2 * g)
                nc.scalar.activation(sq1[:, 0:TT * QR].rearrange("p (t n) -> p t n", t=TT),
                                     PS[:, qb:qb + 2, 0:GH * QKD], ACT.Square).then_inc(sem("grp_sq"), 1)
                act.wait_ge(mm_done, C_HEADS + 2 * g + 2)
                nc.scalar.activation(sq1[:, TT * QR:TT * QR + TT * GH * 64].rearrange("p (t h n) -> p t h n", t=TT, h=GH),
                                     kv[:, :, :, 0:64], ACT.Square).then_inc(sem("grp_sq"), 1)
                nc.scalar.activation(v1[:, :, g * GH * 64:(g + 1) * GH * 64].rearrange("p t (h n) -> p t h n", h=GH),
                                     kv[:, :, :, 64:128], ACT.Copy).then_inc(sem("v_read"), 1)
                act.wait_ge(sem("grp_ms"), g + 1)
                nc.scalar.activation(st[:, 64:80], st[:, 48:64], ACT.Sqrt).then_inc(sem("grp_rt"), 1)
                split_to(C_HEADS + 2 * g + 5)
                if g >= 1:
                    group_evac(g - 1)
            group_evac(GROUPS - 1)
            heads(NH, NH, lg1, pT1)
            split_to(C_MOE)
            norm(3)
            act.wait_ge(sem("top_sub"), 1)
            nc.scalar.activation(rt[:, 4, 0:TT * NE], rt[:, 3, 0:TT * NE], ACT.Exp).then_inc(sem("top_exp"), 1)

            def esplit(i, k):
                c = C_MOE + k
                act.wait_ge(raw_full[c % RAW], 16 * (c // RAW + 1) + i * (16 * EXPERT_CHUNKS // RAW))
                act.wait_ge(mm_done, c - STG + 1 + i * EXPERT_CHUNKS)
                nc.scalar.activation(w_hi[:, c % STG, :], raw[:, c % RAW, :], ACT.Copy).then_inc(hi_done, 1)

            def gathered(i):
                for h in range(2):
                    act.wait_ge(sem("moe_gath"), 2 * i + h + 1)
                    nc.scalar.activation(a_hi[:, 4 * h:4 * h + 4, 0:P],
                                         PS[:, 4 + h, :].rearrange("p (d t) -> p d t", d=4), ACT.Copy)\
                        .then_inc(sem("moe_xhi"), 1)

            def result(i):
                act.wait_ge(mm_done, C_MOE + (i + 1) * EXPERT_CHUNKS)
                nc.scalar.activation(y_hi[:, :].rearrange("p (a n) -> p a n", a=2), PS[:, 2:4, :], ACT.Copy,
                                     scale=st[:, 90:91]).then_inc(sem("moe_yhi"), 1)

            def expert(i, follow):
                for k in range(STG, EXPERT_CHUNKS + STG * follow):
                    esplit(i, k)
                    if k % 4 == 3 and k // 4 < FE_TILES:
                        j = k // 4
                        act.wait_ge(mm_done, C_MOE + 4 * j + 2 + i * EXPERT_CHUNKS)
                        if j >= 2:
                            act.wait_ge(sem("moe_mul"), j - 1 + i * FE_TILES)
                        nc.scalar.activation(sge[:, j % 2, :], PS[:, j % 2, :], ACT.Silu).then_inc(sem("moe_silu"), 1)
                    if k % 4 == 3 and 7 <= k < 7 + 4 * FE_TILES:
                        j = (k - 7) // 4
                        act.wait_ge(sem("moe_tr"), j + 1 + i * FE_TILES)
                        nc.scalar.activation(e_hi[:, 4 * j:4 * j + 4, :],
                                             PS[:, 6 + j % 2, :].rearrange("p (d t) -> p d t", d=4), ACT.Copy)\
                            .then_inc(sem("moe_ahi"), 1)
                    if follow and k == GATHER_AT + 2:
                        gathered(i + 1)
                    if follow and k == EXPERT_CHUNKS + 1:
                        result(i)
                if not follow:
                    result(i)

            for k in range(STG):
                esplit(0, k)
            gathered(0)
            with act.Fori(0, NE - 1) as e:
                expert(e, True)
            expert(NE - 1, False)
            act.wait_ge(sem("need_set"), 1)
            with act.Fori(0, NE) as e:
                i = e + NE
                tokens = act.value_load(need[0:1, bass.ds(e, 1)], min_val=-S, max_val=S)
                with act.If(tokens > 0):
                    for k in range(STG):
                        esplit(i, k)
                    gathered(i)
                    expert(i, False)
                with act.Else():
                    act.drain()
                    act.sem_inc(hi_done, EXPERT_CHUNKS)
                    act.sem_inc(sem("moe_xhi"), 2)
                    act.sem_inc(sem("moe_silu"), FE_TILES)
                    act.sem_inc(sem("moe_ahi"), FE_TILES)
                    act.sem_inc(sem("moe_yhi"), 1)

        @block.vector
        def _(dve):
            steps = [0]

            def step(ins):
                steps[0] += 1
                ins.then_inc(sem("dve_step"), 1)
                dve.wait_ge(sem("dve_step"), steps[0])

            nsplit = [0]

            def split(c):
                assert nsplit[0] == c
                nsplit[0] += 1
                n = chunks[c].shape[1] * chunks[c].shape[2]
                dve.wait_ge(hi_done, c + 1)
                nc.vector.tensor_tensor(w_lo[:, c % STG, 0:n], raw[:, c % RAW, 0:n], w_hi[:, c % STG, 0:n],
                                        ALU.subtract).then_inc(lo_done, 1)

            def split_to(c):
                while nsplit[0] < c:
                    split(nsplit[0])

            def norm(q):
                dve.wait_ge(sem("norm_ss"), 2 * q + 2)
                nc.vector.tensor_scalar(st[:, 8 + 2 * q:10 + 2 * q], st[:, 2 * q:2 * q + 2], 1.0 / D, EPS,
                                        ALU.mult, ALU.add).then_inc(sem("norm_ms"), 1)
                dve.wait_ge(sem("norm_rt"), q + 1)
                step(nc.vector.reciprocal(st[:, 24 - 24 + 40:42], st[:, 16 + 2 * q:18 + 2 * q]))
                for t in range(TT):
                    ins = nc.vector.tensor_scalar(xn[:, t, :], X[:, t, :], st[:, 40 + t:41 + t], None, ALU.mult)
                    if q == 3:
                        step(ins)
                        ins = nc.vector.tensor_tensor(xn[:, t, :], xn[:, t, :], ffg[:, :], ALU.mult)
                        ins.then_inc(sem("hn_set"), 1)
                    else:
                        ins.then_inc(sem("norm_xn"), 1)
                if q == 3:
                    for t in range(TT):
                        dve.wait_ge(sem("hnat_hi"), t + 1)
                        nc.vector.tensor_tensor(h_lo[:, t, :], xn[:, t, :], h_hi[:, t, :], ALU.subtract)\
                            .then_inc(sem("hnat_lo"), 1)
                for c in range(4):
                    dve.wait_ge(sem("norm_hi"), 8 * q + 2 * c + 2)
                    if q == 3:
                        nc.vector.tensor_tensor(a_lo[:, 2 * c:2 * c + 2, :],
                                                PS[:, 4 + c, :].rearrange("p (d t) -> p d t", d=2),
                                                a_hi[:, 2 * c:2 * c + 2, :], ALU.subtract).then_inc(sem("norm_lo"), 2)
                        continue
                    for d in range(2):
                        dc = 2 * c + d
                        nc.vector.scalar_tensor_tensor(out=a_lo[:, dc, :], in0=PS[:, 4 + c, d * S:(d + 1) * S],
                                                       scalar=gain[:, 8 * q + dc:8 * q + dc + 1],
                                                       in1=a_hi[:, dc, :].bitcast(f32), op0=ALU.mult,
                                                       op1=ALU.subtract).then_inc(sem("norm_lo"), 1)

            def heads(h0, n, logits, bias):
                for s in range(n + 5):
                    if s < n:
                        h = h0 + s
                        dve.wait_ge(sem("at_qk"), h + 1)
                        if h >= 4:
                            dve.wait_ge(sem("at_tr"), h - 3)
                        bank = PS[:, 4 + h % 2, :]
                        if bias:
                            nc.vector.tensor_tensor(logits[:, h % 4, 0:P], bank[:, 0:P], brev[:, h, 0:P][:, ::-1], ALU.add)
                            nc.vector.tensor_tensor(logits[:, h % 4, P:LOG], bank[:, P:LOG], brev[:, h, :][:, ::-1],
                                                    ALU.add).then_inc(sem("at_add"), 1)
                            dve.wait_ge(sem("at_add"), h + 1)
                            if h >= 8:
                                step(nc.vector.tensor_tensor(logits[:, h % 4, :], logits[:, h % 4, :], dmask[:, :], ALU.add))
                        else:
                            nc.vector.tensor_tensor(logits[:, h % 4, :], bank[:, 0:LOG], mask, ALU.add)\
                                .then_inc(sem("at_add"), 1)
                            dve.wait_ge(sem("at_add"), h + 1)
                        nc.vector.tensor_reduce(nm[:, h, 0:1], logits[:, h % 4, 0:P], AX.X, ALU.max, negate=True)
                        nc.vector.tensor_reduce(nm[:, h, 1:2], logits[:, h % 4, P:LOG], AX.X, ALU.max, negate=True)\
                            .then_inc(sem("at_max"), 1)
                    if 1 <= s <= n:
                        h = h0 + s - 1
                        dve.wait_ge(sem("at_exp"), 2 * h + 2)
                        nc.vector.reciprocal(rs[:, h, 2:4], rs[:, h, 0:2]).then_inc(sem("at_rcp"), 1)
                    if s >= 5 and (h0 + s - 5) % 2:
                        h = h0 + s - 5
                        dve.wait_ge(sem("at_ohi"), h // 2 + 1)
                        nc.vector.tensor_tensor(a_lo[:, h // 2 % 8, :], PS[:, h // 2 % 2, 0:S], a_hi[:, h // 2 % 8, :],
                                                ALU.subtract).then_inc(sem("at_olo"), 1)

            nc.vector.memset(bias_in[BUCKETS:BUCKETS + 1, LOG:LOG + 16], 1.0).then_inc(sem("ones_set"), 1)
            dve.wait_ge(sem("set_tr"), 2)
            nc.vector.tensor_copy(brow[:, :], PS[0:16, 1, 0:LOG]).then_inc(sem("brow_set"), 1)
            nc.vector.tensor_copy(gain[:, 0:G_ROWS], PS[:, 0, 0:G_ROWS]).then_inc(sem("gain_copy"), 1)
            dve.wait_ge(sem("gain_copy"), 1)
            nc.vector.tensor_scalar(gain[:, G_ROWS:G_ROWS + 4], gain[:, G_HEAD:G_HEAD + 4], HD ** -0.5, None, ALU.mult)\
                .then_inc(sem("gain_set"), 1)
            dve.wait_ge(sem("gain_set"), 1)
            step(nc.vector.memset(gain[64:P, G_MLA:G_MLA + 2], 1.0))
            step(nc.vector.tensor_scalar(gain[:, G_ROWS + 4:G_ROWS + 5], gain[:, G_MLA:G_MLA + 1], QKD ** -0.5, None, ALU.mult))
            split_to(STG)
            norm(0)
            def top_rounds(r0, r1):
                for r in range(r0, r1):
                    nc.vector.max(top8[:, 0:8], score[:, 0:P])
                    step(nc.vector.max(top8[:, 8:16], score[:, P:LOG]))
                    nc.vector.match_replace(score[:, 0:P], top8[:, 0:8], score[:, 0:P], TAKEN)
                    step(nc.vector.match_replace(score[:, P:LOG], top8[:, 8:16], score[:, P:LOG], TAKEN))

            for n in range(7):
                split_to(min(C_IN + 2 * n + 4, C_OUTE + 1))
                dve.wait_ge(mm_done, C_IN + 2 * n + 2)
                pair = PS[:, 2 * (n % 2):2 * (n % 2) + 2, :]
                m = IN_TURN[n]
                if m:
                    dve.wait_ge(sem("sq_set"), m)
                    nc.vector.tensor_reduce(st[:, 80:96], sq[:, :, :].rearrange("p t (h d) -> p (t h) d", d=HD), AX.X, ALU.add)\
                        .then_inc(sem("sq_read"), 1)
                    dve.wait_ge(sem("sq_read"), m)
                    nc.vector.tensor_scalar(st[:, 48:64], st[:, 80:96], 1.0 / HD, EPS, ALU.mult, ALU.add)\
                        .then_inc(sem("qk_ms"), 1)
                    dve.wait_ge(sem("qk_rt"), m)
                    step(nc.vector.reciprocal(st[:, 48:64], st[:, 64:80]))
                    if m >= 3:
                        dve.wait_ge(sem("qk_tr"), 2 * (m - 1))
                    nc.vector.tensor_tensor(qn[:, m % 2, :, :].rearrange("p t (h d) -> p t h d", d=HD),
                                            pair.rearrange("p t (h d) -> p t h d", d=HD),
                                            st[:, 48:64].rearrange("p (t h) -> p t h", t=TT).unsqueeze(3).to_broadcast([P, TT, 8, HD]),
                                            ALU.mult).then_inc(sem("tile_read"), 1)
                elif n:
                    if n == 3:
                        dve.wait_ge(sem("norm_t"), 4)
                    nc.vector.tensor_copy(v0[:, :, (n // 6) * NT:(n // 6 + 1) * NT], pair).then_inc(sem("tile_read"), 1)
                else:
                    nc.vector.tensor_copy(idxn[:, :, 0:320], pair[:, :, 0:320])
                    nc.vector.tensor_copy(idxn[:, :, 320:384], pair[:, :, 256:320])
                    nc.vector.tensor_scalar(st[:, 16:24].rearrange("p (t h) -> p t h", t=TT), pair[:, :, 320:324],
                                            HD ** -0.5 * IDXH ** -0.5, None, ALU.mult).then_inc(sem("tile_read"), 1)
                if n == 2:
                    for h in range(IDXH):
                        dve.wait_ge(sem("idx_relu"), h + 1)
                        for t, (a, b) in enumerate(((0, P), (P, LOG))):
                            if h:
                                dve.wait_ge(sem("idx_acc"), 2 * h - 1 + t)
                            nc.vector.scalar_tensor_tensor(out=score[:, a:b], in0=relu[:, h % 2, a:b],
                                                           scalar=st[:, 16 + 4 * t + h:17 + 4 * t + h],
                                                           in1=(score[:, a:b] if h else cst[:, K_MASK + a:K_MASK + b]),
                                                           op0=ALU.mult, op1=ALU.add).then_inc(sem("idx_acc"), 1)
                    dve.wait_ge(sem("idx_acc"), 2 * IDXH)
                if 3 <= n <= 6:
                    top_rounds(2 * (n - 3), 2 * (n - 2))
            step(nc.vector.tensor_scalar(dmask[:, :], score[:, :], TAKEN / 2, MASKED, ALU.is_gt, ALU.mult))
            split_to(C_OUTE + STG)
            dve.wait_ge(sem("bias_in"), 16)
            heads(0, NH, lg, True)

            def residual(c_last, bank, n, k):
                dve.wait_ge(mm_done, c_last + 1)
                ins = nc.vector.tensor_tensor(X[:, :, n * NT:(n + 1) * NT], X[:, :, n * NT:(n + 1) * NT],
                                              PS[:, bank:bank + 2, :], ALU.add)
                ins.then_inc(sem("resid"), 1) if n == 1 else None

            split_to(C_OUTE + 4)
            residual(C_OUTE + 1, 0, 0, 0)
            residual(C_OUTE + 3, 2, 1, 0)
            split_to(C_FF + STG)
            norm(1)

            def ff_evac(j):
                for k in range(FB0[j], FB0[j + 1]):
                    dve.wait_ge(sem("ff_hi"), k + 1)
                    nc.vector.tensor_tensor(act_lo[:, 2 * k:2 * k + 2, :],
                                            PS[:, 4 + k % 4, :].rearrange("p (d t) -> p d t", d=2),
                                            act_hi[:, 2 * k:2 * k + 2, :], ALU.subtract).then_inc(sem("ff_lo"), 1)

            for k in range(4 * FF_TILES + 4):
                split_to(max(nsplit[0], C_FF + k + 1))
                if k % 4 == 1 and k >= 5:
                    j = (k - 5) // 4
                    w = FF_W[j]
                    dve.wait_ge(sem("gate_read"), j + 1)
                    dve.wait_ge(mm_done, C_FF + 4 * j + 4)
                    if j >= 2:
                        dve.wait_ge(sem("ff_tr"), FB0[j - 1])
                    nc.vector.tensor_tensor(hn[:, j % 2, :, 0:w], PS[:, 2:4, 0:w], sg[:, :, 0:w], ALU.mult)\
                        .then_inc(sem("up_read"), 1)
                if k % 4 == 3 and k >= 7:
                    ff_evac((k - 7) // 4)
            split_to(C_LAT)
            dve.wait_ge(mm_done, C_LAT)
            nc.vector.tensor_tensor(X[:, :, :].rearrange("p t (a n) -> p (t a) n", a=2),
                                    X[:, :, :].rearrange("p t (a n) -> p (t a) n", a=2),
                                    PS[:, 0:4, :], ALU.add).then_inc(sem("resid"), 1)
            split_to(C_LAT + STG)
            norm(2)
            split_to(C_HEADS + 3)
            dve.wait_ge(sem("lat_ss"), 6)
            nc.vector.tensor_scalar(st[:, 30:32], st[:, 24:26], 1.0 / QR, EPS, ALU.mult, ALU.add)
            nc.vector.tensor_scalar(st[:, 32:34], st[:, 26:28], 1.0 / KVR, EPS, ALU.mult, ALU.add)\
                .then_inc(sem("lat_ms"), 1)
            dve.wait_ge(sem("lat_rt"), 1)
            step(nc.vector.reciprocal(st[:, 44:48], st[:, 34:38]))
            for t in range(TT):
                nc.vector.tensor_scalar(latn[:, t, 0:QR], PS[:, t, 0:QR], st[:, 44 + t:45 + t], None, ALU.mult)
                nc.vector.tensor_copy(kpe[:, t, :], PS[:, 2 + t, KVR:KVR + ROPE])
                nc.vector.tensor_scalar(latn[:, t, QR:QR + KVR], PS[:, 2 + t, 0:KVR], st[:, 46 + t:47 + t], None, ALU.mult)\
                    .then_inc(sem("lat_n"), 1)
            for d in range(5):
                bank, off = ((4, 0), (4, S), (5, 0), (6, 0), (6, S))[d]
                dve.wait_ge(sem("lat_hi"), (2, 2, 3, 5, 5)[d])
                nc.vector.scalar_tensor_tensor(out=lat_lo[:, d, :], in0=PS[:, bank, off:off + S],
                                               scalar=gain[:, G_QA + d:G_QA + d + 1],
                                               in1=lat_hi[:, d, :].bitcast(f32), op0=ALU.mult, op1=ALU.subtract)\
                    .then_inc(sem("lat_lo"), 1)
            dve.wait_ge(sem("gbc_in"), 32)
            for b, at in enumerate((K_COS, K_SIN)):
                for s in range(2):
                    tab = cst[:, at:at + TT * 16].rearrange("p (t n) -> p t n", t=TT)
                    ins = nc.vector.tensor_tensor(rtab[:, s, b, :, :].rearrange("p t (a n) -> p t a n", a=2),
                                                  gbc[:, s, :].rearrange("p (a n) -> p a n", a=2).unsqueeze(1).to_broadcast([P, TT, 2, 16]),
                                                  tab.unsqueeze(2).to_broadcast([P, TT, 2, 16]), ALU.mult)
            step(ins)
            rk2 = [rot[:, b, 0:TT * ROPE].rearrange("p (t n) -> p t n", t=TT) for b in range(2)]
            nc.vector.tensor_tensor(rk2[0], kpe[:, :, :], rtab[:, 1, 0, :, :], ALU.mult)
            step(nc.vector.tensor_tensor(rk2[1], kpe[:, :, :], rtab[:, 1, 1, :, :], ALU.mult))
            nc.vector.tensor_tensor(kpe[:, :, 0:16], rk2[0][:, :, 0:16], rk2[1][:, :, 16:32], ALU.subtract)
            step(nc.vector.tensor_tensor(kpe[:, :, 16:32], rk2[0][:, :, 16:32], rk2[1][:, :, 0:16], ALU.add))
            TH = TT * GH
            for g in range(GROUPS):
                qb, kb = 2 * (2 * g % 3), 2 * ((2 * g + 1) % 3)
                dve.wait_ge(sem("grp_sq"), 2 * g + 1)
                nc.vector.tensor_reduce(st[:, 80:80 + TH], sq1[:, 0:TT * QR].rearrange("p (a n) -> p a n", n=QKD),
                                        AX.X, ALU.add).then_inc(sem("grp_sqread"), 1)
                dve.wait_ge(sem("grp_sq"), 2 * g + 2)
                nc.vector.tensor_reduce(st[:, 80 + TH:96],
                                        sq1[:, TT * QR:TT * QR + TH * 64].rearrange("p (a n) -> p a n", n=64),
                                        AX.X, ALU.add).then_inc(sem("grp_sqread"), 1)
                dve.wait_ge(sem("grp_sqread"), 2 * g + 2)
                for t in range(TT):
                    ins = nc.vector.tensor_scalar(st[:, 80 + TH + GH * t:80 + TH + GH * t + GH],
                                                  st[:, 80 + TH + GH * t:80 + TH + GH * t + GH],
                                                  st[:, 28 + t:29 + t], None, ALU.add)
                step(ins)
                nc.vector.tensor_scalar(st[:, 48:64], st[:, 80:96], 1.0 / QKD, EPS, ALU.mult, ALU.add)\
                    .then_inc(sem("grp_ms"), 1)
                dve.wait_ge(sem("grp_rt"), g + 1)
                step(nc.vector.reciprocal(st[:, 48:64], st[:, 64:80]))
                if g >= 2:
                    dve.wait_ge(sem("grp_tr"), GH * (g - 1))
                rq = st[:, 48:48 + TH].rearrange("p (t h) -> p t h", t=TT)
                rk = st[:, 48 + TH:64].rearrange("p (t h) -> p t h", t=TT)
                q4 = qk[:, g % 2, 0:TH, :].rearrange("p (t h) n -> p t h n", t=TT)
                k4 = qk[:, g % 2, TH:2 * TH, :].rearrange("p (t h) n -> p t h n", t=TT)
                kv = PS[:, kb:kb + 2, :].rearrange("p t (h n) -> p t h n", h=GH)
                nc.vector.tensor_tensor(q4, PS[:, qb:qb + 2, 0:GH * QKD].rearrange("p t (h n) -> p t h n", h=GH),
                                        rq.unsqueeze(3).to_broadcast([P, TT, GH, QKD]), ALU.mult).then_inc(sem("item_read"), 1)
                nc.vector.tensor_tensor(k4[:, :, :, 0:64], kv[:, :, :, 0:64],
                                        rk.unsqueeze(3).to_broadcast([P, TT, GH, 64]), ALU.mult).then_inc(sem("item_read"), 1)
                nc.vector.tensor_tensor(k4[:, :, :, 64:96], kpe[:, :, :].unsqueeze(2).to_broadcast([P, TT, GH, ROPE]),
                                        rk.unsqueeze(3).to_broadcast([P, TT, GH, ROPE]), ALU.mult)
                split_to(C_HEADS + 2 * g + 4)
                dve.wait_ge(sem("item_read"), 2 * g + 1)
                xq = q4[:, :, :, 64:96]
                r2 = [rot[:, b, :].rearrange("p (t h n) -> p t h n", t=TT, h=GH) for b in range(2)]
                for b in range(2):
                    ins = nc.vector.tensor_tensor(r2[b], xq, rtab[:, 0, b, :, :].unsqueeze(2).to_broadcast([P, TT, GH, ROPE]),
                                                  ALU.mult)
                step(ins)
                nc.vector.tensor_tensor(xq[:, :, :, 0:16], r2[0][:, :, :, 0:16], r2[1][:, :, :, 16:32], ALU.subtract)
                nc.vector.tensor_tensor(xq[:, :, :, 16:32], r2[0][:, :, :, 16:32], r2[1][:, :, :, 0:16], ALU.add)\
                    .then_inc(sem("grp_qk"), 1)
                split_to(C_HEADS + 2 * g + 5)
            heads(NH, NH, lg1, False)
            split_to(C_OUTO + 4)
            residual(C_OUTO + 1, 0, 0, 0)
            residual(C_OUTO + 3, 2, 1, 0)
            split_to(C_MOE)
            dve.wait_ge(sem("ffg_in"), 16)
            norm(3)

            dve.wait_ge(sem("bias8_in"), 16)
            dve.wait_ge(mm_done, C_ROUTE + 1)
            R = lambda k: rt[:, k, 0:TT * NE].rearrange("p (t e) -> p t e", t=TT)
            F = lambda k: rt[:, k, :].rearrange("p (t e f) -> p t e f", t=TT, e=NE)
            wide = [P, TT, NE, NE]
            step(nc.vector.tensor_tensor(R(0), PS[:, 0:2, 0:NE],
                                         gate_bias[:, :].unsqueeze(1).to_broadcast([P, TT, NE]), ALU.add))
            other, own = R(0).unsqueeze(2).to_broadcast(wide), R(0).unsqueeze(3).to_broadcast(wide)
            low = cst[:, K_LOW:K_LOW + NE * NE].rearrange("p (e f) -> p e f", e=NE).unsqueeze(1).to_broadcast(wide)
            nc.vector.tensor_tensor(F(1), other, own, ALU.is_gt)
            nc.vector.tensor_reduce(st[:, 40:42], R(0), AX.X, ALU.max)
            step(nc.vector.tensor_tensor(F(2), other, own, ALU.is_equal))
            nc.vector.tensor_tensor(R(3), R(0), st[:, 40:42].unsqueeze(2).to_broadcast([P, TT, NE]), ALU.subtract)\
                .then_inc(sem("top_sub"), 1)
            step(nc.vector.tensor_tensor(F(2), F(2), low, ALU.mult))
            step(nc.vector.tensor_tensor(F(1), F(1), F(2), ALU.add))
            step(nc.vector.tensor_reduce(R(5), F(1), AX.X, ALU.add))
            nc.vector.tensor_scalar(R(6), R(5), 1.5, None, ALU.is_lt).then_inc(sem("sel_set"), 1)
            dve.wait_ge(sem("sel_set"), 1)
            dve.wait_ge(sem("top_exp"), 1)
            step(nc.vector.tensor_tensor(R(4), R(4), R(6), ALU.mult))
            step(nc.vector.tensor_reduce(st[:, 42:44], R(4), AX.X, ALU.add))
            step(nc.vector.reciprocal(st[:, 40:42], st[:, 42:44]))
            step(nc.vector.tensor_tensor(comb[:, :, :], R(4), st[:, 40:42].unsqueeze(2).to_broadcast([P, TT, NE]), ALU.mult))
            FAR = 1000.0
            dve.wait_ge(sem("place_mm"), 1)
            step(nc.vector.tensor_scalar(R(7), PS[:, 4:6, 0:NE], FAR, None, ALU.add))
            step(nc.vector.tensor_tensor(R(7), R(7), R(6), ALU.mult))
            for b in range(2):
                nc.vector.tensor_scalar(pos[:, :, b * NE:(b + 1) * NE], R(7), -FAR - b * P, None, ALU.add)
            nc.vector.memset(y_hi[:, :].bitcast(f32), 0.0)
            nc.vector.memset(y_lo[:, :].bitcast(f32), 0.0).then_inc(sem("moe_ylo"), 1)
            nc.vector.memset(backT[:, :].bitcast(f32), 0.0)
            nc.vector.tensor_scalar(need[:, :], PS[0:1, 6, 0:NE], -float(P), None, ALU.add).then_inc(sem("need_set"), 1)
            dve.wait_ge(sem("need_set"), 1)

            def esplit(i, k):
                c = C_MOE + k
                dve.wait_ge(hi_done, c + 1 + i * EXPERT_CHUNKS)
                nc.vector.tensor_tensor(w_lo[:, c % STG, :], raw[:, c % RAW, :], w_hi[:, c % STG, :],
                                        ALU.subtract).then_inc(lo_done, 1)

            def picks(i, e):
                for t in range(TT):
                    nc.vector.tensor_scalar(pick[:, t, :], iota, pos[:, t, bass.ds(i, 1)], None, ALU.is_equal)
                    ins = nc.vector.tensor_scalar(pickg[:, t, :], iota, pos[:, t, bass.ds(i, 1)],
                                                  comb[:, t, bass.ds(e, 1)], ALU.is_equal, ALU.mult)
                ins.then_inc(sem("moe_pick"), 1)

            def gathered(i):
                for h in range(2):
                    dve.wait_ge(sem("moe_xhi"), 2 * i + h + 1)
                    nc.vector.tensor_tensor(a_lo[:, 4 * h:4 * h + 4, 0:P],
                                            PS[:, 4 + h, :].rearrange("p (d t) -> p d t", d=4),
                                            a_hi[:, 4 * h:4 * h + 4, 0:P], ALU.subtract).then_inc(sem("moe_xlo"), 1)

            def result(i):
                dve.wait_ge(sem("moe_yhi"), i + 1)
                nc.vector.scalar_tensor_tensor(out=y_lo[:, :].rearrange("p (a n) -> p a n", a=2), in0=PS[:, 2:4, :],
                                               scalar=st[:, 90:91],
                                               in1=y_hi[:, :].bitcast(f32).rearrange("p (a n) -> p a n", a=2),
                                               op0=ALU.mult, op1=ALU.subtract).then_inc(sem("moe_ylo"), 1)

            def add_back(n):
                for s in range(4):
                    t, h = s // 2, s % 2
                    dve.wait_ge(sem("moe_sc"), 4 * n + s + 1)
                    nc.vector.tensor_tensor(X[:, t, h * NT:(h + 1) * NT], X[:, t, h * NT:(h + 1) * NT],
                                            PS[:, 4 + s % 2, :], ALU.add).then_inc(sem("moe_add"), 1)

            def expert(i, follow, alone=False):
                for k in range(STG, EXPERT_CHUNKS + STG * follow):
                    esplit(i, k)
                    if k == 3:
                        if not alone:
                            add_back(i)
                        dve.wait_ge(sem("moe_turn"), i + 1)
                        nc.vector.tensor_reduce(st[:, 90:91], PS[:, 6, 0:S], AX.X, ALU.add)
                        nc.vector.tensor_scalar(backT[:, :], PS[:, 6, 0:S], 0.0, None, ALU.is_gt).then_inc(sem("moe_back"), 1)
                    if k % 4 == 1 and 5 <= k < 5 + 4 * FE_TILES:
                        j = (k - 5) // 4
                        dve.wait_ge(sem("moe_silu"), j + 1 + i * FE_TILES)
                        dve.wait_ge(mm_done, C_MOE + 4 * j + 4 + i * EXPERT_CHUNKS)
                        if j >= 2:
                            dve.wait_ge(sem("moe_tr"), j - 1 + i * FE_TILES)
                        nc.vector.tensor_tensor(he[:, j % 2, :], PS[:, 2 + j % 2, :], sge[:, j % 2, :], ALU.mult)\
                            .then_inc(sem("moe_mul"), 1)
                    if k % 4 == 3 and 7 <= k < 7 + 4 * FE_TILES:
                        j = (k - 7) // 4
                        dve.wait_ge(sem("moe_ahi"), j + 1 + i * FE_TILES)
                        nc.vector.tensor_tensor(e_lo[:, 4 * j:4 * j + 4, :],
                                                PS[:, 6 + j % 2, :].rearrange("p (d t) -> p d t", d=4),
                                                e_hi[:, 4 * j:4 * j + 4, :], ALU.subtract).then_inc(sem("moe_alo"), 1)
                    if follow and k == GATHER_AT - 6:
                        picks(i + 1, i + 1)
                    if follow and k == GATHER_AT + 3:
                        gathered(i + 1)
                    if follow and k == EXPERT_CHUNKS + 1:
                        result(i)
                if not follow:
                    result(i)
                if alone:
                    add_back(i + 1)

            picks(0, 0)
            for k in range(STG):
                esplit(0, k)
            gathered(0)
            with dve.Fori(0, NE - 1) as e:
                expert(e, True)
            expert(NE - 1, False)
            add_back(NE)
            with dve.Fori(0, NE) as e:
                i = e + NE
                tokens = dve.value_load(need[0:1, bass.ds(e, 1)], min_val=-S, max_val=S)
                with dve.If(tokens > 0):
                    picks(i, e)
                    for k in range(STG):
                        esplit(i, k)
                    gathered(i)
                    expert(i, False, True)
                with dve.Else():
                    dve.drain()
                    dve.sem_inc(lo_done, EXPERT_CHUNKS)
                    dve.sem_inc(sem("moe_pick"), 1)
                    dve.sem_inc(sem("moe_xlo"), 2)
                    dve.sem_inc(sem("moe_back"), 1)
                    dve.sem_inc(sem("moe_mul"), FE_TILES)
                    dve.sem_inc(sem("moe_alo"), FE_TILES)
                    dve.sem_inc(sem("moe_ylo"), 1)
                    dve.sem_inc(sem("moe_add"), 4)

        @block.gpsimd
        def _(pool):
            def heads(h0, n, logits):
                for h in range(h0, h0 + n):
                    pool.wait_ge(sem("at_rcp"), h + 1)
                    nc.gpsimd.tensor_scalar(logits[:, h % 4, 0:P], logits[:, h % 4, 0:P], rs[:, h, 2:3], None, ALU.mult)
                    nc.gpsimd.tensor_scalar(logits[:, h % 4, P:LOG], logits[:, h % 4, P:LOG], rs[:, h, 3:4], None,
                                            ALU.mult).then_inc(sem("at_norm"), 1)

            for m, src in enumerate((mla_q_norm, mla_k_norm)):
                pool.dma_start(grow[G_MLA + m:G_MLA + m + 1, :].rearrange("r (a n) -> r a n", a=2),
                               src[:, 0:64].unsqueeze(1).to_broadcast([1, 2, 64])).then_inc(sem("mla_in"), 16)
            pool.wait_ge(sem("brow_set"), 1)
            pool.dma_start(bias_dram[:, :], brow[:, :]).then_inc(sem("bias_out"), 16)
            pool.wait_ge(sem("bias_out"), 16)
            with nc.allow_non_contiguous_dma(reason="a window of the table for each partition"):
                pool.dma_start(brev[:, :, :], bass.AP(bias_dram, 0, [[1, P], [LOG, NH], [1, S]]))\
                    .then_inc(sem("bias_in"), 16)
            pool.dma_start(gate_bias[:, :], b_router.to_broadcast([P, NE])).then_inc(sem("bias8_in"), 16)
            heads(0, NH, lg)
            pool.wait_ge(sem("resid"), 2)
            pool.dma_start(gbc[:, 0, :], mla_q_norm[:, 64:QKD].to_broadcast([P, ROPE])).then_inc(sem("gbc_in"), 16)
            pool.dma_start(gbc[:, 1, :], mla_k_norm[:, 64:QKD].to_broadcast([P, ROPE])).then_inc(sem("gbc_in"), 16)
            heads(NH, NH, lg1)
            pool.wait_ge(sem("resid"), 3)
            pool.dma_start(ffg[:, :], ffn_norm_o.to_broadcast([P, D])).then_inc(sem("ffg_in"), 16)

        @block.tensor
        def _(pe):
            def product(dst, xh, xl, wh, wl, first, last):
                nc.tensor.matmul(dst, xh, wh, start=first, stop=False)
                nc.tensor.matmul(dst, xh, wl, start=False, stop=False)
                return nc.tensor.matmul(dst, xl, wh, start=False, stop=last)

            def chunk(c, kn, n, body):
                pe.wait_ge(lo_done, c + 1)
                hi = w_hi[:, c % STG, 0:kn * n].rearrange("p (k n) -> p k n", k=kn)
                lo = w_lo[:, c % STG, 0:kn * n].rearrange("p (k n) -> p k n", k=kn)
                body(hi, lo).then_inc(mm_done, 1)

            def project(c0, nchunks, kn, n, bank, xh=a_hi, xl=a_lo, x0=0):
                for q in range(nchunks):
                    def body(hi, lo):
                        for t in range(TT):
                            for k in range(kn):
                                kk = x0 + q * kn + k
                                ins = product(PS[:, bank + t, 0:n], xh[:, kk, t * P:(t + 1) * P], xl[:, kk, t * P:(t + 1) * P],
                                              hi[:, k, :], lo[:, k, :], q == 0 and k == 0, q == nchunks - 1 and k == kn - 1)
                        return ins
                    chunk(c0 + q, kn, n, body)

            def norm(q):
                pe.wait_ge(sem("norm_xn"), 2 * q + 2) if q < 3 else pe.wait_ge(sem("hn_set"), 2)
                for c in range(4):
                    for d in range(2):
                        for t in range(TT):
                            dc = 2 * c + d
                            ins = nc.tensor.transpose(PS[:, 4 + c, d * S + t * P:d * S + (t + 1) * P],
                                                      xn[:, t, dc * P:(dc + 1) * P], ident)
                    ins.then_inc(sem("norm_t"), 1)
                pe.wait_ge(sem("norm_lo"), 8 * (q + 1))

            def heads(h0, n, q_of, k_of, v_of, probs_t):
                for s in range(n + 4):
                    if s < n:
                        h = h0 + s
                        if h >= 2:
                            pe.wait_ge(sem("at_add"), h - 1)
                        bank = PS[:, 4 + h % 2, :]
                        nc.tensor.matmul(bank[:, 0:P], q_of(h, 0), k_of(h)[:, 0:P], start=True, stop=True)
                        nc.tensor.matmul(bank[:, P:LOG], q_of(h, 1), k_of(h), start=True, stop=True).then_inc(sem("at_qk"), 1)
                    if 3 <= s <= n + 2:
                        h = h0 + s - 3
                        pe.wait_ge(sem("at_norm"), h + 1)
                        if h >= 2:
                            pe.wait_ge(sem("at_pt"), h - 1)
                        lgb = (lg if h < NH else lg1)
                        for k in range(3):
                            ins = nc.tensor.transpose(PS[:, 6 + h % 2, k * P:(k + 1) * P], lgb[:, h % 4, k * P:(k + 1) * P], ident)
                        ins.then_inc(sem("at_tr"), 1)
                    if s >= 4:
                        h = h0 + s - 4
                        pe.wait_ge(sem("at_pt"), h + 1)
                        if h >= 4 and h % 2 == 0:
                            pe.wait_ge(sem("at_olo"), h // 2 - 1)
                        dst = PS[64 * (h % 2):64 * (h % 2) + 64, h // 2 % 2, 0:S]
                        nc.tensor.matmul(dst, v_of(h, 0), probs_t[:, h % 2, 0:S], start=True, stop=False)
                        nc.tensor.matmul(dst[:, P:S], v_of(h, 1), probs_t[:, h % 2, S:LOG], start=False, stop=True)\
                            .then_inc(sem("at_pv"), 1)

            pe.wait_ge(sem("x_in"), 32)
            pe.wait_ge(sem("small_in"), 16 * N_SMALL)
            pe.wait_ge(sem("mla_in"), 32)
            pe.wait_ge(sem("ones_set"), 1)
            nc.tensor.transpose(PS[:, 0, 0:G_ROWS], grow[:, :], cst[0:G_ROWS, K_ID:K_ID + G_ROWS]).then_inc(sem("set_tr"), 1)
            nc.tensor.matmul(PS[0:16, 1, 0:LOG], bias_in[:, LOG:LOG + 16], bias_in[:, 0:LOG], start=True, stop=True)\
                .then_inc(sem("set_tr"), 1)
            norm(0)
            def turn_heads(m):
                if m == 2:
                    pe.wait_ge(sem("idx_relu"), IDXH)
                if m >= 2:
                    pe.wait_ge(sem("qk_evac"), 2 * (m - 1))
                for half in range(2):
                    bank = 4 + 2 * (m % 2) + half
                    for d in range(2 if (m or half == 0) else 1):
                        for t in range(TT):
                            f = (2 * half + d) * P
                            src = qn[:, m % 2, t, f:f + P] if m else idxn[:, t, f:f + P]
                            ins = nc.tensor.transpose(PS[:, bank, d * S + t * P:d * S + (t + 1) * P], src, ident)
                    ins.then_inc(sem("qk_tr"), 1)

            def turn_after(n):
                if IN_TURN[n] is not None:
                    pe.wait_ge(sem("tile_read"), n + 1)
                    turn_heads(IN_TURN[n])

            for n in range(7):
                if n >= 2:
                    pe.wait_ge(sem("tile_read"), n - 1)
                elif n == 0:
                    pe.wait_ge(sem("brow_set"), 1)
                    pe.wait_ge(sem("gain_copy"), 1)
                project(C_IN + 2 * n, 2, 4, IN_TILES[n][1], 2 * (n % 2))
                if n >= 1:
                    turn_after(n - 1)
                if n == 2:
                    pe.wait_ge(sem("qk_evac"), 2)
                    for h in range(IDXH):
                        r = HD * (h % 2)
                        if h >= 2:
                            pe.wait_ge(sem("idx_relu"), h - 1)
                        nc.tensor.matmul(PS[:, 4 + h % 2, 0:P], iqT[r:r + HD, h // 2, 0:P], ikT[r:r + HD, 0:P], start=True, stop=True)
                        nc.tensor.matmul(PS[:, 4 + h % 2, P:LOG], iqT[r:r + HD, h // 2, P:S], ikT[r:r + HD, :], start=True, stop=True)\
                            .then_inc(sem("idx_mm"), 1)
            pe.wait_ge(sem("tile_read"), 7)
            pe.wait_ge(sem("qk_evac"), 10)

            def r0(h):
                return HD * (h % 2)
            heads(0, NH, lambda h, t: qT0[r0(h):r0(h) + HD, h // 2, t * P:(t + 1) * P],
                  lambda h: kT0[r0(h):r0(h) + HD, h // 2, :],
                  lambda h, t: v0[:, t, h * HD:(h + 1) * HD], pT)
            pe.wait_ge(sem("at_olo"), NH // 2)
            for n in range(2):
                project(C_OUTE + 2 * n, 2, 4, NT, 2 * n)
            norm(1)

            def turn_ff(j):
                pe.wait_ge(sem("up_read"), j + 1)
                for k in range(FB0[j], FB0[j + 1]):
                    if k >= 4:
                        pe.wait_ge(sem("ff_lo"), k - 3)
                    for d in range(2):
                        for t in range(TT):
                            f = (2 * (k - FB0[j]) + d) * P
                            ins = nc.tensor.transpose(PS[:, 4 + k % 4, d * S + t * P:d * S + (t + 1) * P],
                                                      hn[:, j % 2, t, f:f + P], ident)
                    ins.then_inc(sem("ff_tr"), 1)

            for j in range(FF_TILES):
                if j:
                    pe.wait_ge(sem("gate_read"), j)
                project(C_FF + 4 * j, 2, 4, FF_W[j], 0)
                if j:
                    turn_ff(j - 1)
                project(C_FF + 4 * j + 2, 2, 4, FF_W[j], 2)
            pe.wait_ge(sem("gate_read"), FF_TILES)
            pe.wait_ge(sem("up_read"), FF_TILES)
            for q in range(FFD // 256):
                pe.wait_ge(sem("ff_lo"), q + 1)

                def body(hi, lo):
                    for t in range(TT):
                        for k in range(2):
                            f = 2 * q + k
                            xs = [a[:, f, t * P:(t + 1) * P] for a in (act_hi, act_lo)]
                            for half in range(2):
                                cols = slice(half * NT, (half + 1) * NT)
                                ins = product(PS[:, 2 * t + half, :], *xs, hi[:, k, cols], lo[:, k, cols],
                                              f == 0, f == FFD // P - 1)
                    return ins
                chunk(C_FD + q, 2, D, body)
                if q == 1:
                    turn_ff(FF_TILES - 1)
            norm(2)
            for n in range(2):
                project(C_LAT + 2 * n, 2, 4, LAT[n][1], 2 * n)
            pe.wait_ge(sem("lat_n"), 2)
            for d in range(5):
                bank, off = ((4, 0), (4, S), (5, 0), (6, 0), (6, S))[d]
                for t in range(TT):
                    ins = nc.tensor.transpose(PS[:, bank, off + t * P:off + (t + 1) * P], latn[:, t, d * P:(d + 1) * P], ident)
                if d in (1, 2, 4):
                    ins.then_inc(sem("lat_tr"), 1)
            pe.wait_ge(sem("lat_lo"), 5)

            def turn_group(g):
                pe.wait_ge(sem("grp_qk"), g + 1)
                for h in range(GH * g, GH * g + GH):
                    if h >= 2:
                        pe.wait_ge(sem("grp_ev"), 2 * (h - 1))
                    for s in range(2):
                        for t in range(TT):
                            ins = nc.tensor.transpose(PS[0:QKD, 6 + h % 2, s * S + t * P:s * S + (t + 1) * P],
                                                      qk[:, g % 2, (s * TT + t) * GH + h % GH, :], ident)
                    ins.then_inc(sem("grp_tr"), 1)

            for m in range(2 * GROUPS):
                if m >= 3:
                    pe.wait_ge(sem("item_read"), m - 2)
                    if m % 2 == 0:
                        pe.wait_ge(sem("v_read"), (m - 2) // 2)
                if m % 2 == 0:
                    project(C_HEADS + m, 1, 3, GH * QKD, 2 * (m % 3), lat_hi, lat_lo, 0)
                else:
                    project(C_HEADS + m, 1, 2, GH * P, 2 * (m % 3), lat_hi, lat_lo, 3)
                    if m >= 3:
                        turn_group((m - 3) // 2)
            turn_group(GROUPS - 1)
            pe.wait_ge(sem("item_read"), 2 * GROUPS)
            pe.wait_ge(sem("v_read"), GROUPS)
            pe.wait_ge(sem("grp_ev"), 2 * NH)
            heads(NH, NH, lambda h, t: qkT[0:QKD, h - NH, t * P:(t + 1) * P],
                  lambda h: qkT[0:QKD, h - NH, S:2 * S],
                  lambda h, t: v1[:, t, (h - NH) * 64:(h - NH + 1) * 64], pT1)
            pe.wait_ge(sem("at_olo"), NH)
            for n in range(2):
                project(C_OUTO + 2 * n, 2, 4, NT, 2 * n)
            norm(3)
            project(C_ROUTE, 1, DC, NE, 0)
            pe.wait_ge(sem("sel_set"), 1)
            tri, ones = cst[:, K_TRI:K_TRI + P], cst[:, K_ONES:K_ONES + P]
            sel = [rt[:, 6, t * NE:(t + 1) * NE] for t in range(TT)]
            nc.tensor.matmul(PS[:, 4, 0:NE], tri, sel[0], start=True, stop=True)
            nc.tensor.matmul(PS[:, 5, 0:NE], ones, sel[0], start=True, stop=False)
            nc.tensor.matmul(PS[:, 5, 0:NE], tri, sel[1], start=False, stop=True)
            nc.tensor.matmul(PS[:, 6, 0:NE], ones, sel[0], start=True, stop=False)
            nc.tensor.matmul(PS[:, 6, 0:NE], ones, sel[1], start=False, stop=True).then_inc(sem("place_mm"), 1)
            pe.wait_ge(sem("hnat_lo"), 2)
            pe.wait_ge(sem("need_set"), 1)

            def gather(i):
                pe.wait_ge(sem("moe_pick"), i + 1)
                for dc in range(DC):
                    for t in range(TT):
                        for h, part in enumerate((h_hi, h_lo)):
                            ins = nc.tensor.matmul(PS[:, 4 + dc // 4, (dc % 4) * P:(dc % 4 + 1) * P],
                                                   part[:, t, dc * P:(dc + 1) * P], pick[:, t, :],
                                                   start=(t == 0 and h == 0), stop=(t == 1 and h == 1))
                    if dc % 4 == 3:
                        ins.then_inc(sem("moe_gath"), 1)

            def turn_pick(i):
                for t in range(TT):
                    ins = nc.tensor.transpose(PS[:, 6, t * P:(t + 1) * P], pickg[:, t, :], ident)
                ins.then_inc(sem("moe_turn"), 1)
                pe.wait_ge(sem("moe_back"), i + 1)

            def bring_back(n):
                pe.wait_ge(sem("moe_ylo"), n + 1)
                for s in range(4):
                    t, half = s // 2, s % 2
                    if s >= 2:
                        pe.wait_ge(sem("moe_add"), 4 * n + s - 1)
                    cols = slice(half * NT, (half + 1) * NT)
                    nc.tensor.matmul(PS[:, 4 + s % 2, :], backT[:, t * P:(t + 1) * P], y_hi[:, cols], start=True, stop=False)
                    nc.tensor.matmul(PS[:, 4 + s % 2, :], backT[:, t * P:(t + 1) * P], y_lo[:, cols], start=False, stop=True)\
                        .then_inc(sem("moe_sc"), 1)

            def echunk(i, k, kn, n, body):
                c = C_MOE + k
                pe.wait_ge(lo_done, c + 1 + i * EXPERT_CHUNKS)
                hi = w_hi[:, c % STG, :].rearrange("p (k n) -> p k n", k=kn)
                lo = w_lo[:, c % STG, :].rearrange("p (k n) -> p k n", k=kn)
                body(hi, lo).then_inc(mm_done, 1)

            def turn(i, j):
                pe.wait_ge(sem("moe_mul"), j + 1 + i * FE_TILES)
                if j >= 2:
                    pe.wait_ge(sem("moe_alo"), j - 1 + i * FE_TILES)
                for f in range(4):
                    ins = nc.tensor.transpose(PS[:, 6 + j % 2, f * P:(f + 1) * P], he[:, j % 2, f * P:(f + 1) * P], ident)
                ins.then_inc(sem("moe_tr"), 1)

            def expert(i, follow, alone=False):
                pe.wait_ge(sem("moe_xlo"), 2 * i + 2)
                for k in range(4 * FE_TILES):
                    j, w, kh = k // 4, k // 2 % 2, k % 2
                    if k == 2:
                        if not alone:
                            bring_back(i)
                        turn_pick(i)
                    if j >= 2 and kh == 0:
                        pe.wait_ge(sem("moe_silu" if w == 0 else "moe_mul"), j - 1 + i * FE_TILES)

                    def body(hi, lo):
                        for kk in range(4):
                            dc = 4 * kh + kk
                            ins = product(PS[:, 2 * w + j % 2, :], a_hi[:, dc, 0:P], a_lo[:, dc, 0:P],
                                          hi[:, kk, :], lo[:, kk, :], dc == 0, dc == DC - 1)
                        return ins
                    echunk(i, k, 4, NT, body)
                    if k % 4 == 1 and k >= 5:
                        turn(i, (k - 5) // 4)
                for q in range(FFE // P // 2):
                    if q == 0:
                        pe.wait_ge(sem("moe_mul"), (i + 1) * FE_TILES)
                        turn(i, FE_TILES - 1)
                    if q % 2 == 0:
                        pe.wait_ge(sem("moe_alo"), q // 2 + 1 + i * FE_TILES)

                    def body(hi, lo):
                        for kk in range(2):
                            f = 2 * q + kk
                            for half in range(2):
                                cols = slice(half * NT, (half + 1) * NT)
                                ins = product(PS[:, 2 + half, :], e_hi[:, f, :], e_lo[:, f, :],
                                              hi[:, kk, cols], lo[:, kk, cols], f == 0, f == FFE // P - 1)
                        return ins
                    echunk(i, 4 * FE_TILES + q, 2, D, body)
                    if follow and 4 * FE_TILES + q == GATHER_AT:
                        pe.wait_ge(sem("moe_add"), 4 * i + 4)
                        gather(i + 1)
                if alone:
                    bring_back(i + 1)
                    pe.wait_ge(sem("moe_add"), 4 * i + 8)

            gather(0)
            with pe.Fori(0, NE - 1) as e:
                expert(e, True)
            expert(NE - 1, False)
            bring_back(NE)
            pe.wait_ge(sem("moe_add"), 4 * NE + 4)
            with pe.Fori(0, NE) as e:
                i = e + NE
                tokens = pe.value_load(need[0:1, bass.ds(e, 1)], min_val=-S, max_val=S)
                with pe.If(tokens > 0):
                    gather(i)
                    expert(i, False, True)
                with pe.Else():
                    pe.drain()
                    pe.sem_inc(mm_done, EXPERT_CHUNKS)
                    pe.sem_inc(sem("moe_gath"), 2)
                    pe.sem_inc(sem("moe_turn"), 1)
                    pe.sem_inc(sem("moe_tr"), FE_TILES)
                    pe.sem_inc(sem("moe_sc"), 4)


_INS = ['x', 'rel_bias', 'mix_norm_e', 'w_in_e', 'moba_q_norm', 'moba_k_norm', 'dsa_q_norm', 'dsa_k_norm',
        'w_out_e', 'ffn_norm_e', 'w_gate_e', 'w_up_e', 'w_down_e', 'mix_norm_o', 'w_in_o', 'q_a_norm', 'kv_a_norm',
        'w_uq', 'w_ukv', 'mla_q_norm', 'mla_k_norm', 'w_out_o', 'ffn_norm_o', 'w_router', 'b_router',
        'w_gate_o', 'w_up_o', 'w_down_o']


def shape_constants():
    import math
    import numpy as np
    c = np.zeros((P, K_ALL), np.float32)
    c[:, K_ID:K_ID + P] = np.eye(P)
    c[:, K_IOTA:K_IOTA + P] = np.arange(P)[None]
    c[:, K_TRI:K_TRI + P] = np.arange(P)[:, None] < np.arange(P)[None]
    c[:, K_ONES:K_ONES + P] = 1
    t, s = np.arange(P)[:, None], np.arange(S)[None]
    c[:, K_MASK:K_MASK + P] = np.where(s[:, :P] <= t, 0, MASKED)
    c[:, K_MASK + P:K_MASK + LOG] = np.where(s <= t + P, 0, MASKED)
    half = ROPE // 2
    freqs = np.float32(10000.0) ** (-np.arange(half, dtype=np.float32) / np.float32(half))
    ang = np.arange(S, dtype=np.float32)[:, None] * freqs
    for at, f in ((K_COS, np.cos), (K_SIN, np.sin)):
        c[:, at:at + TT * half] = f(ang).reshape(TT, P, half).transpose(1, 0, 2).reshape(P, TT * half)
    c[:, K_LOW:K_LOW + NE * NE] = (np.arange(NE)[None] < np.arange(NE)[:, None]).reshape(1, -1)
    n = np.arange(LOG) - (P - 1)
    exact = BUCKETS // 2
    nf = np.maximum(n, 1).astype(np.float32)
    large = exact + (np.log(nf / np.float32(exact)) / np.float32(math.log(1024 / exact)) * np.float32(BUCKETS - exact)).astype(np.int32)
    bucket = np.where(n < exact, np.maximum(n, 0), np.minimum(large, BUCKETS - 1))
    b = np.zeros((BUCKETS + 1, LOG), np.float32)
    b[bucket, np.arange(LOG)] = 1
    b[BUCKETS] = np.where(n < 0, MASKED, 0)
    return c, b


def kernel(**inputs):
    import numpy as _np
    import concourse.bacc as _bacc
    from concourse import mybir as _mybir
    from concourse.bass_utils import run_bass_kernel_spmd as _run

    nc = _bacc.Bacc("TRN2", target_bir_lowering=False, num_devices=1)
    arrays, args = {}, []
    consts, buckets = shape_constants()
    given = [(name, inputs[name]) for name in _INS] + [("consts", consts), ("buckets", buckets)]
    for name, value in given:
        a = _np.ascontiguousarray(value)
        arrays[f"in_{name}_dram"] = a
        args.append(nc.dram_tensor(f"in_{name}_dram", a.shape, _mybir.dt.from_np(a.dtype), kind="ExternalInput").ap())
    args.append(nc.dram_tensor("out_0_dram", (1, S, D), _mybir.dt.float32, kind="ExternalOutput").ap())
    hybrid_trunk(nc, *args)
    r = _run(nc, [arrays], core_ids=[0])
    return r.results[0]["out_0_dram"]
```

```python
import concourse.bass as bass
from concourse import mybir
from contextlib import ExitStack

P = 128
S = 256
TT = S // P
D = 1024
DC = D // P
HD = 64
NH = 16
IDXH = 4
BUCKETS = 32
FFD = 2816
QR, KVR, ROPE = 384, 256, 32
QKD = 96
NE = 8
FFE = 3584
DSA_KEEP = 64
EPS = 1e-6
MASKED = -1e30
TAKEN = -3e38

K_ID, K_IOTA, K_TRI, K_ONES = 0, 128, 256, 384
K_MASK = 512
K_COS, K_SIN = 896, 928
K_LOW = 960
K_ALL = 1024
LOG = 384

RAW = 7
STG = 3
CW = 2048
NT = 512

G_MIX_E, G_FFN_E, G_MIX_O, G_FFN_O, G_QA, G_KVA, G_HEAD, G_MLA, G_ROWS = 0, 8, 16, 24, 32, 35, 37, 41, 43

IDXW = IDXH * HD + HD + IDXH
FF_TILES = -(-FFD // NT)
FE_TILES = FFE // NT
EXPERT_CHUNKS = 4 * FE_TILES + FFE // P // 2
GATHER_AT = 4 * FE_TILES + 3
GROUPS = 4
GH = NH // GROUPS


def hybrid_trunk(nc, x, rel_bias, mix_norm_e, w_in_e, moba_q_norm, moba_k_norm, dsa_q_norm,
                 dsa_k_norm, w_out_e, ffn_norm_e, w_gate_e, w_up_e, w_down_e, mix_norm_o, w_in_o,
                 q_a_norm, kv_a_norm, w_uq, w_ukv, mla_q_norm, mla_k_norm, w_out_o, ffn_norm_o,
                 w_router, b_router, w_gate_o, w_up_o, w_down_o, consts, buckets, out):
    f32, f32r, i32 = mybir.dt.float32, mybir.dt.float32r, mybir.dt.int32
    ALU, ACT, AX = mybir.AluOpType, mybir.ActivationFunctionType, mybir.AxisListType

    def rows(w, r0, k, c0, n):
        return w[0][r0:r0 + k * P, c0:c0 + n].rearrange("(k p) n -> p k n", p=P)

    chunks = []

    def plan(aps):
        first = len(chunks)
        chunks.extend(aps)
        return first

    IN_TILES = [(6 * NT, IDXW)] + [(n * NT, NT) for n in range(6)]
    IN_TURN = [0, 1, 2, None, 3, 4, None]
    C_IN = plan([rows(w_in_e, kh * 512, 4, c, n) for c, n in IN_TILES for kh in range(2)])
    C_OUTE = plan([rows(w_out_e, kh * 512, 4, n * NT, NT) for n in range(2) for kh in range(2)])
    FF_W = [min(NT, FFD - j * NT) for j in range(FF_TILES)]
    C_FF = plan([rows(w, kh * 512, 4, j * NT, FF_W[j]) for j in range(FF_TILES)
                 for w in (w_gate_e, w_up_e) for kh in range(2)])
    C_FD = plan([rows(w_down_e, q * 256, 2, 0, D) for q in range(FFD // 256)])
    LAT = [(0, QR), (QR, KVR + ROPE)]
    C_LAT = plan([rows(w_in_o, kh * 512, 4, c, n) for c, n in LAT for kh in range(2)])
    C_HEADS = plan([a for g in range(GROUPS) for a in
                    (rows(w_uq, 0, 3, g * GH * QKD, GH * QKD), rows(w_ukv, 0, 2, g * GH * P, GH * P))])
    C_OUTO = plan([rows(w_out_o, kh * 512, 4, n * NT, NT) for n in range(2) for kh in range(2)])
    C_ROUTE = plan([rows(w_router, 0, DC, 0, NE)])
    C_MOE = len(chunks)

    with ExitStack() as ctx:
        sems = {}

        def sem(name):
            if name not in sems:
                sems[name] = ctx.enter_context(nc.semaphore(name))
            return sems[name]

        def sb(name, shape, dt=f32):
            return ctx.enter_context(nc.sbuf_tensor(name, shape, dt))

        raw = sb("raw", [P, RAW, CW])
        w_hi = sb("w_hi", [P, STG, CW], f32r)
        w_lo = sb("w_lo", [P, STG, CW], f32r)
        X = sb("X", [P, TT, D])
        a_hi = sb("a_hi", [P, DC, S], f32r)
        a_lo = sb("a_lo", [P, DC, S], f32r)
        cst = sb("cst", [P, K_ALL])
        gain = sb("gain", [P, G_ROWS + 5])
        gate_bias = sb("gate_bias", [P, NE])
        st = sb("st", [P, 96])
        nst = sb("nst", [P, 4, 13])
        nm = sb("nm", [P, 2 * NH, 4])
        top8 = sb("top8", [P, 16])
        rs = sb("rs", [P, 2 * NH, 4])
        pos = sb("pos", [P, TT, 2 * NE])
        comb = sb("comb", [P, TT, NE])
        need = sb("need", [1, NE + 1], i32)
        ident = cst[:, K_ID:K_ID + P]
        iota = cst[:, K_IOTA:K_IOTA + P]
        mask = cst[:, K_MASK:K_MASK + LOG]

        arena_words = 18848
        arena = sb("arena", [P, arena_words])
        base = nc.sbuf_base - 4 * arena_words

        def place(at, name, shape, dt=f32):
            n = 1
            for v in shape[1:]:
                n *= v
            assert at + n <= arena_words, (name, at + n)
            return nc.alloc_sbuf_tensor_at(name, shape, dt, offset=base + 4 * at), at + n

        xn, z = place(0, "xn", [P, TT, D])
        v0, _ = place(0, "v0", [P, TT, NH * HD])
        qT0, z = place(z, "qT0", [P, 8, S])
        kT0, z = place(z, "kT0", [P, 8, S])
        brev, z = place(z, "brev", [P, NH, S])
        sq, z = place(z, "sq", [P, TT, NT])
        qn, z1 = place(z, "qn", [P, 2, TT, NT])
        lg, z2 = place(z, "lg", [P, 4, LOG])
        pT, _ = place(z2, "pT", [P, 2, LOG])
        z = max(z1, z2 + 2 * LOG)
        idxn, z1 = place(z, "idxn", [P, TT, 384])
        iqT, z1 = place(z1, "iqT", [P, 2, S])
        ikT, z1 = place(z1, "ikT", [P, S])
        relu, z1 = place(z1, "relu", [P, 2, LOG])
        score, z1 = place(z1, "score", [P, LOG])
        dmask, z1 = place(z1, "dmask", [P, LOG])
        brow, z1 = place(z1, "brow", [16, LOG])
        bias_in, z1 = place(z1, "bias_in", [BUCKETS + 1, LOG + 16])
        grow, _ = place(z - 512, "grow", [G_ROWS, P])
        z0 = TT * D
        act_hi, z = place(z0, "act_hi", [P, FFD // P, S], f32r)
        act_lo, z = place(z, "act_lo", [P, FFD // P, S], f32r)
        sg, z = place(z, "sg", [P, TT, NT])
        hn, z = place(z, "hn", [P, 2, TT, NT])
        v1, _ = place(0, "v1", [P, TT, NH * 64])
        latn, z = place(z0, "latn", [P, TT, QR + KVR])
        rot, _ = place(z0, "rot", [P, 2, TT * GH * ROPE])
        lat_hi, z = place(z, "lat_hi", [P, 5, S], f32r)
        lg1, z1 = place(z0, "lg1", [P, 4, LOG])
        pT1, z1 = place(z1, "pT1", [P, 2, LOG])
        assert z1 <= z
        lat_lo, z = place(z, "lat_lo", [P, 5, S], f32r)
        kpe, z = place(z, "kpe", [P, TT, ROPE])
        qkT, z = place(z, "qkT", [P, NH, 2 * S])
        kpj, _ = place(z, "kpj", [P, TT * ROPE])
        qk, z = place(z, "qk", [P, 2, 2 * TT * GH, QKD])
        ffg, _ = place(z, "ffg", [P, D])
        sq1, z = place(z, "sq1", [P, TT * (QR + KVR)])
        gbc, z = place(z, "gbc", [P, 2, ROPE])
        rtab, z = place(z, "rtab", [P, 2, 2, TT, ROPE])
        h_hi, z = place(z0, "h_hi", [P, TT, D], f32r)
        h_lo, z = place(z, "h_lo", [P, TT, D], f32r)
        zr = z
        rt, _ = place(zr + D, "rt", [P, 10, TT * NE * NE])
        e_hi, z = place(zr, "e_hi", [P, FFE // P, P], f32r)
        e_lo, z = place(z, "e_lo", [P, FFE // P, P], f32r)
        sge, z = place(z, "sge", [P, 2, NT])
        he, z = place(z, "he", [P, 2, NT])
        y_hi, z = place(z, "y_hi", [P, D], f32r)
        xg, z = place(z, "xg", [P, D])
        y_lo, z = place(0, "y_lo", [P, D], f32r)
        pick, z = place(z, "pick", [P, TT, P], f32r)
        pickg, z = place(z, "pickg", [P, TT, P])
        backT, z = place(z, "backT", [P, S], f32r)

        PS = ctx.enter_context(nc.psum_tensor("PS", [P, 8, NT], f32))
        bias_dram = nc.dram_tensor("bias_scratch", [16, LOG], f32)

        raw_full = [sem(f"raw_full{i}") for i in range(RAW)]
        hi_done, lo_done, mm_done = sem("hi_done"), sem("lo_done"), sem("mm_done")

        FB0 = [sum(w // 256 for w in FF_W[:j]) for j in range(FF_TILES + 1)]
        N_GAINS = 6 + 4

        block = ctx.enter_context(nc.Block())

        @block.sync
        def _(sp):
            sp.dma_start(X[:, :, :], x[0].rearrange("(t p) d -> p t d", p=P)).then_inc(sem("x_in"), 16)
            sp.dma_start(ident, consts[:, K_ID:K_ID + P]).then_inc(sem("id_in"), 16)
            for r0, src in ((G_MIX_E, mix_norm_e), (G_FFN_E, ffn_norm_e), (G_MIX_O, mix_norm_o),
                            (G_FFN_O, ffn_norm_o), (G_QA, q_a_norm), (G_KVA, kv_a_norm)):
                n = src.shape[1] // P
                sp.dma_start(grow[r0:r0 + n, :], src[0].rearrange("(r p) -> r p", p=P)).then_inc(sem("gains_in"), 16)
            for m, src in enumerate((moba_q_norm, moba_k_norm, dsa_q_norm, dsa_k_norm)):
                sp.dma_start(grow[G_HEAD + m:G_HEAD + m + 1, :].rearrange("r (a n) -> r a n", a=2),
                             src.unsqueeze(1).to_broadcast([1, 2, HD])).then_inc(sem("gains_in"), 16)
            for c, src in enumerate(chunks):
                if c == 2:
                    sp.dma_start(cst[:, P:K_ALL], consts[:, P:K_ALL]).then_inc(sem("cst_in"), 16)
                    sp.dma_start(bias_in[:, 0:LOG], buckets).then_inc(sem("buckets_in"), 16)
                    sp.dma_start(bias_in[0:BUCKETS, LOG:LOG + 16], rel_bias).then_inc(sem("buckets_in"), 16)
                if c >= RAW:
                    sp.wait_ge(lo_done, c - RAW + 1)
                k, n = src.shape[1], src.shape[2]
                sp.dma_start(raw[:, c % RAW, 0:k * n].rearrange("p (k n) -> p k n", k=k), src)\
                    .then_inc(raw_full[c % RAW], 16)

            def expert_weights(i, e):
                for k in range(EXPERT_CHUNKS):
                    slot = (C_MOE + k) % RAW
                    sp.wait_ge(lo_done, C_MOE + k - RAW + 1 + i * EXPERT_CHUNKS)
                    if k < 4 * FE_TILES:
                        w = (w_gate_o, w_up_o)[k // 2 % 2]
                        src = w[0][bass.ds(e, 1), (k % 2) * 512:(k % 2) * 512 + 512, (k // 4) * NT:(k // 4 + 1) * NT]
                    else:
                        q = k - 4 * FE_TILES
                        src = w_down_o[0][bass.ds(e, 1), q * 256:(q + 1) * 256, :]
                    src = src.rearrange("a (k p) n -> p (a k) n", p=P)
                    sp.dma_start(raw[:, slot, :].rearrange("p (k n) -> p k n", k=src.shape[1]), src)\
                        .then_inc(raw_full[slot], 16)

            with sp.Fori(0, NE) as e:
                expert_weights(e, e)
            sp.wait_ge(sem("moe_add"), 4 * (NE + 1))
            sp.wait_ge(sem("need_set"), 1)
            most = sp.value_load(need[0:1, NE:NE + 1], min_val=-S, max_val=S)
            with sp.If(most > 0):
                with sp.Fori(0, NE) as e:
                    tokens = sp.value_load(need[0:1, bass.ds(e, 1)], min_val=-S, max_val=S)
                    with sp.If(tokens > 0):
                        expert_weights(e + NE, e)
                    with sp.Else():
                        sp.wait_ge(lo_done, C_MOE + (e + NE) * EXPERT_CHUNKS)
                        for slot in range(RAW):
                            sp.sem_inc(raw_full[slot], 16 * EXPERT_CHUNKS // RAW)
                sp.wait_ge(sem("moe_add"), 4 * (2 * NE + 1))
            sp.dma_start(out[0].rearrange("(t p) d -> p t d", p=P), X[:, :, :]).then_inc(sem("stored"), 16)
            sp.wait_ge(sem("stored"), 16)

        @block.scalar
        def _(act):
            nsplit = [0]

            def split(c):
                assert nsplit[0] == c
                nsplit[0] += 1
                act.wait_ge(raw_full[c % RAW], 16 * (c // RAW + 1))
                if c >= STG:
                    act.wait_ge(mm_done, c - STG + 1)
                n = chunks[c].shape[1] * chunks[c].shape[2]
                nc.scalar.activation(w_hi[:, c % STG, 0:n], raw[:, c % RAW, 0:n], ACT.Copy).then_inc(hi_done, 1)

            def split_to(c):
                while nsplit[0] < c:
                    split(nsplit[0])

            def norm(q):
                if q == 0:
                    act.wait_ge(sem("spare_set"), 1)
                nc.scalar.activation(nst[:, q, 12:13], nst[:, q, 12:13], ACT.Sqrt)
                if q == 0:
                    act.wait_ge(sem("x_in"), 16)
                for half in range(2):
                    cols = slice(half * NT, (half + 1) * NT)
                    if q:
                        act.wait_ge(sem("resid"), 2 * (q - 1) + half + 1)
                    for t in range(TT):
                        nc.scalar.activation(xn[:, t, cols], X[:, t, cols], ACT.Square,
                                             accum_out=nst[:, q, 2 * half + t:2 * half + t + 1]).then_inc(sem("norm_ss"), 1)
                act.wait_ge(sem("norm_ms"), q + 1)
                nc.scalar.activation(nst[:, q, 8:10], nst[:, q, 6:8], ACT.Sqrt).then_inc(sem("norm_rt"), 1)
                if q < 3:
                    act.wait_ge(sem("norm_rc"), q + 1)
                    for half in range(2):
                        cols = slice(half * NT, (half + 1) * NT)
                        nc.scalar.activation(xn[:, 1, cols], X[:, 1, cols], ACT.Copy, scale=nst[:, q, 11:12])\
                            .then_inc(sem("norm_xn1"), 1)
                if q == 0:
                    act.wait_ge(sem("gain_set"), 1)
                for c in range(4):
                    act.wait_ge(sem("norm_t"), 4 * q + c + 1)
                    if q == 3:
                        nc.scalar.activation(a_hi[:, 2 * c:2 * c + 2, :],
                                             PS[:, 4 + c, :].rearrange("p (d t) -> p d t", d=2), ACT.Copy)\
                            .then_inc(sem("norm_hi"), 2)
                        continue
                    for d in range(2):
                        dc = 2 * c + d
                        nc.scalar.activation(a_hi[:, dc, :], PS[:, 4 + c, d * S:(d + 1) * S], ACT.Copy,
                                             scale=gain[:, 8 * q + dc:8 * q + dc + 1]).then_inc(sem("norm_hi"), 1)
                if q == 3:
                    act.wait_ge(sem("hn_set"), 4)
                    for t in range(TT):
                        nc.scalar.activation(h_hi[:, t, :], xn[:, t, :], ACT.Copy).then_inc(sem("hnat_hi"), 1)

            def heads(h0, n, logits, probs_t):
                for s in range(n + 4):
                    if 3 <= s <= n + 2:
                        h = h0 + s - 3
                        act.wait_ge(sem("at_tr"), h + 1)
                        if h >= 2:
                            act.wait_ge(sem("at_pv"), h - 1)
                        nc.scalar.activation(probs_t[:, h % 2, :], PS[:, 6 + h % 2, 0:LOG], ACT.Copy)\
                            .then_inc(sem("at_pt"), 1)
                    if s < n:
                        h = h0 + s
                        act.wait_ge(sem("at_max"), h + 1)
                        nc.scalar.activation(logits[:, h % 4, 0:P], logits[:, h % 4, 0:P], ACT.Exp,
                                             bias=nm[:, h, 0:1], accum_out=rs[:, h, 0:1]).then_inc(sem("at_exp"), 1)
                        nc.scalar.activation(logits[:, h % 4, P:LOG], logits[:, h % 4, P:LOG], ACT.Exp,
                                             bias=nm[:, h, 1:2], accum_out=rs[:, h, 1:2]).then_inc(sem("at_exp"), 1)
                    if s >= 4 and (h0 + s - 4) % 2:
                        h = h0 + s - 4
                        act.wait_ge(sem("at_pv"), h + 1)
                        nc.scalar.activation(a_hi[:, h // 2 % 8, :], PS[:, h // 2 % 2, 0:S], ACT.Copy)\
                            .then_inc(sem("at_ohi"), 1)

            norm(0)
            split_to(STG)
            def qk_evac(m):
                for half in range(2):
                    act.wait_ge(sem("qk_tr"), 2 * m + half + 1)
                    bank = 4 + 2 * (m % 2) + half
                    src = PS[:, bank, :].rearrange("p (d t) -> p d t", d=2)
                    if m == 0:
                        if half == 0:
                            ins = nc.scalar.activation(iqT[:, :, :], src, ACT.Copy)
                        else:
                            ins = nc.scalar.activation(ikT[:, :], PS[:, bank, 0:S], ACT.Copy)
                    else:
                        pair, is_k = (m - 1) // 2, (m - 1) % 2
                        dst = (qT0, kT0)[is_k][:, 4 * pair + 2 * half:4 * pair + 2 * half + 2, :]
                        g = G_HEAD + m - 1 if is_k else G_ROWS + m - 1
                        ins = nc.scalar.activation(dst, src, ACT.Copy, scale=gain[:, g:g + 1])
                    ins.then_inc(sem("qk_evac"), 1)

            for n in range(7):
                split_to(min(C_IN + 2 * n + 4, C_OUTE + 1))
                m = IN_TURN[n]
                if m:
                    act.wait_ge(mm_done, C_IN + 2 * n + 2)
                    if m >= 2:
                        act.wait_ge(sem("sq_read"), m - 1)
                    nc.scalar.activation(sq[:, :, :], PS[:, 2 * (n % 2):2 * (n % 2) + 2, :], ACT.Square)\
                        .then_inc(sem("sq_set"), 1)
                    act.wait_ge(sem("qk_ms"), m)
                    nc.scalar.activation(st[:, 64:80], st[:, 48:64], ACT.Sqrt).then_inc(sem("qk_rt"), 1)
                if n >= 1 and IN_TURN[n - 1] is not None:
                    qk_evac(IN_TURN[n - 1])
                if n == 2:
                    for h in range(IDXH):
                        act.wait_ge(sem("idx_mm"), h + 1)
                        if h >= 2:
                            act.wait_ge(sem("idx_acc"), 2 * (h - 1))
                        nc.scalar.activation(relu[:, h % 2, :], PS[:, 4 + h % 2, 0:LOG], ACT.Relu).then_inc(sem("idx_relu"), 1)
            split_to(C_OUTE + STG)
            heads(0, NH, lg, pT)
            split_to(C_FF + 2)
            norm(1)

            def ff_evac(j):
                for k in range(FB0[j], FB0[j + 1]):
                    act.wait_ge(sem("ff_tr"), k + 1)
                    nc.scalar.activation(act_hi[:, 2 * k:2 * k + 2, :],
                                         PS[:, 4 + k % 4, :].rearrange("p (d t) -> p d t", d=2), ACT.Copy)\
                        .then_inc(sem("ff_hi"), 1)

            for k in range(4 * FF_TILES + 4):
                split_to(max(nsplit[0], C_FF + k + 1))
                if k % 4 == 3 and k // 4 < FF_TILES:
                    j = k // 4
                    w = FF_W[j]
                    act.wait_ge(mm_done, C_FF + 4 * j + 2)
                    if j >= 1:
                        act.wait_ge(sem("up_read"), j)
                    nc.scalar.activation(sg[:, :, 0:w], PS[:, 0:2, 0:w], ACT.Silu).then_inc(sem("gate_read"), 1)
                if k % 4 == 3 and k >= 7:
                    ff_evac((k - 7) // 4)
            split_to(C_LAT + 2)

            norm(2)
            split_to(C_LAT + 4)

            def lat_evac(ds):
                for d in ds:
                    bank, off = ((4, 0), (4, S), (5, 0), (6, 0), (6, S))[d]
                    act.wait_ge(sem("lat_tr"), bank - 3)
                    nc.scalar.activation(lat_hi[:, d, :], PS[:, bank, off:off + S], ACT.Copy,
                                         scale=gain[:, G_QA + d:G_QA + d + 1]).then_inc(sem("lat_hi"), 1)

            act.wait_ge(mm_done, C_LAT + 2)
            for t in range(TT):
                nc.scalar.activation(sq1[:, t * QR:(t + 1) * QR], PS[:, t, 0:QR], ACT.Square,
                                     accum_out=st[:, 24 + t:25 + t]).then_inc(sem("lat_ss"), 1)
            act.wait_ge(sem("lat_ms"), 1)
            nc.scalar.activation(st[:, 34:36], st[:, 30:32], ACT.Sqrt).then_inc(sem("lat_rt"), 1)
            split_to(C_HEADS + 2)
            lat_evac((0, 1, 2))
            act.wait_ge(mm_done, C_LAT + 4)
            for t in range(TT):
                nc.scalar.activation(sq1[:, TT * QR + t * KVR:TT * QR + (t + 1) * KVR], PS[:, 2 + t, 0:KVR], ACT.Square,
                                     accum_out=st[:, 26 + t:27 + t]).then_inc(sem("lat_ss"), 1)
                nc.scalar.activation(kpj[:, t * ROPE:(t + 1) * ROPE], PS[:, 2 + t, KVR:KVR + ROPE], ACT.Square,
                                     accum_out=st[:, 28 + t:29 + t]).then_inc(sem("lat_ss"), 1)
            act.wait_ge(sem("lat_ms"), 2)
            nc.scalar.activation(st[:, 36:38], st[:, 32:34], ACT.Sqrt).then_inc(sem("lat_rt"), 1)
            lat_evac((3, 4))
            split_to(C_HEADS + 3)
            def group_evac(g, half):
                for h in range(GH * g + 2 * half, GH * g + 2 * half + 2):
                    act.wait_ge(sem("grp_tr"), h + 1)
                    for s, col in enumerate((G_ROWS + 4, G_MLA + 1)):
                        nc.scalar.activation(qkT[0:QKD, h, s * S:(s + 1) * S], PS[0:QKD, 6 + h % 2, s * S:(s + 1) * S],
                                             ACT.Copy, scale=gain[0:QKD, col:col + 1]).then_inc(sem("grp_ev"), 1)

            for g in range(GROUPS):
                qb, kb = 2 * (2 * g % 3), 2 * ((2 * g + 1) % 3)
                kv = PS[:, kb:kb + 2, :].rearrange("p t (h n) -> p t h n", h=GH)
                act.wait_ge(mm_done, C_HEADS + 2 * g + 1)
                if g >= 1:
                    act.wait_ge(sem("grp_sqread"), 2 * g)
                nc.scalar.activation(sq1[:, 0:TT * QR].rearrange("p (t n) -> p t n", t=TT),
                                     PS[:, qb:qb + 2, 0:GH * QKD], ACT.Square).then_inc(sem("grp_sq"), 1)
                if g >= 2:
                    group_evac(g - 2, 1)
                act.wait_ge(mm_done, C_HEADS + 2 * g + 2)
                nc.scalar.activation(sq1[:, TT * QR:TT * QR + TT * GH * 64].rearrange("p (t h n) -> p t h n", t=TT, h=GH),
                                     kv[:, :, :, 0:64], ACT.Square).then_inc(sem("grp_sq"), 1)
                nc.scalar.activation(v1[:, :, g * GH * 64:(g + 1) * GH * 64].rearrange("p t (h n) -> p t h n", h=GH),
                                     kv[:, :, :, 64:128], ACT.Copy).then_inc(sem("v_read"), 1)
                act.wait_ge(sem("grp_ms"), g + 1)
                nc.scalar.activation(st[:, 64:80], st[:, 48:64], ACT.Sqrt).then_inc(sem("grp_rt"), 1)
                split_to(C_HEADS + 2 * g + 4)
                if g >= 1:
                    group_evac(g - 1, 0)
                split_to(C_HEADS + 2 * g + 5)
            group_evac(GROUPS - 2, 1)
            group_evac(GROUPS - 1, 0)
            group_evac(GROUPS - 1, 1)
            heads(NH, NH, lg1, pT1)
            split_to(C_MOE)
            norm(3)

            def esplit(i, k):
                c = C_MOE + k
                act.wait_ge(raw_full[c % RAW], 16 * (c // RAW + 1) + i * (16 * EXPERT_CHUNKS // RAW))
                act.wait_ge(mm_done, c - STG + 1 + i * EXPERT_CHUNKS)
                nc.scalar.activation(w_hi[:, c % STG, :], raw[:, c % RAW, :], ACT.Copy).then_inc(hi_done, 1)

            def gathered(i):
                for h in range(2):
                    act.wait_ge(sem("moe_gath"), 2 * i + h + 1)
                    nc.scalar.activation(xg[:, h * NT:(h + 1) * NT], PS[:, 4 + h, :], ACT.Copy).then_inc(sem("moe_xg"), 1)

            def turned(i):
                for h in range(2):
                    act.wait_ge(sem("moe_xt"), 2 * i + h + 1)
                    nc.scalar.activation(a_hi[:, 4 * h:4 * h + 4, 0:P],
                                         PS[:, 4 + h, :].rearrange("p (d t) -> p d t", d=4), ACT.Copy)\
                        .then_inc(sem("moe_xhi"), 1)

            def result(i):
                act.wait_ge(mm_done, C_MOE + (i + 1) * EXPERT_CHUNKS)
                nc.scalar.activation(y_hi[:, :].rearrange("p (a n) -> p a n", a=2), PS[:, 2:4, :], ACT.Copy,
                                     scale=st[:, 90:91]).then_inc(sem("moe_yhi"), 1)

            def expert(i, follow):
                for k in range(STG, EXPERT_CHUNKS + STG * follow):
                    esplit(i, k)
                    if k % 4 == 3 and k // 4 < FE_TILES:
                        j = k // 4
                        act.wait_ge(mm_done, C_MOE + 4 * j + 2 + i * EXPERT_CHUNKS)
                        if j >= 2:
                            act.wait_ge(sem("moe_mul"), j - 1 + i * FE_TILES)
                        nc.scalar.activation(sge[:, j % 2, :], PS[:, j % 2, :], ACT.Silu).then_inc(sem("moe_silu"), 1)
                    if k % 4 == 3 and 7 <= k < 7 + 4 * FE_TILES:
                        j = (k - 7) // 4
                        act.wait_ge(sem("moe_tr"), j + 1 + i * FE_TILES)
                        nc.scalar.activation(e_hi[:, 4 * j:4 * j + 4, :],
                                             PS[:, 6 + j % 2, :].rearrange("p (d t) -> p d t", d=4), ACT.Copy)\
                            .then_inc(sem("moe_ahi"), 1)
                    if follow and k == GATHER_AT + 2:
                        gathered(i + 1)
                    if follow and k == GATHER_AT + 6:
                        turned(i + 1)
                    if follow and k == EXPERT_CHUNKS + 1:
                        result(i)
                if not follow:
                    result(i)

            for k in range(STG):
                esplit(0, k)
                if k == 0:
                    act.wait_ge(sem("top_sub"), 1)
                    nc.scalar.activation(rt[:, 4, 0:TT * NE], rt[:, 3, 0:TT * NE], ACT.Exp).then_inc(sem("top_exp"), 1)
            gathered(0)
            turned(0)
            with act.Fori(0, NE - 1) as e:
                expert(e, True)
            expert(NE - 1, False)
            act.wait_ge(sem("need_set"), 1)
            most = act.value_load(need[0:1, NE:NE + 1], min_val=-S, max_val=S)
            with act.If(most > 0):
                with act.Fori(0, NE) as e:
                    i = e + NE
                    tokens = act.value_load(need[0:1, bass.ds(e, 1)], min_val=-S, max_val=S)
                    with act.If(tokens > 0):
                        for k in range(STG):
                            esplit(i, k)
                        gathered(i)
                        turned(i)
                        expert(i, False)
                    with act.Else():
                        act.drain()
                        act.sem_inc(hi_done, EXPERT_CHUNKS)
                        act.sem_inc(sem("moe_xg"), 2)
                        act.sem_inc(sem("moe_xhi"), 2)
                        act.sem_inc(sem("moe_silu"), FE_TILES)
                        act.sem_inc(sem("moe_ahi"), FE_TILES)
                        act.sem_inc(sem("moe_yhi"), 1)

        @block.vector
        def _(dve):
            steps = [0]

            def step(ins):
                steps[0] += 1
                ins.then_inc(sem("dve_step"), 1)
                dve.wait_ge(sem("dve_step"), steps[0])

            nsplit = [0]

            def split(c):
                assert nsplit[0] == c
                nsplit[0] += 1
                n = chunks[c].shape[1] * chunks[c].shape[2]
                dve.wait_ge(hi_done, c + 1)
                nc.vector.tensor_tensor(w_lo[:, c % STG, 0:n], raw[:, c % RAW, 0:n], w_hi[:, c % STG, 0:n],
                                        ALU.subtract).then_inc(lo_done, 1)

            def split_to(c):
                while nsplit[0] < c:
                    split(nsplit[0])

            def gains():
                dve.wait_ge(sem("gain_tr"), 1)
                nc.vector.tensor_copy(gain[:, 0:G_ROWS], PS[:, 0, 0:G_ROWS]).then_inc(sem("gain_copy"), 1)
                dve.wait_ge(sem("gain_copy"), 1)
                nc.vector.tensor_scalar(gain[:, G_ROWS:G_ROWS + 4], gain[:, G_HEAD:G_HEAD + 4], HD ** -0.5, None, ALU.mult)\
                    .then_inc(sem("gain_set"), 1)
                dve.wait_ge(sem("gain_set"), 1)
                step(nc.vector.memset(gain[64:P, G_MLA:G_MLA + 2], 1.0))
                step(nc.vector.tensor_scalar(gain[:, G_ROWS + 4:G_ROWS + 5], gain[:, G_MLA:G_MLA + 1], QKD ** -0.5, None, ALU.mult))

            def norm(q):
                dve.wait_ge(sem("norm_ss"), 4 * q + 2)
                step(nc.vector.tensor_scalar(nst[:, q, 4:6], nst[:, q, 0:2], 1.0 / D, EPS, ALU.mult, ALU.add))
                dve.wait_ge(sem("norm_ss"), 4 * q + 4)
                nc.vector.scalar_tensor_tensor(out=nst[:, q, 6:8], in0=nst[:, q, 2:4], scalar=1.0 / D, in1=nst[:, q, 4:6],
                                               op0=ALU.mult, op1=ALU.add).then_inc(sem("norm_ms"), 1)
                dve.wait_ge(sem("norm_rt"), q + 1)
                nc.vector.reciprocal(nst[:, q, 10:12], nst[:, q, 8:10]).then_inc(sem("norm_rc"), 1)
                dve.wait_ge(sem("norm_rc"), q + 1)
                for half in range(2):
                    cols = slice(half * NT, (half + 1) * NT)
                    if q < 3:
                        nc.vector.tensor_scalar(xn[:, 0, cols], X[:, 0, cols], nst[:, q, 10:11], None, ALU.mult)\
                            .then_inc(sem("norm_xn0"), 1)
                        continue
                    for t in range(TT):
                        nc.vector.scalar_tensor_tensor(out=xn[:, t, cols], in0=X[:, t, cols], scalar=nst[:, q, 10 + t:11 + t],
                                                       in1=ffg[:, cols], op0=ALU.mult, op1=ALU.mult).then_inc(sem("hn_set"), 1)
                if q == 0:
                    gains()
                for c in range(4):
                    dve.wait_ge(sem("norm_hi"), 8 * q + 2 * c + 2)
                    if q == 3:
                        nc.vector.tensor_tensor(a_lo[:, 2 * c:2 * c + 2, :],
                                                PS[:, 4 + c, :].rearrange("p (d t) -> p d t", d=2),
                                                a_hi[:, 2 * c:2 * c + 2, :], ALU.subtract).then_inc(sem("norm_lo"), 2)
                        continue
                    for d in range(2):
                        dc = 2 * c + d
                        nc.vector.scalar_tensor_tensor(out=a_lo[:, dc, :], in0=PS[:, 4 + c, d * S:(d + 1) * S],
                                                       scalar=gain[:, 8 * q + dc:8 * q + dc + 1],
                                                       in1=a_hi[:, dc, :].bitcast(f32), op0=ALU.mult,
                                                       op1=ALU.subtract).then_inc(sem("norm_lo"), 1)
                if q == 3:
                    for t in range(TT):
                        dve.wait_ge(sem("hnat_hi"), t + 1)
                        nc.vector.tensor_tensor(h_lo[:, t, :], xn[:, t, :], h_hi[:, t, :], ALU.subtract)\
                            .then_inc(sem("hnat_lo"), 1)

            def heads(h0, n, logits, bias):
                for s in range(n + 5):
                    if s < n:
                        h = h0 + s
                        dve.wait_ge(sem("at_qk"), h + 1)
                        if h >= 4:
                            dve.wait_ge(sem("at_tr"), h - 3)
                        bank = PS[:, 4 + h % 2, :]
                        for t, (a, b) in enumerate(((0, P), (P, LOG))):
                            out, top = logits[:, h % 4, a:b], nm[:, h, 2 + t:3 + t]
                            if bias and h >= 8:
                                ins = nc.vector.tensor_tensor(out, bank[:, a:b], brev[:, h, 0:b - a][:, ::-1], ALU.add)
                            else:
                                ins = nc.vector.tensor_tensor_reduce(
                                    out, bank[:, a:b], brev[:, h, 0:b - a][:, ::-1] if bias else mask[:, a:b],
                                    1.0, TAKEN, ALU.add, ALU.max, top)
                        ins.then_inc(sem("at_add"), 1)
                        dve.wait_ge(sem("at_add"), h + 1)
                        if bias and h >= 8:
                            for t, (a, b) in enumerate(((0, P), (P, LOG))):
                                out, top = logits[:, h % 4, a:b], nm[:, h, 2 + t:3 + t]
                                ins = nc.vector.tensor_tensor_reduce(out, out, dmask[:, a:b], 1.0, TAKEN, ALU.add, ALU.max, top)
                            step(ins)
                        nc.vector.tensor_scalar(nm[:, h, 0:2], nm[:, h, 2:4], -1.0, None, ALU.mult).then_inc(sem("at_max"), 1)
                    if 1 <= s <= n:
                        h = h0 + s - 1
                        dve.wait_ge(sem("at_exp"), 2 * h + 2)
                        nc.vector.reciprocal(rs[:, h, 2:4], rs[:, h, 0:2]).then_inc(sem("at_rcp"), 1)
                        dve.wait_ge(sem("at_rcp"), h + 1)
                        nc.vector.tensor_scalar(logits[:, h % 4, 0:P], logits[:, h % 4, 0:P], rs[:, h, 2:3], None, ALU.mult)\
                            .then_inc(sem("at_norm0"), 1)
                    if s >= 5 and (h0 + s - 5) % 2:
                        h = h0 + s - 5
                        dve.wait_ge(sem("at_ohi"), h // 2 + 1)
                        nc.vector.tensor_tensor(a_lo[:, h // 2 % 8, :], PS[:, h // 2 % 2, 0:S], a_hi[:, h // 2 % 8, :],
                                                ALU.subtract).then_inc(sem("at_olo"), 1)

            nc.vector.memset(bias_in[BUCKETS:BUCKETS + 1, LOG:LOG + 16], 1.0).then_inc(sem("ones_set"), 1)
            nc.vector.memset(nst[:, :, 12:13], 1.0).then_inc(sem("spare_set"), 1)
            norm(0)
            split_to(STG)

            def top_rounds(r0, r1):
                for r in range(r0, r1):
                    nc.vector.max(top8[:, 0:8], score[:, 0:P])
                    step(nc.vector.max(top8[:, 8:16], score[:, P:LOG]))
                    nc.vector.match_replace(score[:, 0:P], top8[:, 0:8], score[:, 0:P], TAKEN)
                    step(nc.vector.match_replace(score[:, P:LOG], top8[:, 8:16], score[:, P:LOG], TAKEN))

            for n in range(7):
                split_to(min(C_IN + 2 * n + 4, C_OUTE + 1))
                dve.wait_ge(mm_done, C_IN + 2 * n + 2)
                pair = PS[:, 2 * (n % 2):2 * (n % 2) + 2, :]
                m = IN_TURN[n]
                if m:
                    dve.wait_ge(sem("sq_set"), m)
                    nc.vector.tensor_reduce(st[:, 80:96], sq[:, :, :].rearrange("p t (h d) -> p (t h) d", d=HD), AX.X, ALU.add)\
                        .then_inc(sem("sq_read"), 1)
                    dve.wait_ge(sem("sq_read"), m)
                    nc.vector.tensor_scalar(st[:, 48:64], st[:, 80:96], 1.0 / HD, EPS, ALU.mult, ALU.add)\
                        .then_inc(sem("qk_ms"), 1)
                    dve.wait_ge(sem("qk_rt"), m)
                    step(nc.vector.reciprocal(st[:, 48:64], st[:, 64:80]))
                    if m >= 3:
                        dve.wait_ge(sem("qk_tr"), 2 * (m - 1))
                    nc.vector.tensor_tensor(qn[:, m % 2, :, :].rearrange("p t (h d) -> p t h d", d=HD),
                                            pair.rearrange("p t (h d) -> p t h d", d=HD),
                                            st[:, 48:64].rearrange("p (t h) -> p t h", t=TT).unsqueeze(3).to_broadcast([P, TT, 8, HD]),
                                            ALU.mult).then_inc(sem("tile_read"), 1)
                elif n:
                    if n == 3:
                        dve.wait_ge(sem("norm_t"), 4)
                    nc.vector.tensor_copy(v0[:, :, (n // 6) * NT:(n // 6 + 1) * NT], pair).then_inc(sem("tile_read"), 1)
                else:
                    nc.vector.tensor_copy(idxn[:, :, 0:320], pair[:, :, 0:320])
                    nc.vector.tensor_copy(idxn[:, :, 320:384], pair[:, :, 256:320])
                    nc.vector.tensor_scalar(st[:, 16:24].rearrange("p (t h) -> p t h", t=TT), pair[:, :, 320:324],
                                            HD ** -0.5 * IDXH ** -0.5, None, ALU.mult).then_inc(sem("tile_read"), 1)
                    dve.wait_ge(sem("brow_mm"), 1)
                    nc.vector.tensor_copy(brow[:, :], PS[0:16, 7, 0:LOG]).then_inc(sem("brow_set"), 1)
                if n == 2:
                    dve.wait_ge(sem("cst_in"), 16)
                    for h in range(IDXH):
                        dve.wait_ge(sem("idx_relu"), h + 1)
                        for t, (a, b) in enumerate(((0, P), (P, LOG))):
                            if h:
                                dve.wait_ge(sem("idx_acc"), 2 * h - 1 + t)
                            nc.vector.scalar_tensor_tensor(out=score[:, a:b], in0=relu[:, h % 2, a:b],
                                                           scalar=st[:, 16 + 4 * t + h:17 + 4 * t + h],
                                                           in1=(score[:, a:b] if h else cst[:, K_MASK + a:K_MASK + b]),
                                                           op0=ALU.mult, op1=ALU.add).then_inc(sem("idx_acc"), 1)
                    dve.wait_ge(sem("idx_acc"), 2 * IDXH)
                if 3 <= n <= 6:
                    top_rounds(2 * (n - 3), 2 * (n - 2))
            step(nc.vector.tensor_scalar(dmask[:, :], score[:, :], TAKEN / 2, MASKED, ALU.is_gt, ALU.mult))
            split_to(C_OUTE + STG)
            dve.wait_ge(sem("bias_in"), 16)
            heads(0, NH, lg, True)

            def residual(n, result):
                half = X[:, :, n * NT:(n + 1) * NT]
                nc.vector.tensor_tensor(half, half, result, ALU.add).then_inc(sem("resid"), 1)

            def residuals(c_out, c_next):
                split_to(c_out + 4)
                dve.wait_ge(mm_done, c_out + 2)
                residual(0, PS[:, 0:2, :])
                split_to(c_next)
                dve.wait_ge(mm_done, c_out + 4)
                residual(1, PS[:, 2:4, :])

            residuals(C_OUTE, C_FF + 2)
            norm(1)

            def ff_evac(j):
                for k in range(FB0[j], FB0[j + 1]):
                    dve.wait_ge(sem("ff_hi"), k + 1)
                    nc.vector.tensor_tensor(act_lo[:, 2 * k:2 * k + 2, :],
                                            PS[:, 4 + k % 4, :].rearrange("p (d t) -> p d t", d=2),
                                            act_hi[:, 2 * k:2 * k + 2, :], ALU.subtract).then_inc(sem("ff_lo"), 1)

            for k in range(4 * FF_TILES + 4):
                split_to(max(nsplit[0], C_FF + k + 1))
                if k % 4 == 1 and k >= 5:
                    j = (k - 5) // 4
                    w = FF_W[j]
                    dve.wait_ge(sem("gate_read"), j + 1)
                    dve.wait_ge(mm_done, C_FF + 4 * j + 4)
                    if j >= 2:
                        dve.wait_ge(sem("ff_tr"), FB0[j - 1])
                    nc.vector.tensor_tensor(hn[:, j % 2, :, 0:w], PS[:, 2:4, 0:w], sg[:, :, 0:w], ALU.mult)\
                        .then_inc(sem("up_read"), 1)
                if k % 4 == 3 and k >= 7:
                    ff_evac((k - 7) // 4)
            split_to(C_LAT + 1)
            dve.wait_ge(sem("down_half"), 1)
            residual(0, PS[:, 0:2, :])
            split_to(C_LAT + 2)
            dve.wait_ge(mm_done, C_LAT)
            residual(1, PS[:, 2:4, :])
            norm(2)
            split_to(C_LAT + 4)

            def lat_split(ds):
                for d in ds:
                    bank, off = ((4, 0), (4, S), (5, 0), (6, 0), (6, S))[d]
                    dve.wait_ge(sem("lat_hi"), (2, 2, 3, 5, 5)[d])
                    nc.vector.scalar_tensor_tensor(out=lat_lo[:, d, :], in0=PS[:, bank, off:off + S],
                                                   scalar=gain[:, G_QA + d:G_QA + d + 1],
                                                   in1=lat_hi[:, d, :].bitcast(f32), op0=ALU.mult, op1=ALU.subtract)\
                        .then_inc(sem("lat_lo"), 1)

            dve.wait_ge(sem("lat_ss"), 2)
            nc.vector.tensor_scalar(st[:, 30:32], st[:, 24:26], 1.0 / QR, EPS, ALU.mult, ALU.add).then_inc(sem("lat_ms"), 1)
            dve.wait_ge(sem("lat_rt"), 1)
            step(nc.vector.reciprocal(st[:, 44:46], st[:, 34:36]))
            for t in range(TT):
                ins = nc.vector.tensor_scalar(latn[:, t, 0:QR], PS[:, t, 0:QR], st[:, 44 + t:45 + t], None, ALU.mult)
            ins.then_inc(sem("lat_n"), 1)
            split_to(C_HEADS + 2)
            lat_split((0, 1, 2))
            dve.wait_ge(sem("lat_ss"), 6)
            nc.vector.tensor_scalar(st[:, 32:34], st[:, 26:28], 1.0 / KVR, EPS, ALU.mult, ALU.add).then_inc(sem("lat_ms"), 1)
            dve.wait_ge(sem("lat_rt"), 2)
            step(nc.vector.reciprocal(st[:, 46:48], st[:, 36:38]))
            for t in range(TT):
                nc.vector.tensor_copy(kpe[:, t, :], PS[:, 2 + t, KVR:KVR + ROPE])
                ins = nc.vector.tensor_scalar(latn[:, t, QR:QR + KVR], PS[:, 2 + t, 0:KVR], st[:, 46 + t:47 + t], None, ALU.mult)
            ins.then_inc(sem("lat_n"), 1)
            lat_split((3, 4))
            split_to(C_HEADS + 3)
            dve.wait_ge(sem("gbc_in"), 32)
            for b, at in enumerate((K_COS, K_SIN)):
                for s in range(2):
                    tab = cst[:, at:at + TT * 16].rearrange("p (t n) -> p t n", t=TT)
                    ins = nc.vector.tensor_tensor(rtab[:, s, b, :, :].rearrange("p t (a n) -> p t a n", a=2),
                                                  gbc[:, s, :].rearrange("p (a n) -> p a n", a=2).unsqueeze(1).to_broadcast([P, TT, 2, 16]),
                                                  tab.unsqueeze(2).to_broadcast([P, TT, 2, 16]), ALU.mult)
            step(ins)
            rk2 = [rot[:, b, 0:TT * ROPE].rearrange("p (t n) -> p t n", t=TT) for b in range(2)]
            nc.vector.tensor_tensor(rk2[0], kpe[:, :, :], rtab[:, 1, 0, :, :], ALU.mult)
            step(nc.vector.tensor_tensor(rk2[1], kpe[:, :, :], rtab[:, 1, 1, :, :], ALU.mult))
            nc.vector.tensor_tensor(kpe[:, :, 0:16], rk2[0][:, :, 0:16], rk2[1][:, :, 16:32], ALU.subtract)
            step(nc.vector.tensor_tensor(kpe[:, :, 16:32], rk2[0][:, :, 16:32], rk2[1][:, :, 0:16], ALU.add))
            TH = TT * GH
            for g in range(GROUPS):
                qb, kb = 2 * (2 * g % 3), 2 * ((2 * g + 1) % 3)
                dve.wait_ge(sem("grp_sq"), 2 * g + 1)
                nc.vector.tensor_reduce(st[:, 80:80 + TH], sq1[:, 0:TT * QR].rearrange("p (a n) -> p a n", n=QKD),
                                        AX.X, ALU.add).then_inc(sem("grp_sqread"), 1)
                dve.wait_ge(sem("grp_sq"), 2 * g + 2)
                nc.vector.tensor_reduce(st[:, 80 + TH:96],
                                        sq1[:, TT * QR:TT * QR + TH * 64].rearrange("p (a n) -> p a n", n=64),
                                        AX.X, ALU.add).then_inc(sem("grp_sqread"), 1)
                dve.wait_ge(sem("grp_sqread"), 2 * g + 2)
                for t in range(TT):
                    ins = nc.vector.tensor_scalar(st[:, 80 + TH + GH * t:80 + TH + GH * t + GH],
                                                  st[:, 80 + TH + GH * t:80 + TH + GH * t + GH],
                                                  st[:, 28 + t:29 + t], None, ALU.add)
                step(ins)
                nc.vector.tensor_scalar(st[:, 48:64], st[:, 80:96], 1.0 / QKD, EPS, ALU.mult, ALU.add)\
                    .then_inc(sem("grp_ms"), 1)
                dve.wait_ge(sem("grp_rt"), g + 1)
                step(nc.vector.reciprocal(st[:, 48:64], st[:, 64:80]))
                if g >= 2:
                    dve.wait_ge(sem("grp_tr"), GH * (g - 1))
                rq = st[:, 48:48 + TH].rearrange("p (t h) -> p t h", t=TT)
                rk = st[:, 48 + TH:64].rearrange("p (t h) -> p t h", t=TT)
                q4 = qk[:, g % 2, 0:TH, :].rearrange("p (t h) n -> p t h n", t=TT)
                k4 = qk[:, g % 2, TH:2 * TH, :].rearrange("p (t h) n -> p t h n", t=TT)
                kv = PS[:, kb:kb + 2, :].rearrange("p t (h n) -> p t h n", h=GH)
                nc.vector.tensor_tensor(q4, PS[:, qb:qb + 2, 0:GH * QKD].rearrange("p t (h n) -> p t h n", h=GH),
                                        rq.unsqueeze(3).to_broadcast([P, TT, GH, QKD]), ALU.mult).then_inc(sem("item_read"), 1)
                nc.vector.tensor_tensor(k4[:, :, :, 0:64], kv[:, :, :, 0:64],
                                        rk.unsqueeze(3).to_broadcast([P, TT, GH, 64]), ALU.mult).then_inc(sem("item_read"), 1)
                nc.vector.tensor_tensor(k4[:, :, :, 64:96], kpe[:, :, :].unsqueeze(2).to_broadcast([P, TT, GH, ROPE]),
                                        rk.unsqueeze(3).to_broadcast([P, TT, GH, ROPE]), ALU.mult)
                split_to(C_HEADS + 2 * g + 4)
                dve.wait_ge(sem("item_read"), 2 * g + 1)
                xq = q4[:, :, :, 64:96]
                r2 = [rot[:, b, :].rearrange("p (t h n) -> p t h n", t=TT, h=GH) for b in range(2)]
                for b in range(2):
                    ins = nc.vector.tensor_tensor(r2[b], xq, rtab[:, 0, b, :, :].unsqueeze(2).to_broadcast([P, TT, GH, ROPE]),
                                                  ALU.mult)
                step(ins)
                nc.vector.tensor_tensor(xq[:, :, :, 0:16], r2[0][:, :, :, 0:16], r2[1][:, :, :, 16:32], ALU.subtract)
                nc.vector.tensor_tensor(xq[:, :, :, 16:32], r2[0][:, :, :, 16:32], r2[1][:, :, :, 0:16], ALU.add)\
                    .then_inc(sem("grp_qk"), 1)
                split_to(C_HEADS + 2 * g + 5)
            heads(NH, NH, lg1, False)
            residuals(C_OUTO, C_MOE)
            dve.wait_ge(sem("ffg_in"), 16)
            norm(3)

            dve.wait_ge(sem("bias8_in"), 16)
            dve.wait_ge(mm_done, C_ROUTE + 1)
            R = lambda k: rt[:, k, 0:TT * NE].rearrange("p (t e) -> p t e", t=TT)
            F = lambda k: rt[:, k, :].rearrange("p (t e f) -> p t e f", t=TT, e=NE)
            wide = [P, TT, NE, NE]
            step(nc.vector.tensor_tensor(R(0), PS[:, 0:2, 0:NE],
                                         gate_bias[:, :].unsqueeze(1).to_broadcast([P, TT, NE]), ALU.add))
            other, own = R(0).unsqueeze(2).to_broadcast(wide), R(0).unsqueeze(3).to_broadcast(wide)
            low = cst[:, K_LOW:K_LOW + NE * NE].rearrange("p (e f) -> p e f", e=NE).unsqueeze(1).to_broadcast(wide)
            nc.vector.tensor_tensor(F(1), other, own, ALU.is_gt)
            nc.vector.tensor_reduce(st[:, 40:42], R(0), AX.X, ALU.max)
            step(nc.vector.tensor_tensor(F(2), other, own, ALU.is_equal))
            nc.vector.tensor_tensor(R(3), R(0), st[:, 40:42].unsqueeze(2).to_broadcast([P, TT, NE]), ALU.subtract)\
                .then_inc(sem("top_sub"), 1)
            step(nc.vector.tensor_tensor(F(2), F(2), low, ALU.mult))
            step(nc.vector.tensor_tensor(F(1), F(1), F(2), ALU.add))
            step(nc.vector.tensor_reduce(R(5), F(1), AX.X, ALU.add))
            nc.vector.tensor_scalar(R(6), R(5), 1.5, None, ALU.is_lt).then_inc(sem("sel_set"), 1)
            dve.wait_ge(sem("sel_set"), 1)
            FAR = 1000.0
            dve.wait_ge(sem("place_mm"), 1)
            step(nc.vector.tensor_scalar(R(7), PS[:, 4:6, 0:NE], FAR, None, ALU.add))
            step(nc.vector.tensor_tensor(R(7), R(7), R(6), ALU.mult))
            for b in range(2):
                ins = nc.vector.tensor_scalar(pos[:, :, b * NE:(b + 1) * NE], R(7), -FAR - b * P, None, ALU.add)
            step(ins)
            nc.vector.tensor_scalar(need[:, 0:NE], PS[0:1, 6, 0:NE], -float(P), None, ALU.add)
            step(nc.vector.tensor_reduce(st[0:1, 92:93], PS[0:1, 6, 0:NE], AX.X, ALU.max))
            nc.vector.tensor_scalar(need[:, NE:NE + 1], st[0:1, 92:93], -float(P), None, ALU.add).then_inc(sem("need_set"), 1)

            def gates():
                dve.wait_ge(sem("top_exp"), 1)
                step(nc.vector.tensor_tensor(R(4), R(4), R(6), ALU.mult))
                step(nc.vector.tensor_reduce(st[:, 42:44], R(4), AX.X, ALU.add))
                step(nc.vector.reciprocal(st[:, 40:42], st[:, 42:44]))
                step(nc.vector.tensor_tensor(comb[:, :, :], R(4), st[:, 40:42].unsqueeze(2).to_broadcast([P, TT, NE]), ALU.mult))

            def esplit(i, k):
                c = C_MOE + k
                dve.wait_ge(hi_done, c + 1 + i * EXPERT_CHUNKS)
                nc.vector.tensor_tensor(w_lo[:, c % STG, :], raw[:, c % RAW, :], w_hi[:, c % STG, :],
                                        ALU.subtract).then_inc(lo_done, 1)

            def picks(i, e):
                for t in range(TT):
                    ins = nc.vector.tensor_scalar(pick[:, t, :], iota, pos[:, t, bass.ds(i, 1)], None, ALU.is_equal)
                ins.then_inc(sem("moe_pick"), 1)

            def gated_picks(i, e):
                for t in range(TT):
                    ins = nc.vector.tensor_scalar(pickg[:, t, :], iota, pos[:, t, bass.ds(i, 1)],
                                                  comb[:, t, bass.ds(e, 1)], ALU.is_equal, ALU.mult)
                ins.then_inc(sem("moe_pickg"), 1)

            def turned(i):
                for h in range(2):
                    dve.wait_ge(sem("moe_xhi"), 2 * i + h + 1)
                    nc.vector.tensor_tensor(a_lo[:, 4 * h:4 * h + 4, 0:P],
                                            PS[:, 4 + h, :].rearrange("p (d t) -> p d t", d=4),
                                            a_hi[:, 4 * h:4 * h + 4, 0:P], ALU.subtract).then_inc(sem("moe_xlo"), 1)

            def result(i):
                dve.wait_ge(sem("moe_yhi"), i + 1)
                nc.vector.scalar_tensor_tensor(out=y_lo[:, :].rearrange("p (a n) -> p a n", a=2), in0=PS[:, 2:4, :],
                                               scalar=st[:, 90:91],
                                               in1=y_hi[:, :].bitcast(f32).rearrange("p (a n) -> p a n", a=2),
                                               op0=ALU.mult, op1=ALU.subtract).then_inc(sem("moe_ylo"), 1)

            def add_back(n):
                for s in range(4):
                    t, h = s // 2, s % 2
                    dve.wait_ge(sem("moe_sc"), 4 * n + s + 1)
                    nc.vector.tensor_tensor(X[:, t, h * NT:(h + 1) * NT], X[:, t, h * NT:(h + 1) * NT],
                                            PS[:, 4 + s, :], ALU.add).then_inc(sem("moe_add"), 1)

            def expert(i, follow, alone=False):
                for k in range(STG, EXPERT_CHUNKS + STG * follow):
                    esplit(i, k)
                    if k == 3:
                        if not alone:
                            add_back(i)
                        dve.wait_ge(sem("moe_turn"), i + 1)
                        nc.vector.tensor_reduce(st[:, 90:91], PS[:, 3, 0:S], AX.X, ALU.add)
                        nc.vector.tensor_scalar(backT[:, :], PS[:, 3, 0:S], 0.0, None, ALU.is_gt).then_inc(sem("moe_back"), 1)
                    if k % 4 == 1 and 5 <= k < 5 + 4 * FE_TILES:
                        j = (k - 5) // 4
                        dve.wait_ge(sem("moe_silu"), j + 1 + i * FE_TILES)
                        dve.wait_ge(mm_done, C_MOE + 4 * j + 4 + i * EXPERT_CHUNKS)
                        if j >= 2:
                            dve.wait_ge(sem("moe_tr"), j - 1 + i * FE_TILES)
                        nc.vector.tensor_tensor(he[:, j % 2, :], PS[:, 2 + j % 2, :], sge[:, j % 2, :], ALU.mult)\
                            .then_inc(sem("moe_mul"), 1)
                    if k % 4 == 3 and 7 <= k < 7 + 4 * FE_TILES:
                        j = (k - 7) // 4
                        dve.wait_ge(sem("moe_ahi"), j + 1 + i * FE_TILES)
                        nc.vector.tensor_tensor(e_lo[:, 4 * j:4 * j + 4, :],
                                                PS[:, 6 + j % 2, :].rearrange("p (d t) -> p d t", d=4),
                                                e_hi[:, 4 * j:4 * j + 4, :], ALU.subtract).then_inc(sem("moe_alo"), 1)
                    if follow and k == GATHER_AT - 6:
                        picks(i + 1, i + 1)
                        gated_picks(i + 1, i + 1)
                    if follow and k == GATHER_AT + 7:
                        turned(i + 1)
                    if follow and k == EXPERT_CHUNKS + 1:
                        result(i)
                if not follow:
                    result(i)
                if alone:
                    add_back(i + 1)

            picks(0, 0)
            esplit(0, 0)
            gates()
            gated_picks(0, 0)
            esplit(0, 1)
            esplit(0, 2)
            turned(0)
            with dve.Fori(0, NE - 1) as e:
                expert(e, True)
            expert(NE - 1, False)
            add_back(NE)
            most = dve.value_load(need[0:1, NE:NE + 1], min_val=-S, max_val=S)
            with dve.If(most > 0):
                with dve.Fori(0, NE) as e:
                    i = e + NE
                    tokens = dve.value_load(need[0:1, bass.ds(e, 1)], min_val=-S, max_val=S)
                    with dve.If(tokens > 0):
                        picks(i, e)
                        gated_picks(i, e)
                        for k in range(STG):
                            esplit(i, k)
                        turned(i)
                        expert(i, False, True)
                    with dve.Else():
                        dve.drain()
                        dve.sem_inc(lo_done, EXPERT_CHUNKS)
                        dve.sem_inc(sem("moe_pick"), 1)
                        dve.sem_inc(sem("moe_pickg"), 1)
                        dve.sem_inc(sem("moe_xlo"), 2)
                        dve.sem_inc(sem("moe_back"), 1)
                        dve.sem_inc(sem("moe_mul"), FE_TILES)
                        dve.sem_inc(sem("moe_alo"), FE_TILES)
                        dve.sem_inc(sem("moe_ylo"), 1)
                        dve.sem_inc(sem("moe_add"), 4)

        @block.gpsimd
        def _(pool):
            def heads(h0, n, logits):
                for h in range(h0, h0 + n):
                    pool.wait_ge(sem("at_rcp"), h + 1)
                    nc.gpsimd.tensor_scalar(logits[:, h % 4, P:LOG], logits[:, h % 4, P:LOG], rs[:, h, 3:4], None,
                                            ALU.mult).then_inc(sem("at_norm"), 1)

            for m, src in enumerate((mla_q_norm, mla_k_norm)):
                pool.dma_start(grow[G_MLA + m:G_MLA + m + 1, :].rearrange("r (a n) -> r a n", a=2),
                               src[:, 0:64].unsqueeze(1).to_broadcast([1, 2, 64])).then_inc(sem("mla_in"), 16)
            pool.wait_ge(sem("brow_set"), 1)
            pool.dma_start(bias_dram[:, :], brow[:, :]).then_inc(sem("bias_out"), 16)
            pool.wait_ge(sem("bias_out"), 16)
            with nc.allow_non_contiguous_dma(reason="a window of the table for each partition"):
                pool.dma_start(brev[:, :, :], bass.AP(bias_dram, 0, [[1, P], [LOG, NH], [1, S]]))\
                    .then_inc(sem("bias_in"), 16)
            pool.dma_start(gate_bias[:, :], b_router.to_broadcast([P, NE])).then_inc(sem("bias8_in"), 16)
            heads(0, NH, lg)
            pool.wait_ge(sem("resid"), 4)
            pool.dma_start(gbc[:, 0, :], mla_q_norm[:, 64:QKD].to_broadcast([P, ROPE])).then_inc(sem("gbc_in"), 16)
            pool.dma_start(gbc[:, 1, :], mla_k_norm[:, 64:QKD].to_broadcast([P, ROPE])).then_inc(sem("gbc_in"), 16)
            pool.wait_ge(sem("grp_sqread"), 2 * GROUPS)
            pool.dma_start(ffg[:, :], ffn_norm_o.to_broadcast([P, D])).then_inc(sem("ffg_in"), 16)
            heads(NH, NH, lg1)
            pool.wait_ge(sem("hnat_lo"), 2)
            nc.gpsimd.memset(y_hi[:, :].bitcast(f32), 0.0)
            nc.gpsimd.memset(backT[:, :].bitcast(f32), 0.0)
            nc.gpsimd.memset(y_lo[:, :].bitcast(f32), 0.0).then_inc(sem("moe_ylo"), 1)

        @block.tensor
        def _(pe):
            def product(dst, xh, xl, wh, wl, first, last):
                nc.tensor.matmul(dst, xh, wh, start=first, stop=False)
                nc.tensor.matmul(dst, xh, wl, start=False, stop=False)
                return nc.tensor.matmul(dst, xl, wh, start=False, stop=last)

            def chunk(c, kn, n, body):
                pe.wait_ge(lo_done, c + 1)
                hi = w_hi[:, c % STG, 0:kn * n].rearrange("p (k n) -> p k n", k=kn)
                lo = w_lo[:, c % STG, 0:kn * n].rearrange("p (k n) -> p k n", k=kn)
                body(hi, lo).then_inc(mm_done, 1)

            def project(c0, nchunks, kn, n, bank, xh=a_hi, xl=a_lo, x0=0, norm=None):
                for q in range(nchunks):
                    def body(hi, lo):
                        for t in range(TT):
                            for k in range(kn):
                                kk = x0 + q * kn + k
                                if norm is not None and t == 0:
                                    pe.wait_ge(sem("norm_lo"), 8 * norm + kk + 1)
                                ins = product(PS[:, bank + t, 0:n], xh[:, kk, t * P:(t + 1) * P], xl[:, kk, t * P:(t + 1) * P],
                                              hi[:, k, :], lo[:, k, :], q == 0 and k == 0, q == nchunks - 1 and k == kn - 1)
                        return ins
                    chunk(c0 + q, kn, n, body)

            def norm(q):
                for c in range(4):
                    if c % 2 == 0:
                        if q < 3:
                            pe.wait_ge(sem("norm_xn0"), 2 * q + c // 2 + 1)
                            pe.wait_ge(sem("norm_xn1"), 2 * q + c // 2 + 1)
                        else:
                            pe.wait_ge(sem("hn_set"), c + 2)
                    for d in range(2):
                        for t in range(TT):
                            dc = 2 * c + d
                            ins = nc.tensor.transpose(PS[:, 4 + c, d * S + t * P:d * S + (t + 1) * P],
                                                      xn[:, t, dc * P:(dc + 1) * P], ident)
                    ins.then_inc(sem("norm_t"), 1)

            def heads(h0, n, q_of, k_of, v_of, probs_t):
                for s in range(n + 4):
                    if s < n:
                        h = h0 + s
                        if h >= 2:
                            pe.wait_ge(sem("at_add"), h - 1)
                        bank = PS[:, 4 + h % 2, :]
                        nc.tensor.matmul(bank[:, 0:P], q_of(h, 0), k_of(h)[:, 0:P], start=True, stop=True)
                        nc.tensor.matmul(bank[:, P:LOG], q_of(h, 1), k_of(h), start=True, stop=True).then_inc(sem("at_qk"), 1)
                    if 3 <= s <= n + 2:
                        h = h0 + s - 3
                        pe.wait_ge(sem("at_norm0"), h + 1)
                        pe.wait_ge(sem("at_norm"), h + 1)
                        if h >= 2:
                            pe.wait_ge(sem("at_pt"), h - 1)
                        lgb = (lg if h < NH else lg1)
                        for k in range(3):
                            ins = nc.tensor.transpose(PS[:, 6 + h % 2, k * P:(k + 1) * P], lgb[:, h % 4, k * P:(k + 1) * P], ident)
                        ins.then_inc(sem("at_tr"), 1)
                    if s >= 4:
                        h = h0 + s - 4
                        pe.wait_ge(sem("at_pt"), h + 1)
                        if h >= 4 and h % 2 == 0:
                            pe.wait_ge(sem("at_olo"), h // 2 - 1)
                        dst = PS[64 * (h % 2):64 * (h % 2) + 64, h // 2 % 2, 0:S]
                        nc.tensor.matmul(dst, v_of(h, 0), probs_t[:, h % 2, 0:S], start=True, stop=False)
                        nc.tensor.matmul(dst[:, P:S], v_of(h, 1), probs_t[:, h % 2, S:LOG], start=False, stop=True)\
                            .then_inc(sem("at_pv"), 1)

            pe.wait_ge(sem("id_in"), 16)
            pe.wait_ge(sem("gains_in"), 16 * N_GAINS)
            pe.wait_ge(sem("mla_in"), 32)
            nc.tensor.transpose(PS[:, 0, 0:G_ROWS], grow[:, :], cst[0:G_ROWS, K_ID:K_ID + G_ROWS]).then_inc(sem("gain_tr"), 1)
            norm(0)
            def turn_heads(m):
                if m == 2:
                    pe.wait_ge(sem("idx_relu"), IDXH)
                if m >= 2:
                    pe.wait_ge(sem("qk_evac"), 2 * (m - 1))
                for half in range(2):
                    bank = 4 + 2 * (m % 2) + half
                    for d in range(2 if (m or half == 0) else 1):
                        for t in range(TT):
                            f = (2 * half + d) * P
                            src = qn[:, m % 2, t, f:f + P] if m else idxn[:, t, f:f + P]
                            ins = nc.tensor.transpose(PS[:, bank, d * S + t * P:d * S + (t + 1) * P], src, ident)
                    ins.then_inc(sem("qk_tr"), 1)

            def turn_after(n):
                if IN_TURN[n] is not None:
                    pe.wait_ge(sem("tile_read"), n + 1)
                    turn_heads(IN_TURN[n])

            for n in range(7):
                if n >= 2:
                    pe.wait_ge(sem("tile_read"), n - 1)
                elif n == 0:
                    pe.wait_ge(sem("gain_copy"), 1)
                project(C_IN + 2 * n, 2, 4, IN_TILES[n][1], 2 * (n % 2), norm=0)
                if n == 0:
                    pe.wait_ge(sem("buckets_in"), 32)
                    pe.wait_ge(sem("ones_set"), 1)
                    nc.tensor.matmul(PS[0:16, 7, 0:LOG], bias_in[:, LOG:LOG + 16], bias_in[:, 0:LOG], start=True, stop=True)\
                        .then_inc(sem("brow_mm"), 1)
                if n == 2:
                    pe.wait_ge(sem("brow_set"), 1)
                if n >= 1:
                    turn_after(n - 1)
                if n == 2:
                    pe.wait_ge(sem("qk_evac"), 2)
                    for h in range(IDXH):
                        r = HD * (h % 2)
                        if h >= 2:
                            pe.wait_ge(sem("idx_relu"), h - 1)
                        nc.tensor.matmul(PS[:, 4 + h % 2, 0:P], iqT[r:r + HD, h // 2, 0:P], ikT[r:r + HD, 0:P], start=True, stop=True)
                        nc.tensor.matmul(PS[:, 4 + h % 2, P:LOG], iqT[r:r + HD, h // 2, P:S], ikT[r:r + HD, :], start=True, stop=True)\
                            .then_inc(sem("idx_mm"), 1)
            pe.wait_ge(sem("tile_read"), 7)
            pe.wait_ge(sem("qk_evac"), 10)

            def r0(h):
                return HD * (h % 2)
            heads(0, NH, lambda h, t: qT0[r0(h):r0(h) + HD, h // 2, t * P:(t + 1) * P],
                  lambda h: kT0[r0(h):r0(h) + HD, h // 2, :],
                  lambda h, t: v0[:, t, h * HD:(h + 1) * HD], pT)
            pe.wait_ge(sem("at_olo"), NH // 2)
            for n in range(2):
                project(C_OUTE + 2 * n, 2, 4, NT, 2 * n)
            norm(1)

            def turn_ff(j):
                pe.wait_ge(sem("up_read"), j + 1)
                for k in range(FB0[j], FB0[j + 1]):
                    if k >= 4:
                        pe.wait_ge(sem("ff_lo"), k - 3)
                    for d in range(2):
                        for t in range(TT):
                            f = (2 * (k - FB0[j]) + d) * P
                            ins = nc.tensor.transpose(PS[:, 4 + k % 4, d * S + t * P:d * S + (t + 1) * P],
                                                      hn[:, j % 2, t, f:f + P], ident)
                    ins.then_inc(sem("ff_tr"), 1)

            for j in range(FF_TILES):
                if j:
                    pe.wait_ge(sem("gate_read"), j)
                project(C_FF + 4 * j, 2, 4, FF_W[j], 0, norm=None if j else 1)
                if j:
                    turn_ff(j - 1)
                project(C_FF + 4 * j + 2, 2, 4, FF_W[j], 2)
            pe.wait_ge(sem("gate_read"), FF_TILES)
            pe.wait_ge(sem("up_read"), FF_TILES)
            for q in range(FFD // 256):
                pe.wait_ge(sem("ff_lo"), q + 1)

                def body(hi, lo):
                    for half in range(2):
                        cols = slice(half * NT, (half + 1) * NT)
                        for t in range(TT):
                            for k in range(2):
                                f = 2 * q + k
                                xs = [a[:, f, t * P:(t + 1) * P] for a in (act_hi, act_lo)]
                                ins = product(PS[:, 2 * half + t, :], *xs, hi[:, k, cols], lo[:, k, cols],
                                              f == 0, f == FFD // P - 1)
                        if half == 0 and q == FFD // 256 - 1:
                            ins.then_inc(sem("down_half"), 1)
                    return ins
                chunk(C_FD + q, 2, D, body)
                if q == 1:
                    turn_ff(FF_TILES - 1)
            norm(2)
            for n in range(2):
                project(C_LAT + 2 * n, 2, 4, LAT[n][1], 2 * n, norm=None if n else 2)

            def turn_lat(ds):
                for d in ds:
                    bank, off = ((4, 0), (4, S), (5, 0), (6, 0), (6, S))[d]
                    for t in range(TT):
                        ins = nc.tensor.transpose(PS[:, bank, off + t * P:off + (t + 1) * P], latn[:, t, d * P:(d + 1) * P], ident)
                    if d in (1, 2, 4):
                        ins.then_inc(sem("lat_tr"), 1)

            pe.wait_ge(sem("lat_n"), 1)
            turn_lat((0, 1, 2))
            pe.wait_ge(sem("lat_lo"), 3)

            def turn_group(g, half):
                pe.wait_ge(sem("grp_qk"), g + 1)
                for h in range(GH * g + 2 * half, GH * g + 2 * half + 2):
                    if h >= 2:
                        pe.wait_ge(sem("grp_ev"), 2 * (h - 1))
                    for s in range(2):
                        for t in range(TT):
                            ins = nc.tensor.transpose(PS[0:QKD, 6 + h % 2, s * S + t * P:s * S + (t + 1) * P],
                                                      qk[:, g % 2, (s * TT + t) * GH + h % GH, :], ident)
                    ins.then_inc(sem("grp_tr"), 1)

            for m in range(2 * GROUPS):
                if m == 1:
                    pe.wait_ge(sem("lat_n"), 2)
                    turn_lat((3, 4))
                    pe.wait_ge(sem("lat_lo"), 5)
                if m >= 3:
                    pe.wait_ge(sem("item_read"), m - 2)
                    if m % 2 == 0:
                        pe.wait_ge(sem("v_read"), (m - 2) // 2)
                if m % 2 == 0:
                    project(C_HEADS + m, 1, 3, GH * QKD, 2 * (m % 3), lat_hi, lat_lo, 0)
                    if m >= 4:
                        turn_group(m // 2 - 2, 1)
                else:
                    project(C_HEADS + m, 1, 2, GH * P, 2 * (m % 3), lat_hi, lat_lo, 3)
                    if m >= 3:
                        turn_group((m - 3) // 2, 0)
            turn_group(GROUPS - 2, 1)
            turn_group(GROUPS - 1, 0)
            turn_group(GROUPS - 1, 1)
            pe.wait_ge(sem("item_read"), 2 * GROUPS)
            pe.wait_ge(sem("v_read"), GROUPS)
            pe.wait_ge(sem("grp_ev"), 2 * NH)
            heads(NH, NH, lambda h, t: qkT[0:QKD, h - NH, t * P:(t + 1) * P],
                  lambda h: qkT[0:QKD, h - NH, S:2 * S],
                  lambda h, t: v1[:, t, (h - NH) * 64:(h - NH + 1) * 64], pT1)
            pe.wait_ge(sem("at_olo"), NH)
            for n in range(2):
                project(C_OUTO + 2 * n, 2, 4, NT, 2 * n)
            norm(3)
            project(C_ROUTE, 1, DC, NE, 0, norm=3)
            pe.wait_ge(sem("sel_set"), 1)
            tri, ones = cst[:, K_TRI:K_TRI + P], cst[:, K_ONES:K_ONES + P]
            sel = [rt[:, 6, t * NE:(t + 1) * NE] for t in range(TT)]
            nc.tensor.matmul(PS[:, 4, 0:NE], tri, sel[0], start=True, stop=True)
            nc.tensor.matmul(PS[:, 5, 0:NE], ones, sel[0], start=True, stop=False)
            nc.tensor.matmul(PS[:, 5, 0:NE], tri, sel[1], start=False, stop=True)
            nc.tensor.matmul(PS[:, 6, 0:NE], ones, sel[0], start=True, stop=False)
            nc.tensor.matmul(PS[:, 6, 0:NE], ones, sel[1], start=False, stop=True).then_inc(sem("place_mm"), 1)
            pe.wait_ge(sem("hnat_lo"), 2)
            pe.wait_ge(sem("need_set"), 1)

            def gather(i):
                pe.wait_ge(sem("moe_pick"), i + 1)
                for half in range(2):
                    for t in range(TT):
                        for h, part in enumerate((h_hi, h_lo)):
                            ins = nc.tensor.matmul(PS[:, 4 + half, :], pick[:, t, :], part[:, t, half * NT:(half + 1) * NT],
                                                   start=(t == 0 and h == 0), stop=(t == 1 and h == 1))
                    ins.then_inc(sem("moe_gath"), 1)

            def turn_block(i):
                for half in range(2):
                    pe.wait_ge(sem("moe_xg"), 2 * i + half + 1)
                    for d in range(4):
                        dc = 4 * half + d
                        ins = nc.tensor.transpose(PS[:, 4 + half, d * P:(d + 1) * P], xg[:, dc * P:(dc + 1) * P], ident)
                    ins.then_inc(sem("moe_xt"), 1)

            def turn_pick(i):
                pe.wait_ge(sem("moe_pickg"), i + 1)
                for t in range(TT):
                    ins = nc.tensor.transpose(PS[:, 3, t * P:(t + 1) * P], pickg[:, t, :], ident)
                ins.then_inc(sem("moe_turn"), 1)

            def bring_back(n):
                pe.wait_ge(sem("moe_ylo"), n + 1)
                for s in range(4):
                    t, half = s // 2, s % 2
                    cols = slice(half * NT, (half + 1) * NT)
                    nc.tensor.matmul(PS[:, 4 + s, :], backT[:, t * P:(t + 1) * P], y_hi[:, cols], start=True, stop=False)
                    nc.tensor.matmul(PS[:, 4 + s, :], backT[:, t * P:(t + 1) * P], y_lo[:, cols], start=False, stop=True)\
                        .then_inc(sem("moe_sc"), 1)

            def echunk(i, k, kn, n, body):
                c = C_MOE + k
                pe.wait_ge(lo_done, c + 1 + i * EXPERT_CHUNKS)
                hi = w_hi[:, c % STG, :].rearrange("p (k n) -> p k n", k=kn)
                lo = w_lo[:, c % STG, :].rearrange("p (k n) -> p k n", k=kn)
                body(hi, lo).then_inc(mm_done, 1)

            def turn(i, j):
                pe.wait_ge(sem("moe_mul"), j + 1 + i * FE_TILES)
                if j >= 2:
                    pe.wait_ge(sem("moe_alo"), j - 1 + i * FE_TILES)
                for f in range(4):
                    ins = nc.tensor.transpose(PS[:, 6 + j % 2, f * P:(f + 1) * P], he[:, j % 2, f * P:(f + 1) * P], ident)
                ins.then_inc(sem("moe_tr"), 1)

            def expert(i, follow, alone=False):
                pe.wait_ge(sem("moe_xlo"), 2 * i + 2)
                for k in range(4 * FE_TILES):
                    j, w, kh = k // 4, k // 2 % 2, k % 2
                    if k == 2:
                        if not alone:
                            bring_back(i)
                        turn_pick(i)
                    if j >= 2 and kh == 0:
                        pe.wait_ge(sem("moe_silu" if w == 0 else "moe_mul"), j - 1 + i * FE_TILES)

                    def body(hi, lo):
                        for kk in range(4):
                            dc = 4 * kh + kk
                            ins = product(PS[:, 2 * w + j % 2, :], a_hi[:, dc, 0:P], a_lo[:, dc, 0:P],
                                          hi[:, kk, :], lo[:, kk, :], dc == 0, dc == DC - 1)
                        return ins
                    echunk(i, k, 4, NT, body)
                    if k == 5:
                        if not alone:
                            pe.wait_ge(sem("moe_add"), 4 * i + 4)
                        pe.wait_ge(sem("moe_back"), i + 1)
                    if k % 4 == 1 and k >= 5:
                        turn(i, (k - 5) // 4)
                for q in range(FFE // P // 2):
                    if q == 0:
                        pe.wait_ge(sem("moe_mul"), (i + 1) * FE_TILES)
                        turn(i, FE_TILES - 1)
                    if q % 2 == 0:
                        pe.wait_ge(sem("moe_alo"), q // 2 + 1 + i * FE_TILES)

                    def body(hi, lo):
                        for kk in range(2):
                            f = 2 * q + kk
                            for half in range(2):
                                cols = slice(half * NT, (half + 1) * NT)
                                ins = product(PS[:, 2 + half, :], e_hi[:, f, :], e_lo[:, f, :],
                                              hi[:, kk, cols], lo[:, kk, cols], f == 0, f == FFE // P - 1)
                        return ins
                    echunk(i, 4 * FE_TILES + q, 2, D, body)
                    if follow and 4 * FE_TILES + q == GATHER_AT:
                        gather(i + 1)
                    if follow and 4 * FE_TILES + q == GATHER_AT + 3:
                        turn_block(i + 1)
                if alone:
                    bring_back(i + 1)
                    pe.wait_ge(sem("moe_add"), 4 * i + 8)

            gather(0)
            turn_block(0)
            with pe.Fori(0, NE - 1) as e:
                expert(e, True)
            expert(NE - 1, False)
            bring_back(NE)
            pe.wait_ge(sem("moe_add"), 4 * NE + 4)
            most = pe.value_load(need[0:1, NE:NE + 1], min_val=-S, max_val=S)
            with pe.If(most > 0):
                with pe.Fori(0, NE) as e:
                    i = e + NE
                    tokens = pe.value_load(need[0:1, bass.ds(e, 1)], min_val=-S, max_val=S)
                    with pe.If(tokens > 0):
                        gather(i)
                        turn_block(i)
                        expert(i, False, True)
                    with pe.Else():
                        pe.drain()
                        pe.sem_inc(mm_done, EXPERT_CHUNKS)
                        pe.sem_inc(sem("moe_gath"), 2)
                        pe.sem_inc(sem("moe_xt"), 2)
                        pe.sem_inc(sem("moe_turn"), 1)
                        pe.sem_inc(sem("moe_tr"), FE_TILES)
                        pe.sem_inc(sem("moe_sc"), 4)


_INS = ['x', 'rel_bias', 'mix_norm_e', 'w_in_e', 'moba_q_norm', 'moba_k_norm', 'dsa_q_norm', 'dsa_k_norm',
        'w_out_e', 'ffn_norm_e', 'w_gate_e', 'w_up_e', 'w_down_e', 'mix_norm_o', 'w_in_o', 'q_a_norm', 'kv_a_norm',
        'w_uq', 'w_ukv', 'mla_q_norm', 'mla_k_norm', 'w_out_o', 'ffn_norm_o', 'w_router', 'b_router',
        'w_gate_o', 'w_up_o', 'w_down_o']


def shape_constants():
    import math
    import numpy as np
    c = np.zeros((P, K_ALL), np.float32)
    c[:, K_ID:K_ID + P] = np.eye(P)
    c[:, K_IOTA:K_IOTA + P] = np.arange(P)[None]
    c[:, K_TRI:K_TRI + P] = np.arange(P)[:, None] < np.arange(P)[None]
    c[:, K_ONES:K_ONES + P] = 1
    t, s = np.arange(P)[:, None], np.arange(S)[None]
    c[:, K_MASK:K_MASK + P] = np.where(s[:, :P] <= t, 0, MASKED)
    c[:, K_MASK + P:K_MASK + LOG] = np.where(s <= t + P, 0, MASKED)
    half = ROPE // 2
    freqs = np.float32(10000.0) ** (-np.arange(half, dtype=np.float32) / np.float32(half))
    ang = np.arange(S, dtype=np.float32)[:, None] * freqs
    for at, f in ((K_COS, np.cos), (K_SIN, np.sin)):
        c[:, at:at + TT * half] = f(ang).reshape(TT, P, half).transpose(1, 0, 2).reshape(P, TT * half)
    c[:, K_LOW:K_LOW + NE * NE] = (np.arange(NE)[None] < np.arange(NE)[:, None]).reshape(1, -1)
    n = np.arange(LOG) - (P - 1)
    exact = BUCKETS // 2
    nf = np.maximum(n, 1).astype(np.float32)
    large = exact + (np.log(nf / np.float32(exact)) / np.float32(math.log(1024 / exact)) * np.float32(BUCKETS - exact)).astype(np.int32)
    bucket = np.where(n < exact, np.maximum(n, 0), np.minimum(large, BUCKETS - 1))
    b = np.zeros((BUCKETS + 1, LOG), np.float32)
    b[bucket, np.arange(LOG)] = 1
    b[BUCKETS] = np.where(n < 0, MASKED, 0)
    return c, b


def kernel(**inputs):
    import numpy as _np
    import concourse.bacc as _bacc
    from concourse import mybir as _mybir
    from concourse.bass_utils import run_bass_kernel_spmd as _run

    nc = _bacc.Bacc("TRN2", target_bir_lowering=False, num_devices=1)
    arrays, args = {}, []
    consts, buckets = shape_constants()
    given = [(name, inputs[name]) for name in _INS] + [("consts", consts), ("buckets", buckets)]
    for name, value in given:
        a = _np.ascontiguousarray(value)
        arrays[f"in_{name}_dram"] = a
        args.append(nc.dram_tensor(f"in_{name}_dram", a.shape, _mybir.dt.from_np(a.dtype), kind="ExternalInput").ap())
    args.append(nc.dram_tensor("out_0_dram", (1, S, D), _mybir.dt.float32, kind="ExternalOutput").ap())
    hybrid_trunk(nc, *args)
    r = _run(nc, [arrays], core_ids=[0])
    return r.results[0]["out_0_dram"]
```
